# Optimizing a Trainium2 kernel written in Bass

```python
import math
import jax, jax.numpy as jnp
from jax import lax
import numpy as np

D_MODEL = 2048
BATCH = 1
SEQ = 256
DEPTH = 2

MIX_WIDTH = D_MODEL
A_HEAD_DIM = 64
A_WIDTH = 3 * D_MODEL // 8
A_Q_HEADS = A_WIDTH // A_HEAD_DIM
A_KV_HEADS = A_Q_HEADS // 3
A_GROUP = A_Q_HEADS // A_KV_HEADS
A_KV_WIDTH = A_KV_HEADS * A_HEAD_DIM
WINDOW = 128
ATTN_BLOCK = 128
ROPE_THETA = 500000.0
ROT_DIM = A_HEAD_DIM // 4
B_WIDTH = D_MODEL // 4
B_CONV_WIDTH = 31
C_HEAD_DIM = 128
C_HEADS = (MIX_WIDTH - A_WIDTH - B_WIDTH) // C_HEAD_DIM
C_WIDTH = C_HEADS * C_HEAD_DIM
C_CONV_WIDTH = 4
CHUNK = 64

EPS = 1e-6
MAX_POS_OFFSET = 4096

COL_SPLITS = (A_WIDTH, A_KV_WIDTH, A_KV_WIDTH, A_WIDTH,
              2 * B_WIDTH, B_WIDTH,
              3 * C_WIDTH, C_HEADS, C_HEADS, C_WIDTH)
IN_COLS = sum(COL_SPLITS)


def _split_cols(p):
    idx = []
    s = 0
    for n in COL_SPLITS[:-1]:
        s += n
        idx.append(s)
    return jnp.split(p, idx, axis=-1)

def rms_norm(x, w):
    x32 = x.astype(jnp.float32)
    y = x32 * lax.rsqrt(jnp.mean(x32 * x32, axis=-1, keepdims=True) + EPS)
    return (y * w.astype(jnp.float32)).astype(x.dtype)

def layer_norm(x, w, b):
    x32 = x.astype(jnp.float32)
    mu = jnp.mean(x32, axis=-1, keepdims=True)
    var = jnp.mean(jnp.square(x32 - mu), axis=-1, keepdims=True)
    y = (x32 - mu) * lax.rsqrt(var + EPS)
    return (y * w.astype(jnp.float32) + b.astype(jnp.float32)).astype(x.dtype)

def l2_norm(x):
    return x * lax.rsqrt(jnp.sum(x * x, axis=-1, keepdims=True) + EPS)

def causal_depthwise_conv(x, w):
    K, C = w.shape
    return lax.conv_general_dilated(
        x, w[:, None, :].astype(x.dtype), window_strides=(1,), padding=[(K - 1, 0)],
        dimension_numbers=('NWC', 'WIO', 'NWC'), feature_group_count=C)

def rope_tables(positions):
    inv_freq = ROPE_THETA ** (-jnp.arange(0, ROT_DIM, 2, dtype=jnp.float32) / ROT_DIM)
    ang = positions.astype(jnp.float32)[..., None] * inv_freq
    return jnp.cos(ang)[:, :, None, :], jnp.sin(ang)[:, :, None, :]

def apply_partial_rope(x, cos, sin):
    half = ROT_DIM // 2
    x1 = x[..., :half].astype(jnp.float32)
    x2 = x[..., half:ROT_DIM].astype(jnp.float32)
    rot = jnp.concatenate([x1 * cos - x2 * sin, x2 * cos + x1 * sin], axis=-1)
    return jnp.concatenate([rot.astype(x.dtype), x[..., ROT_DIM:]], axis=-1)

def sliding_window_sink_attention(q, k, v, sinks):
    bsz, T = q.shape[0], q.shape[1]
    nb = T // ATTN_BLOCK
    qb = q.reshape(bsz, nb, ATTN_BLOCK, A_KV_HEADS, A_GROUP, A_HEAD_DIM)
    kb = k.reshape(bsz, nb, ATTN_BLOCK, A_KV_HEADS, A_HEAD_DIM)
    vb = v.reshape(bsz, nb, ATTN_BLOCK, A_KV_HEADS, A_HEAD_DIM)
    prev = lambda t: jnp.concatenate([jnp.zeros_like(t[:, :1]), t[:, :-1]], axis=1)
    kk = jnp.concatenate([prev(kb), kb], axis=2)
    vv = jnp.concatenate([prev(vb), vb], axis=2)
    s = jnp.einsum('bnqhgd,bnkhd->bnhgqk', qb, kk).astype(jnp.float32) * (A_HEAD_DIM ** -0.5)
    qi = jnp.arange(ATTN_BLOCK)[:, None]
    kj = jnp.arange(2 * ATTN_BLOCK)[None, :]
    dist = qi + ATTN_BLOCK - kj
    band = (dist >= 0) & (dist < WINDOW)
    not_pad = (jnp.arange(nb)[:, None, None] > 0) | (kj[None] >= ATTN_BLOCK)
    valid = band[None] & not_pad
    s = jnp.where(valid[None, :, None, None], s, -jnp.inf)
    sink = sinks.reshape(A_KV_HEADS, A_GROUP).astype(jnp.float32)[None, None, :, :, None, None]
    sink = jnp.broadcast_to(sink, s.shape[:-1] + (1,))
    p = jax.nn.softmax(jnp.concatenate([s, sink], axis=-1), axis=-1)[..., :-1]
    o = jnp.einsum('bnhgqk,bnkhd->bnqhgd', p.astype(v.dtype), vv)
    return o.reshape(bsz, T, A_Q_HEADS * A_HEAD_DIM)

def conformer_conv_module(u, conv_w, conv_b, ln_w, ln_b, pw_w, pw_b):
    a, gt = jnp.split(u, 2, axis=-1)
    h = a * jax.nn.sigmoid(gt)
    h = causal_depthwise_conv(h, conv_w) + conv_b.astype(h.dtype)
    h = jax.nn.silu(layer_norm(h, ln_w, ln_b))
    return h @ pw_w + pw_b

def gated_delta_rule_chunked(q, k, v, g, beta):
    bsz, T, H, Dk = q.shape
    Dv = v.shape[-1]
    n = T // CHUNK
    q = q * (Dk ** -0.5)

    def to_chunks(t):
        return t.reshape(bsz, n, CHUNK, H, t.shape[-1]).transpose(0, 1, 3, 2, 4)

    qc, kc, vc = to_chunks(q), to_chunks(k), to_chunks(v)
    bc = beta.reshape(bsz, n, CHUNK, H).transpose(0, 1, 3, 2)
    gc = jnp.cumsum(g.reshape(bsz, n, CHUNK, H).transpose(0, 1, 3, 2), axis=-1)
    idx = jnp.arange(CHUNK)
    incl = idx[:, None] >= idx[None, :]
    strict = idx[:, None] > idx[None, :]
    decay = jnp.exp(jnp.where(incl, gc[..., :, None] - gc[..., None, :], -jnp.inf))
    kb = kc * bc[..., None]
    lower = jnp.where(strict, jnp.einsum('bnhid,bnhjd->bnhij', kb, kc) * decay, 0.0)
    eye = jnp.eye(CHUNK, dtype=lower.dtype)
    rhs = jnp.concatenate([vc * bc[..., None], kb * jnp.exp(gc)[..., None]], axis=-1)
    sol = lax.linalg.triangular_solve(lower + eye, rhs, left_side=True, lower=True,
                                      unit_diagonal=True)
    u, w = sol[..., :Dv], sol[..., Dv:]
    intra = jnp.where(incl, jnp.einsum('bnhid,bnhjd->bnhij', qc, kc) * decay, 0.0)

    def step(S, xs):
        q_i, k_i, u_i, w_i, g_i, a_i = xs
        v_new = u_i - jnp.einsum('bhck,bhkv->bhcv', w_i, S)
        o_i = (jnp.einsum('bhck,bhkv->bhcv', q_i * jnp.exp(g_i)[..., None], S)
               + jnp.einsum('bhij,bhjv->bhiv', a_i, v_new))
        g_last = g_i[..., -1:]
        S = (S * jnp.exp(g_last)[..., None]
             + jnp.einsum('bhck,bhcv->bhkv', k_i * jnp.exp(g_last - g_i)[..., None], v_new))
        return S, o_i

    S0 = jnp.zeros((bsz, H, Dk, Dv), q.dtype)
    xs = tuple(jnp.moveaxis(t, 1, 0) for t in (qc, kc, u, w, gc, intra))
    _, o = lax.scan(step, S0, xs)
    return o.transpose(1, 0, 3, 2, 4).reshape(bsz, T, H, Dv)

def gated_deltanet(qkv_raw, b_raw, a_raw, conv_w, a_log, dt_bias):
    bsz, T = qkv_raw.shape[0], qkv_raw.shape[1]
    qkv = jax.nn.silu(causal_depthwise_conv(qkv_raw, conv_w)).astype(jnp.float32)
    q, k, v = jnp.split(qkv, 3, axis=-1)
    q = l2_norm(q.reshape(bsz, T, C_HEADS, C_HEAD_DIM))
    k = l2_norm(k.reshape(bsz, T, C_HEADS, C_HEAD_DIM))
    v = v.reshape(bsz, T, C_HEADS, C_HEAD_DIM)
    beta = jax.nn.sigmoid(b_raw.astype(jnp.float32))
    g = -jnp.exp(a_log.astype(jnp.float32)) * jax.nn.softplus(
        a_raw.astype(jnp.float32) + dt_bias.astype(jnp.float32))
    return gated_delta_rule_chunked(q, k, v, g, beta)

def first_inputs(seed: int = 0) -> dict:
    key = jax.random.key(seed)
    ks = jax.random.split(key, 24)
    nrm = jax.random.normal
    x = nrm(ks[0], (BATCH, SEQ, D_MODEL), jnp.float32)
    offset = jax.random.randint(ks[1], (BATCH, 1), 0, MAX_POS_OFFSET, dtype=jnp.int32)
    positions = (offset + jnp.arange(SEQ, dtype=jnp.int32)[None, :]).astype(jnp.int32)
    norm_w = 1.0 + 0.02 * nrm(ks[2], (DEPTH, D_MODEL))
    w_in = nrm(ks[3], (DEPTH, D_MODEL, IN_COLS)) * D_MODEL ** -0.5
    q_norm_w = 1.0 + 0.02 * nrm(ks[4], (DEPTH, A_HEAD_DIM))
    k_norm_w = 1.0 + 0.02 * nrm(ks[5], (DEPTH, A_HEAD_DIM))
    sinks = nrm(ks[6], (DEPTH, A_Q_HEADS))
    b_conv_w = nrm(ks[7], (DEPTH, B_CONV_WIDTH, B_WIDTH)) * B_CONV_WIDTH ** -0.5
    b_conv_b = 0.02 * nrm(ks[8], (DEPTH, B_WIDTH))
    b_ln_w = 1.0 + 0.02 * nrm(ks[9], (DEPTH, B_WIDTH))
    b_ln_b = 0.02 * nrm(ks[10], (DEPTH, B_WIDTH))
    b_pw_w = nrm(ks[11], (DEPTH, B_WIDTH, B_WIDTH)) * B_WIDTH ** -0.5
    b_pw_b = 0.02 * nrm(ks[12], (DEPTH, B_WIDTH))
    c_conv_w = nrm(ks[13], (DEPTH, C_CONV_WIDTH, 3 * C_WIDTH)) * C_CONV_WIDTH ** -0.5
    c_a_log = jnp.log(jax.random.uniform(ks[14], (DEPTH, C_HEADS), minval=1.0, maxval=16.0))
    dt = jnp.exp(jax.random.uniform(ks[15], (DEPTH, C_HEADS),
                                    minval=math.log(1e-3), maxval=math.log(1e-1)))
    c_dt_bias = dt + jnp.log(-jnp.expm1(-dt))
    c_onorm_w = 1.0 + 0.02 * nrm(ks[16], (DEPTH, C_HEAD_DIM))
    w_out = nrm(ks[17], (DEPTH, MIX_WIDTH, D_MODEL)) * MIX_WIDTH ** -0.5
    return {"x": x, "positions": positions, "norm_w": norm_w, "w_in": w_in,
            "q_norm_w": q_norm_w, "k_norm_w": k_norm_w, "sinks": sinks,
            "b_conv_w": b_conv_w, "b_conv_b": b_conv_b, "b_ln_w": b_ln_w,
            "b_ln_b": b_ln_b, "b_pw_w": b_pw_w, "b_pw_b": b_pw_b,
            "c_conv_w": c_conv_w, "c_a_log": c_a_log, "c_dt_bias": c_dt_bias,
            "c_onorm_w": c_onorm_w, "w_out": w_out}

def first_block(x, positions, norm_w, w_in, q_norm_w, k_norm_w, sinks, b_conv_w, b_conv_b,
              b_ln_w, b_ln_b, b_pw_w, b_pw_b, c_conv_w, c_a_log, c_dt_bias, c_onorm_w,
              w_out):
    bsz, T = x.shape[0], x.shape[1]
    cos, sin = rope_tables(positions)
    for l in range(DEPTH):
        h = rms_norm(x, norm_w[l])
        p = h @ w_in[l]
        qa, ka, va, za, ub, zb, qkv_c, b_c, a_c, zc = _split_cols(p)
        qa = apply_partial_rope(rms_norm(qa.reshape(bsz, T, A_Q_HEADS, A_HEAD_DIM), q_norm_w[l]), cos, sin)
        ka = apply_partial_rope(rms_norm(ka.reshape(bsz, T, A_KV_HEADS, A_HEAD_DIM), k_norm_w[l]), cos, sin)
        va = va.reshape(bsz, T, A_KV_HEADS, A_HEAD_DIM)
        oa = sliding_window_sink_attention(qa, ka, va, sinks[l]) * jax.nn.silu(za)
        ob = conformer_conv_module(ub, b_conv_w[l], b_conv_b[l], b_ln_w[l], b_ln_b[l],
                                   b_pw_w[l], b_pw_b[l]) * jax.nn.silu(zb)
        oc = gated_deltanet(qkv_c, b_c, a_c, c_conv_w[l], c_a_log[l], c_dt_bias[l]).astype(x.dtype)
        oc = rms_norm(oc, c_onorm_w[l]) * jax.nn.silu(zc.reshape(bsz, T, C_HEADS, C_HEAD_DIM))
        oc = oc.reshape(bsz, T, C_WIDTH)
        y = jnp.concatenate([oa, ob, oc], axis=-1)
        x = x + y @ w_out[l]
    return x


EXPAND = 2
D_INNER = EXPAND * D_MODEL
PLE_DIM = 256
N_MIXERS = 2
POOL_WINDOWS = (2, 4, 8, 16)
N_POOL_GROUPS = len(POOL_WINDOWS)
POOL_GROUP_DIM = D_INNER // N_POOL_GROUPS
LRU_HEADS = 16
LRU_BLOCK = D_INNER // LRU_HEADS
CONV_WIDTH = 4
LRU_C = 8.0
RMS_EPS = 1e-6
N_POOL_LAYERS = (DEPTH + 1) // 2
N_LRU_LAYERS = DEPTH // 2


def rmsnorm(x, g):
    xf = x.astype(jnp.float32)
    var = jnp.mean(xf * xf, axis=-1, keepdims=True)
    return (xf * lax.rsqrt(var + RMS_EPS) * g.astype(jnp.float32)).astype(x.dtype)

def pool_mixer(u, w_grp, b, scale):
    B, S, E = u.shape
    maxw = POOL_WINDOWS[-1]
    uf = u.astype(jnp.float32)
    cs = jnp.cumsum(uf, axis=1)
    csp = jnp.pad(cs, ((0, 0), (maxw, 0), (0, 0)))
    pos = jnp.arange(1, S + 1, dtype=jnp.int32)
    diffs = []
    for g, w in enumerate(POOL_WINDOWS):
        c0, c1 = g * POOL_GROUP_DIM, (g + 1) * POOL_GROUP_DIM
        win_sum = csp[:, maxw:, c0:c1] - csp[:, maxw - w:maxw - w + S, c0:c1]
        count = jnp.minimum(pos, w).astype(jnp.float32)[None, :, None]
        diffs.append(win_sum / count - uf[..., c0:c1])
    d = jnp.stack(diffs, axis=2).astype(u.dtype)
    y = jnp.einsum('bsgc,gcd->bsgd', d, w_grp).reshape(B, S, E) + b
    return y * scale

def causal_depthwise_conv_2(x, w, b):
    S = x.shape[1]
    xp = jnp.pad(x, ((0, 0), (CONV_WIDTH - 1, 0), (0, 0)))
    y = b
    for k in range(CONV_WIDTH):
        y = y + xp[:, k:k + S] * w[k]
    return y

def rglru(x, wa, ba, wx, bx, lam):
    B, S, E = x.shape
    xb = x.reshape(B, S, LRU_HEADS, LRU_BLOCK)
    r = jax.nn.sigmoid((jnp.einsum('bshi,hij->bshj', xb, wa).reshape(B, S, E) + ba).astype(jnp.float32))
    ig = jax.nn.sigmoid((jnp.einsum('bshi,hij->bshj', xb, wx).reshape(B, S, E) + bx).astype(jnp.float32))
    log_a = -LRU_C * r * jax.nn.softplus(-lam.astype(jnp.float32))
    a = jnp.exp(log_a)
    mult = jnp.sqrt(jnp.maximum(-jnp.expm1(2.0 * log_a), 0.0))
    bterm = mult * ig * x.astype(jnp.float32)

    def combine(left, right):
        a1, b1 = left
        a2, b2 = right
        return a1 * a2, a2 * b1 + b2

    _, h = lax.associative_scan(combine, (a, bterm), axis=1)
    return h.astype(x.dtype)

def second_inputs(seed: int = 0) -> dict:
    key = jax.random.key(seed)
    ks = jax.random.split(key, 24)
    f32 = jnp.float32

    def nrm(k, shape, fan_in):
        return jax.random.normal(k, shape, f32) * (fan_in ** -0.5)

    def gain(k, shape):
        return 1.0 + 0.05 * jax.random.normal(k, shape, f32)

    def bias(k, shape):
        return 0.01 * jax.random.normal(k, shape, f32)

    a0 = jax.random.uniform(ks[15], (N_LRU_LAYERS, D_INNER), f32, 0.9, 0.999)
    lru_L = jnp.log(a0) - jnp.log1p(-a0)
    return {
        "x": jax.random.normal(ks[0], (BATCH, SEQ, D_MODEL), f32),
        "p": jax.random.normal(ks[1], (DEPTH, BATCH, SEQ, PLE_DIM), f32),
        "w_in": nrm(ks[2], (DEPTH, D_MODEL, 2 * D_INNER), D_MODEL),
        "w_out": nrm(ks[3], (DEPTH, D_INNER, D_MODEL), D_INNER),
        "g_pre": gain(ks[4], (DEPTH, D_MODEL)),
        "g_post": gain(ks[5], (DEPTH, D_MODEL)),
        "pool_w": nrm(ks[6], (N_POOL_LAYERS, N_POOL_GROUPS, POOL_GROUP_DIM, POOL_GROUP_DIM), POOL_GROUP_DIM),
        "pool_b": bias(ks[7], (N_POOL_LAYERS, D_INNER)),
        "pool_scale": gain(ks[8], (N_POOL_LAYERS, D_INNER)),
        "conv_w": nrm(ks[9], (N_LRU_LAYERS, CONV_WIDTH, D_INNER), CONV_WIDTH),
        "conv_b": bias(ks[10], (N_LRU_LAYERS, D_INNER)),
        "lru_wa": nrm(ks[11], (N_LRU_LAYERS, LRU_HEADS, LRU_BLOCK, LRU_BLOCK), LRU_BLOCK),
        "lru_ba": bias(ks[12], (N_LRU_LAYERS, D_INNER)),
        "lru_wx": nrm(ks[13], (N_LRU_LAYERS, LRU_HEADS, LRU_BLOCK, LRU_BLOCK), LRU_BLOCK),
        "lru_bx": bias(ks[14], (N_LRU_LAYERS, D_INNER)),
        "lru_L": lru_L,
        "w_ple": nrm(ks[16], (DEPTH, PLE_DIM, D_MODEL), PLE_DIM),
        "w_ple_gate": nrm(ks[17], (DEPTH, D_MODEL, D_MODEL), D_MODEL),
        "g_ple_in": gain(ks[18], (DEPTH, D_MODEL)),
        "g_ple_out": gain(ks[19], (DEPTH, D_MODEL)),
    }

def second_block(x, p, w_in, w_out, g_pre, g_post, pool_w, pool_b, pool_scale,
              conv_w, conv_b, lru_wa, lru_ba, lru_wx, lru_bx, lru_L,
              w_ple, w_ple_gate, g_ple_in, g_ple_out):
    for i in range(DEPTH):
        h = rmsnorm(x, g_pre[i])
        uz = jnp.einsum('bsd,de->bse', h, w_in[i])
        u, z = uz[..., :D_INNER], uz[..., D_INNER:]
        j = i // N_MIXERS
        if i % N_MIXERS == 0:
            y = pool_mixer(u, pool_w[j], pool_b[j], pool_scale[j])
        else:
            uc = causal_depthwise_conv_2(u, conv_w[j], conv_b[j])
            y = rglru(uc, lru_wa[j], lru_ba[j], lru_wx[j], lru_bx[j], lru_L[j])
        y = y * jax.nn.silu(z)
        o = jnp.einsum('bse,ed->bsd', y, w_out[i])
        x = x + rmsnorm(o, g_post[i])
        gate = jax.nn.sigmoid(jnp.einsum('bsd,de->bse', rmsnorm(x, g_ple_in[i]), w_ple_gate[i]))
        e = jnp.einsum('bsk,kd->bsd', p[i], w_ple[i])
        x = x + rmsnorm(e * gate, g_ple_out[i])
    return x


def setup_inputs(seed=0):
    out = dict(first_inputs(seed))
    for name, value in second_inputs(seed + 1).items():
        if name != "x":
            out[name + "_2"] = value
    return out


def reference(
    x, positions, norm_w, w_in, q_norm_w, k_norm_w, sinks, b_conv_w, b_conv_b, b_ln_w, b_ln_b,
    b_pw_w, b_pw_b, c_conv_w, c_a_log, c_dt_bias, c_onorm_w, w_out, p_2, w_in_2, w_out_2,
    g_pre_2, g_post_2, pool_w_2, pool_b_2, pool_scale_2, conv_w_2, conv_b_2, lru_wa_2, lru_ba_2,
    lru_wx_2, lru_bx_2, lru_L_2, w_ple_2, w_ple_gate_2, g_ple_in_2, g_ple_out_2,
):
    x = first_block(
        x, positions, norm_w, w_in, q_norm_w, k_norm_w, sinks, b_conv_w, b_conv_b, b_ln_w,
        b_ln_b, b_pw_w, b_pw_b, c_conv_w, c_a_log, c_dt_bias, c_onorm_w, w_out,
    )
    return second_block(
        x, p_2, w_in_2, w_out_2, g_pre_2, g_post_2, pool_w_2, pool_b_2, pool_scale_2, conv_w_2,
        conv_b_2, lru_wa_2, lru_ba_2, lru_wx_2, lru_bx_2, lru_L_2, w_ple_2, w_ple_gate_2,
        g_ple_in_2, g_ple_out_2,
    )


_drawn_inputs = setup_inputs


def setup_inputs(seed=0):
    import zlib

    import numpy as np

    out = dict(_drawn_inputs(seed))
    spreads = {}
    factors = {'norm_w': 2.894,
     'q_norm_w': 8.0,
     'k_norm_w': 8.0,
     'sinks': 18.051,
     'b_conv_b': 5.075,
     'b_ln_w': 8.0,
     'b_ln_b': 8.0,
     'b_pw_b': 6.482,
     'c_onorm_w': 5.056,
     'conv_b_2': 26.952,
     'lru_ba_2': 194.001,
     'lru_bx_2': 64.0,
     'g_ple_in_2': 32.84,
     'g_pre_2': 6.934,
     'g_post_2': 8.0,
     'pool_b_2': 8.0,
     'pool_scale_2': 8.0,
     'lru_wa_2': 4.732,
     'g_ple_out_2': 8.0}
    for name, (base, spread) in spreads.items():
        noise = np.random.default_rng([zlib.crc32(name.encode()), seed]).standard_normal(out[name].shape)
        drawn = base * np.exp(spread * noise) if base else spread * noise
        out[name] = __import__('jax').numpy.asarray(drawn.astype(out[name].dtype))
    for name, factor in factors.items():
        out[name] = (out[name] * factor).astype(out[name].dtype)
    return out
```

```python
import numpy as np
import concourse.bass as bass
from concourse import mybir
from contextlib import ExitStack

F32 = mybir.dt.float32
I32 = mybir.dt.int32
ALU = mybir.AluOpType
ACT = mybir.ActivationFunctionType
AX = mybir.AxisListType

T = 256
NSLOT = 6
SLOT = 2048
LNEXP = "natural_log_exp_and_others"



def plan():
    ch = []

    def cols(name, l, c0, n, nkt=16, step=4):
        for k in range(0, nkt, step):
            ch.append((name, l, k, min(step, nkt - k), c0, n))

    for l in range(2):
        for i in range(4):
            cols("w_in", l, 3584 + 512 * i, 512)
        cols("w_in", l, 5632, 268)
        cols("w_in", l, 5900, 512)
        cols("w_in", l, 6412, 256, step=8)
        for c in (2048, 2560, 3072, 0, 512):
            cols("w_in", l, c, 512)
        cols("w_in", l, 1024, 256, step=8)
        cols("b_pw_w", l, 0, 512, nkt=4)
        cols("w_in", l, 1280, 512)
        cols("w_in", l, 1792, 256, step=8)
        late = ((6, 4), (10, 4), (14, 2))
        soon = ((0, 4), (4, 2))
        for part, gs in ((late, (0, 1)), (soon, (0, 1)), (late + soon, (2,)), (late + soon, (3,))):
            for g in gs:
                for k, n in part:
                    ch.append(("w_out", l, k, n, 512 * g, 512))
    for l in range(2):
        if l == 0:
            def u(g):
                for i in range(2):
                    cols("w_in_2", 0, 1024 * g + 512 * i, 512)

            def z(g):
                for i in range(2):
                    cols("w_in_2", 0, 4096 + 1024 * g + 512 * i, 512)

            def pool(g):
                for i in range(2):
                    for k in (0, 4):
                        ch.append(("pool_w_2", g, k, 4, 512 * i, 512))

            u(0)
            for g in range(4):
                z(g)
                if g < 3:
                    u(g + 1)
                pool(g)
        else:
            def gates(g):
                ch.append(("lru_wa_2", 0, 8 * g, 8, 0, 256))
                ch.append(("lru_wx_2", 0, 8 * g, 8, 0, 256))

            for g in range(4):
                for i in range(2):
                    cols("w_in_2", 1, 1024 * g + 512 * i, 512)
                for i in range(2):
                    cols("w_in_2", 1, 4096 + 1024 * g + 512 * i, 512)
                gates(g)
        for g in range(4):
            cols("w_out_2", l, 512 * g, 512, nkt=32)
        for g in range(2):
            ch.append(("w_ple_2", l, 0, 2, 1024 * g, 1024))
        for g in range(4):
            cols("w_ple_gate_2", l, 512 * g, 512)
    return ch



def const_columns():
    i = np.arange(128)
    c = {}
    c["ident"] = np.eye(128)
    same = (i[:, None] // 64) == (i[None, :] // 64)
    c["cum"] = same & (i[:, None] <= i[None, :])
    c["last"] = same
    c["incl"] = same & (i[:, None] <= i[None, :])
    c["strict"] = -1.0 * (same & (i[:, None] < i[None, :]))
    up = lambda m: ((i[:, None] // m) == (i[None, :] // m)) & ((i[:, None] % m) < m // 2) & ((i[None, :] % m) >= m // 2)
    c["lv2"] = up(2)
    for m in (4, 8, 16, 32, 64):
        c[f"lv{m}"] = up(m).T
    q = i[:, None]
    k = i[None, :]
    neg = np.float32(-1e30)
    c["amask"] = np.concatenate([np.where(k <= q, 0, neg), np.where(k > q, 0, neg), np.where(k <= q, 0, neg)], axis=1)
    c["ones"] = np.ones((128, 128))
    c["eps"] = np.full((128, 1), 1e-6)
    c["zero"] = np.zeros((128, 1))
    inv = np.float32(500000.0) ** (-np.arange(0, 16, 2, dtype=np.float32) / np.float32(16))
    c["invf"] = np.broadcast_to(inv, (128, 8))
    for g, w in enumerate((2, 4, 8, 16)):
        cnt = np.minimum(np.arange(1, T + 1), w)
        c[f"cnt{g}"] = np.broadcast_to(1.0 / cnt.astype(np.float32), (128, T))
    return {n: np.ascontiguousarray(v, dtype=np.float32) for n, v in c.items()}


CHAN = ["norm_w", "b_conv_w", "b_conv_b", "b_ln_w", "b_ln_b", "b_pw_b", "c_conv_w", "c_onorm_w", "g_pre_2",
        "pool_b_2", "pool_scale_2", "conv_w_2", "conv_b_2", "lru_ba_2", "lru_bx_2", "lru_L_2", "g_ple_in_2"]
ROW = ["q_norm_w", "k_norm_w", "sinks", "c_a_log", "c_dt_bias"]
SHAPE = {"norm_w": (2, 2048), "b_conv_w": (2, 31, 512), "b_conv_b": (2, 512), "b_ln_w": (2, 512), "b_ln_b": (2, 512),
         "b_pw_b": (2, 512), "c_conv_w": (2, 4, 2304), "c_onorm_w": (2, 128), "g_pre_2": (2, 2048),
         "pool_b_2": (1, 4096), "pool_scale_2": (1, 4096), "conv_w_2": (1, 4, 4096), "conv_b_2": (1, 4096),
         "lru_ba_2": (1, 4096), "lru_bx_2": (1, 4096), "lru_L_2": (1, 4096), "g_ple_in_2": (2, 2048),
         "q_norm_w": (2, 64), "k_norm_w": (2, 64), "sinks": (2, 12), "c_a_log": (2, 6), "c_dt_bias": (2, 6)}


def column_table():
    at, n = {}, 0
    for name, v in const_columns().items():
        at[name] = n
        n += v.shape[1]
    for name in CHAN:
        at[name] = n
        n += int(np.prod(SHAPE[name])) // 128
    for name in ROW:
        at[name] = n
        n += int(np.prod(SHAPE[name]))
    return at, n


class Eng:

    def __init__(self, sem, chain=False):
        self.sem, self.n, self.q, self.seen, self.chain = sem, 0, [], {}, chain

    def wait(self, *toks):
        for t in toks:
            if t is None:
                continue
            if isinstance(t, list):
                self.wait(*t)
            elif self.seen.get(id(t[0]), 0) < t[1]:
                self.seen[id(t[0])] = t[1]
                self.q.append(("wait", t[0], t[1]))

    def op(self, fn, *toks, inc=True):
        self.wait(*toks)
        if self.chain and self.n:
            self.wait((self.sem, self.n))
        self.q.append(("op", fn, inc))
        if inc:
            self.n += 1
            return (self.sem, self.n)
        return None

    def play(self, e):
        for item in self.q:
            if item[0] == "wait":
                e.wait_ge(item[1], item[2])
            elif item[2]:
                item[1](e).then_inc(self.sem, 1)
            else:
                item[1](e)


def program(nc, wall, tab, pos_d, pT_d, xin, gpost_d, gplo_d, out):
    chunks = plan()
    AT, NT = column_table()
    ctx = ExitStack()
    with ctx:
        X = ctx.enter_context(nc.sbuf_tensor("X", [128, 2, 2048], F32))
        H = ctx.enter_context(nc.sbuf_tensor("H", [128, 16, 256], F32))
        Y = ctx.enter_context(nc.sbuf_tensor("Y", [128, 16, 256], F32))
        W = ctx.enter_context(nc.sbuf_tensor("W", [128, NSLOT, SLOT], F32))
        TB = ctx.enter_context(nc.sbuf_tensor("TB", [128, NT], F32))
        SM = ctx.enter_context(nc.sbuf_tensor("SM", [128, 1024], F32))
        NS = 22560
        SC = ctx.enter_context(nc.sbuf_tensor("SC", [128, NS], F32))
        POSI = ctx.enter_context(nc.sbuf_tensor("POSI", [128, 2], I32))
        PS = ctx.enter_context(nc.psum_tensor("PS", [128, 4096], F32))

        def sem(n):
            return ctx.enter_context(nc.semaphore(n))

        pe, dv, ac = Eng(sem("s_pe")), Eng(sem("s_dv"), chain=True), Eng(sem("s_ac"), chain=True)
        s_slot = [sem(f"s_w{i}") for i in range(NSLOT)]
        s_tab, s_x, s_g, s_out = sem("s_tab"), sem("s_x"), sem("s_g"), sem("s_out")
        sync_late = []

        def tb(name, off=0, n=1):
            return TB[:, AT[name] + off:AT[name] + off + n]

        def tbl(name, n=128):
            return TB[:, AT[name]:AT[name] + n]

        def row(name, l):
            w = SHAPE[name][1]
            return TB[:, AT[name] + l * w:AT[name] + (l + 1) * w]

        ident, ones = tbl("ident"), tbl("ones")
        tabt, xt = (s_tab, 48), (s_x, 32)

        def sc(off, n):
            assert off + n <= NS, (off, n)
            return SC[:, off:off + n]

        def tt(o, a, b, op, *w):
            return dv.op(lambda e: e.tensor_tensor(o, a, b, op), *w)

        def stt(o, a, s, b, op0, op1, *w):
            return dv.op(lambda e: e.scalar_tensor_tensor(out=o, in0=a, scalar=s, in1=b, op0=op0, op1=op1), *w)

        def ts(o, a, s1, s2, op0, op1, *w):
            if s2 is None:
                return dv.op(lambda e: e.tensor_scalar(o, a, s1, None, op0), *w)
            return dv.op(lambda e: e.tensor_scalar(o, a, s1, s2, op0, op1), *w)

        def act(o, a, f, *w, **k):
            return ac.op(lambda e: e.activation(o, a, f, **k), *w)

        def lnexp():
            ac.op(lambda e: e.preload_act_table_set(LNEXP), inc=False)

        def mm(o, l, r, *w, start=True, stop=True, inc=False):
            return pe.op(lambda e: e.matmul(o, l, r, start=start, stop=stop, skip_group_check=True), *w, inc=inc)

        def tp(o, a, *w, inc=False):
            return pe.op(lambda e: e.transpose(o, a, ident), *w, inc=inc)

        side_free = [None] * 4
        side_at = [0]

        def side():
            i = side_at[0] % 4
            side_at[0] += 1
            return i, side_free[i]

        def sbank(i):
            return PS[:, 2048 + 512 * i:2560 + 512 * i]

        main_free = [None, None]
        main_at = [0]
        sides = []

        def pump():
            for g in list(sides):
                try:
                    next(g)
                except StopIteration:
                    sides.remove(g)

        def finish(g):
            while g in sides:
                pump()

        used = [0]
        released = []

        class Group:

            def __init__(self, src, src_toks, ncols, mode, nk):
                self.i = main_at[0] % 2
                main_at[0] += 1
                self.bank = [PS[:, 1024 * self.i + 512 * b:1024 * self.i + 512 * b + 512] for b in range(2)]
                self.free = main_free[self.i]
                self.src, self.src_toks, self.ncols, self.mode, self.nk, self.done = src, src_toks, ncols, mode, nk, 0

            def feed(self, kts=None, col=0, last_use=True, stride=None):
                c = used[0]
                name, l, k0, nk, c0, n = chunks[c]
                slot = c % NSLOT
                w = W[:, slot, 0:nk * n].rearrange("p (k n) -> p k n", k=nk)
                pe.wait((s_slot[slot], 16 * (c // NSLOT + 1)), self.free)
                kts = range(k0, k0 + nk) if kts is None else kts
                for kl, kt in enumerate(kts):
                    first, last = self.done == 0, self.done == self.nk - 1
                    s = self.src(kt)
                    tok = self.src_toks(kt)
                    end = kl == nk - 1
                    if self.mode == "cm":
                        m = self.ncols // 128
                        for j in range(m):
                            t = mm(self.bank[j // 2][:, 256 * (j % 2):256 * (j % 2) + 256],
                                   w[:, kl, col + 128 * j:col + 128 * j + 128], s, tok,
                                   start=first and j % 2 == 0, stop=last, inc=end and j == m - 1)
                    elif self.mode == "cm+":
                        for j in range(2):
                            mm(self.bank[0][:, 256 * j:256 * j + 256], w[:, kl, 128 * j:128 * j + 128], s, tok,
                               start=first and j == 0, stop=last)
                        for j in range(2):
                            t = mm(self.bank[1][:, 16 * j:16 * j + 12], s[:, 128 * j:128 * j + 128], w[:, kl, 256:268],
                                   start=first and j == 0, stop=last, inc=end and j == 1)
                    else:
                        for j in range(2):
                            t = mm(self.bank[j][:, 0:self.ncols], s[:, 128 * j:128 * j + 128],
                                   w[:, kl, col:col + self.ncols], tok, start=first, stop=last,
                                   inc=end and j == 1)
                    self.done += 1
                self.tok = t
                if last_use:
                    used[0] += 1
                    released.append(t)
                pump()

            def all(self):
                while self.done < self.nk:
                    self.feed()
                return self

            def free_with(self, toks):
                main_free[self.i] = toks

        def from_h(kt):
            return H[:, kt, :]

        h_tok = [None] * 16

        def ht(kt):
            return h_tok[kt]

        def proj(ncols, mode="cm", nk=16):
            return Group(from_h, ht, ncols, mode, nk).all()

        x_tok = [xt] * 4
        h_read = [None]
        NXN = 0

        sq_war = [None]

        def sumsq(g, tok, scratch):
            for t in range(2):
                r = act(scratch, X[:, t, 512 * g:512 * g + 512], ACT.Square, tok, sq_war[0],
                        accum_out=SM[:, 4 * t + g:4 * t + g + 1])
            sq_war[0] = None
            return r

        def rstd_of(ssum, n, o, tok, eps="eps"):
            lnexp()
            a = act(o, ssum, ACT.Ln, tok, tabt, scale=1.0 / n, bias=tb(eps))
            return act(o, o, ACT.Exp, a, scale=-0.5, bias=0.0)

        def norm_to_h(gname, l, ss_tok, xn, xn_war):
            a = dv.op(lambda e: e.tensor_reduce(SM[:, 8:10], SM[:, 0:8].rearrange("p (t g) -> p t g", t=2), AX.X,
                                                ALU.add), ss_tok)
            r = rstd_of(SM[:, 8:10], 2048, SM[:, 10:12], a)
            xv = xn.rearrange("p (t c) -> p t c", t=2)
            xtk = {}
            for g in range(4):
                for t in range(2):
                    xtk[g] = ts(xv[:, t, 512 * g:512 * g + 512], X[:, t, 512 * g:512 * g + 512], SM[:, 10 + t:11 + t],
                                None, ALU.mult, None, r, x_tok[g], xn_war)
            off = AT[gname] + 16 * l
            for k in range(0, 16, 2):
                i, fr = side()
                for j in range(2):
                    for t in range(2):
                        c = 128 * (k + j)
                        p = tp(sbank(i)[:, 256 * j + 128 * t:256 * j + 128 * t + 128], xv[:, t, c:c + 128],
                               fr, xtk[k // 4], tabt, inc=(j == 1 and t == 1))
                for j in range(2):
                    g_ap = TB[:, off + k + j:off + k + j + 1]
                    src = sbank(i)[:, 256 * j:256 * j + 256]
                    if k % 4 == 0:
                        t0 = h_tok[k + j] = ts(H[:, k + j, :], src, g_ap, None, ALU.mult, None, p, h_read[0])
                    else:
                        t1 = h_tok[k + j] = act(H[:, k + j, :], src, ACT.Copy, p, h_read[0], scale=g_ap)
                side_free[i] = h_tok[k + 1]
            return [t0, t1]

        ROPE = SM[:, 64:64 + 32]
        sin_t = ROPE[:, 0:16].rearrange("p (t c) -> p t c", t=2)
        cos_t = ROPE[:, 16:32].rearrange("p (t c) -> p t c", t=2)

        def rope_tables():
            posf = SM[:, 12:14]
            ang = SM[:, 16:32]
            kk = SM[:, 32:48]
            a = dv.op(lambda e: e.tensor_copy(posf, POSI[:, :]), tabt)
            for t in range(2):
                b = ts(ang[:, 8 * t:8 * t + 8], tbl("invf", 8), posf[:, t:t + 1], None, ALU.mult, None, a)
            C1, C2 = 6.28125, float(np.float32(2 * np.pi - 6.28125))
            C3 = float(np.float32(2 * np.pi - 6.28125 - float(np.float32(2 * np.pi - 6.28125))))
            MAGIC = 12582912.0
            lim = 3.1415925
            for shift, add, dst in ((0.0, 0.0, ROPE[:, 0:16]), (0.25, float(np.float32(np.pi / 2)), ROPE[:, 16:32])):
                b = ts(kk, ang, float(1 / (2 * np.pi)), shift, ALU.mult, ALU.add, b)
                b = ts(kk, kk, MAGIC, None, ALU.add, None, b)
                b = ts(kk, kk, -MAGIC, None, ALU.add, None, b)
                b = stt(dst, kk, -C1, ang, ALU.mult, ALU.add, b)
                b = stt(dst, kk, -C2, dst, ALU.mult, ALU.add, b)
                b = stt(dst, kk, -C3, dst, ALU.mult, ALU.add, b)
                b = ts(dst, dst, add, lim, ALU.add, ALU.min, b)
                b = ts(dst, dst, -lim, None, ALU.max, None, b)
            return act(ROPE, ROPE, ACT.Sin, b)

        def softplus(o, x, s, n, tok):
            e_, z, q = s[:, 0:n], s[:, n:2 * n], s[:, 2 * n:3 * n]
            a = act(e_, x, ACT.Abs, tok)
            a = act(e_, e_, ACT.Exp, a, scale=-1.0, bias=0.0)
            a = ts(z, e_, 2.0, None, ALU.add, None, a)
            a = dv.op(lambda e: e.reciprocal(z, z), a)
            a = tt(z, z, e_, ALU.mult, a)
            a = tt(q, z, z, ALU.mult, a)
            a = ts(e_, q, 1.0 / 17, None, ALU.mult, None, a)
            for k in (15, 13, 11, 9, 7, 5, 3):
                a = stt(e_, e_, 1.0 / k, q, ALU.add, ALU.mult, a)
            a = stt(e_, e_, 1.0, z, ALU.add, ALU.mult, a)
            a = ts(e_, e_, 2.0, None, ALU.mult, None, a)
            return stt(o, x, 0.0, e_, ALU.max, ALU.add, a)

        RAW = sc(0, 18 * 259).rearrange("p (i c) -> p i c", i=18)
        CT = sc(4662, 4608).rearrange("p (i c) -> p i c", i=18)
        CQ, CK, CV = sc(4662, 1536), sc(4662 + 1536, 1536), sc(4662 + 3072, 1536)
        o0 = 4662 + 4608
        KB, EG, DS, DI, KD, SS, VN = (sc(o0, 1536), sc(o0 + 1536, 1536), sc(o0 + 3072, 1536), sc(o0 + 4608, 1536),
                                      sc(o0 + 6144, 1536), sc(o0 + 7680, 1536), sc(o0 + 9216, 768))
        UU, TT_, XX = sc(0, 1536), sc(1536, 1536), sc(3072, 1536)
        RV, RW, U2, WT, OC = KB, CV, TT_, XX, DS

        def heads(ap):
            return ap.rearrange("p (h t c) -> p h t c", h=6, t=2)

        gs = SM[:, 128:512]
        c_free = [None]

        def delta_net(l, silu_tok, ba_tok, ba_bank_free):
            bt = gs[:, 0:12].rearrange("p (h t) -> p h t", h=6)
            gg = gs[:, 12:24].rearrange("p (h t) -> p h t", h=6)
            ea = gs[:, 24:30]
            gcs, gls = gs[:, 36:48], gs[:, 48:60]
            bw, kdw = gs[:, 60:72], gs[:, 72:84]
            th = gs[:, 84:96]
            a = act(th, gs[:, 120:132], ACT.Tanh, ba_tok, scale=0.5, bias=0.0)
            b1 = ts(gs[:, 0:12], th, 0.5, 0.5, ALU.mult, ALU.add, a)
            e1 = act(ea, row("c_a_log", l), ACT.Exp, tabt, scale=1.0, bias=0.0)
            a = tt(gs[:, 132:144].rearrange("p (h t) -> p h t", h=6), gs[:, 132:144].rearrange("p (h t) -> p h t", h=6),
                   row("c_dt_bias", l).unsqueeze(2).to_broadcast([128, 6, 2]), ALU.add, ba_tok)
            a = softplus(gs[:, 12:24], gs[:, 132:144], gs[:, 144:180], 12, a)
            a = ts(gs[:, 12:24], gs[:, 12:24], -1.0, None, ALU.mult, None, a)
            g_t = tt(gg, gg, ea.unsqueeze(2).to_broadcast([128, 6, 2]), ALU.mult, a, e1)
            sq = sc(0, 3072)
            q1 = act(sq, sc(4662, 3072), ACT.Square, silu_tok)
            yield
            yield
            i, fr = side()
            b = sbank(i)
            mm(b[:, 0:12], tbl("cum"), gs[:, 12:24], g_t, fr)
            p = mm(b[:, 16:28], tbl("last"), gs[:, 12:24], start=False, inc=True)
            a = dv.op(lambda e: e.tensor_copy(gs[:, 36:60].rearrange("p (a c) -> p a c", a=2),
                                              b[:, 0:32].rearrange("p (a c) -> p a c", a=2)[:, :, 0:12]), p)
            side_free[i] = a
            gc_t = a
            a1 = act(bw, gcs, ACT.Exp, a, scale=1.0, bias=0.0)
            bw_t = tt(bw, bw, gs[:, 0:12], ALU.mult, a1, b1)
            a2 = tt(kdw, gls, gcs, ALU.subtract, a)
            kd_t = act(kdw, kdw, ACT.Exp, a2, scale=1.0, bias=0.0)
            dsts = []
            for bk in range(3):
                i, fr = side()
                bnk = sbank(i)
                for j in range(4):
                    u = 4 * bk + j
                    p = mm(bnk[:, 128 * j:128 * j + 128], gs[:, 12 + u:13 + u].to_broadcast([128, 128]), tbl("cum"),
                           g_t, fr, start=(j == 0), inc=(j == 3))
                cs = slice(512 * bk, 512 * bk + 512)
                for j in range(4):
                    u = 4 * bk + j
                    d1 = ts(DI[:, 128 * u:128 * u + 128], bnk[:, 128 * j:128 * j + 128], gcs[:, u:u + 1], 0.0,
                            ALU.subtract, ALU.min, p, gc_t, c_free[0])
                e2 = act(EG[:, cs], bnk, ACT.Exp, p, d1, c_free[0], scale=1.0, bias=0.0)
                e3 = act(DI[:, cs], DI[:, cs], ACT.Exp, d1, scale=1.0, bias=0.0)
                side_free[i] = [d1, e2]
                dsts.append((e2, e3))
            eg_t, di_t = dsts[-1]
            yield
            lnexp()
            rn = sc(0, 3072)
            rt = []
            for k in range(6):
                i, fr = side()
                p = mm(sbank(i), ones, sq[:, 512 * k:512 * k + 512], q1, fr, inc=True)
                a = act(rn[:, 512 * k:512 * k + 512], sbank(i), ACT.Ln, p, scale=1.0, bias=tb("eps"))
                side_free[i] = a
                rt.append(a)
            a = act(rn, rn, ACT.Exp, a, scale=-0.5, bias=0.0)
            q_t = stt(CQ, CQ, float(128 ** -0.5), rn[:, 0:1536], ALU.mult, ALU.mult, a)
            k_t = tt(CK, CK, rn[:, 1536:3072], ALU.mult, a)
            yield
            for bk in range(3):
                i, fr = side()
                bnk = sbank(i)
                for j in range(4):
                    u = 4 * bk + j
                    p = mm(bnk[:, 128 * j:128 * j + 128], gs[:, u:u + 1].to_broadcast([128, 128]), ident,
                           b1, fr, start=(j == 0), inc=(j == 3))
                cs = slice(512 * bk, 512 * bk + 512)
                kb_t = tt(KB[:, cs], CK[:, cs], bnk, ALU.mult, p, k_t)
                side_free[i] = kb_t
            ds_t = tt(DS.rearrange("p (u c) -> p u c", u=12), DI.rearrange("p (u c) -> p u c", u=12),
                      tbl("strict").unsqueeze(1).to_broadcast([128, 12, 128]), ALU.mult, di_t)
            dm_t = tt(DI.rearrange("p (u c) -> p u c", u=12), DI.rearrange("p (u c) -> p u c", u=12),
                      tbl("incl").unsqueeze(1).to_broadcast([128, 12, 128]), ALU.mult, ds_t)
            yield
            for bk in range(3):
                cs = slice(512 * bk, 512 * bk + 512)
                for dst, rhs_, tok in ((DS, KB, kb_t), (DI, CQ, q_t)):
                    i, fr = side()
                    bnk = sbank(i)
                    for j in range(4):
                        u = 4 * bk + j
                        us = slice(128 * u, 128 * u + 128)
                        p = mm(bnk[:, 128 * j:128 * j + 128], CK[:, us], rhs_[:, us], k_t, tok, fr, start=(j == 0),
                               inc=(j == 3))
                    a = tt(dst[:, cs], bnk, dst[:, cs], ALU.mult, p, ds_t, dm_t)
                    side_free[i] = a
                    if dst is DS:
                        v3 = UU[:, cs].rearrange("p (u c) -> p u c", u=4)
                        b_ = tt(v3, DS[:, cs].rearrange("p (u c) -> p u c", u=4),
                                tbl("lv2").unsqueeze(1).to_broadcast([128, 4, 128]), ALU.mult, a, k_t, q_t)
                        u_t = tt(v3, v3, ident.unsqueeze(1).to_broadcast([128, 4, 128]), ALU.add, b_)
                        ns_t = a
                    else:
                        in_t = a
            yield
            for bk in range(3):
                i, fr = side()
                bnk = sbank(i)
                cs = slice(512 * bk, 512 * bk + 512)
                for j in range(4):
                    u = 4 * bk + j
                    p = tp(bnk[:, 128 * j:128 * j + 128], UU[:, 128 * u:128 * u + 128], u_t, fr, inc=(j == 3))
                t_t = act(TT_[:, cs], bnk, ACT.Copy, p, q_t, k_t)
                side_free[i] = t_t
            lastk = None
            for src, which in ((CV, "v"), (CK, "k")):
                for bk in range(3):
                    i, fr = side()
                    bnk = sbank(i)
                    cs = slice(512 * bk, 512 * bk + 512)
                    for j in range(4):
                        u = 4 * bk + j
                        p = tp(bnk[:, 128 * j:128 * j + 128], src[:, 128 * u:128 * u + 128], fr, silu_tok, k_t,
                               inc=(j == 3))
                    b3 = bnk.rearrange("p (u c) -> p u c", u=4)

                    def per(v):
                        return v[:, 4 * bk:4 * bk + 4].unsqueeze(2).to_broadcast([128, 4, 128])
                    r3 = lambda v: v[:, cs].rearrange("p (u c) -> p u c", u=4)
                    if which == "v":
                        a = tt(r3(RV), b3, per(gs[:, 0:12]), ALU.mult, p, b1, ns_t, in_t)
                        side_free[i] = a
                        vtp = p
                        rv_t = a
                    else:
                        a = tt(r3(RW), b3, per(bw), ALU.mult, p, bw_t, vtp)
                        a2 = tt(r3(KD), b3, per(kdw), ALU.mult, kd_t, c_free[0])
                        side_free[i] = [a, a2]
                        rw_t, kdt = a, a2
            qg_t = tt(CQ, CQ, EG, ALU.mult, eg_t, in_t)
            yield
            for m in (4, 8, 16, 32, 64):
                for bk in range(3):
                    i, fr = side()
                    bnk = sbank(i)
                    cs = slice(512 * bk, 512 * bk + 512)
                    for j in range(4):
                        u = 4 * bk + j
                        us = slice(128 * u, 128 * u + 128)
                        p = mm(bnk[:, 128 * j:128 * j + 128], DS[:, us], TT_[:, us], t_t, ns_t, fr, start=(j == 0),
                               inc=(j == 3))
                    a = tt(XX[:, cs].rearrange("p (u c) -> p u c", u=4), bnk.rearrange("p (u c) -> p u c", u=4),
                           tbl(f"lv{m}").unsqueeze(1).to_broadcast([128, 4, 128]), ALU.mult, p, u_t)
                    side_free[i] = a
                    x_t = a
                yield
                ups = []
                for bk in range(3):
                    cs = slice(512 * bk, 512 * bk + 512)
                    for which in (0, 1) if m < 64 else (0,):
                        i, fr = side()
                        bnk = sbank(i)
                        for j in range(4):
                            u = 4 * bk + j
                            us = slice(128 * u, 128 * u + 128)
                            l_, r_ = (XX[:, us], UU[:, us]) if which == 0 else (UU[:, us], XX[:, us])
                            p = mm(bnk[:, 128 * j:128 * j + 128], l_, r_, x_t, u_t, fr, start=(j == 0), inc=(j == 3))
                        ups.append((which, cs, bnk, i))
                    for which, cs2, bnk, i in ups:
                        dst = UU if which == 0 else TT_
                        a = tt(dst[:, cs2], dst[:, cs2], bnk, ALU.add, p)
                        side_free[i] = a
                        if which == 0:
                            u_t2 = a
                        else:
                            t_t = a
                    ups = []
                u_t = u_t2
                yield
            for bk in range(3):
                cs = slice(512 * bk, 512 * bk + 512)
                for which in (0, 1):
                    i, fr = side()
                    bnk = sbank(i)
                    for j in range(4):
                        u = 4 * bk + j
                        us = slice(128 * u, 128 * u + 128)
                        l_, r_ = (UU[:, us], RV[:, us]) if which == 0 else (RW[:, us], UU[:, us])
                        p = mm(bnk[:, 128 * j:128 * j + 128], l_, r_, u_t, rv_t, rw_t, fr, start=(j == 0),
                               inc=(j == 3))
                    dst = (U2, WT)[which]
                    a = act(dst[:, cs], bnk, ACT.Copy, p, u_t, t_t)
                    side_free[i] = a
                    uw_t = a
            s_t = dv.op(lambda e: e.memset(SS[:, 0:768], 0.0), c_free[0])
            yield
            EG4 = EG.rearrange("p (h t) -> p h t", h=6)
            o_rd = [None, None]
            for c in range(4):
                half, p0 = c // 2, 64 * (c % 2)
                S = SS[:, 768 * (c % 2):768 * (c % 2) + 768]
                S2 = SS[:, 768 * ((c + 1) % 2):768 * ((c + 1) % 2) + 768]
                (i1, f1), (i2, f2) = side(), side()
                for h in range(6):
                    bnk = sbank(i1) if h < 4 else sbank(i2)
                    hh = h % 4
                    us = 256 * h + 128 * half + p0
                    p = mm(bnk[p0:p0 + 64, 128 * hh:128 * hh + 128], WT[:, us:us + 64], S[:, 128 * h:128 * h + 128],
                           s_t, uw_t, f1, f2, start=(hh == 0), inc=(h in (3, 5)))
                for n_, i_, h0, nh in ((0, i1, 0, 4), (1, i2, 4, 2)):
                    v_t = tt(VN[p0:p0 + 64, 128 * h0:128 * (h0 + nh)].rearrange("p (h c) -> p h c", h=nh),
                             heads(U2)[p0:p0 + 64, h0:h0 + nh, half, :],
                             sbank(i_)[p0:p0 + 64, 0:128 * nh].rearrange("p (h c) -> p h c", h=nh),
                             ALU.subtract, p, uw_t, o_rd[c % 2])
                    side_free[i_] = v_t
                yield
                if c < 3:
                    (i1, f1), (i2, f2) = side(), side()
                    for h in range(6):
                        bnk = sbank(i1) if h < 4 else sbank(i2)
                        hh = h % 4
                        us = 256 * h + 128 * half
                        p = mm(bnk[:, 128 * hh:128 * hh + 128], KD[p0:p0 + 64, us:us + 128],
                               VN[p0:p0 + 64, 128 * h:128 * h + 128], v_t, kdt, f1, f2, start=(hh == 0),
                               inc=(h in (3, 5)))
                    for h in range(6):
                        i_ = i1 if h < 4 else i2
                        hh = h % 4
                        s_n = stt(S2[:, 128 * h:128 * h + 128], S[:, 128 * h:128 * h + 128],
                                  EG4[:, h, 64 * c + 63:64 * c + 64], sbank(i_)[:, 128 * hh:128 * hh + 128],
                                  ALU.mult, ALU.add, p, o_rd[(c + 1) % 2], eg_t)
                        side_free[i_] = s_n
                i, fr = side()
                for h in range(6):
                    ob = sbank(i)[:, 64 * h:64 * h + 64]
                    cs = slice(256 * h + 64 * c, 256 * h + 64 * c + 64)
                    mm(ob, S[:, 128 * h:128 * h + 128], CQ[:, cs], fr, qg_t, start=(h == 0), stop=False)
                    u0 = 256 * h + 128 * half + p0
                    p = mm(ob, VN[p0:p0 + 64, 128 * h:128 * h + 128], DI[p0:p0 + 64, u0:u0 + 64], v_t, in_t,
                           start=False, inc=(h == 5))
                o_t = act(OC.rearrange("p (h t) -> p h t", h=6)[:, :, 64 * c:64 * c + 64],
                          sbank(i)[:, 0:384].rearrange("p (h t) -> p h t", h=6), ACT.Copy, p, u_t)
                side_free[i] = o_t
                o_rd[c % 2] = p
                if c < 3:
                    s_t = s_n
                yield
            a = act(XX, OC, ACT.Square, o_t)
            yield
            lnexp()
            for k in range(3):
                i, fr = side()
                p = mm(sbank(i), ones, XX[:, 512 * k:512 * k + 512], a, fr, inc=True)
                r = act(TT_[:, 512 * k:512 * k + 512], sbank(i), ACT.Ln, p, scale=1.0 / 128, bias=tb("eps"))
                side_free[i] = r
            r = act(TT_, TT_, ACT.Exp, r, scale=-0.5, bias=0.0)
            a = stt(OC, OC, TB[:, AT["c_onorm_w"] + l:AT["c_onorm_w"] + l + 1], TT_, ALU.mult, ALU.mult, r)
            yc = Y[:, 10:16, :].rearrange("p i c -> p (i c)")
            c_done[0] = tt(yc, yc, OC, ALU.mult, a, zc_tok[0])

        c_done, zc_tok, zb_tok, za_tok, b_ready, a_done = [None], [None], [None], [None], [None], [None]

        def conformer(l, hb, acc, tmp, h_t):
            wo = AT["b_conv_w"] + 124 * l
            av = acc.rearrange("p (m c) -> p m c", m=4)
            last = [None] * 4
            for k in range(31):
                for m in range(4):
                    wk = TB[:, wo + 4 * k + m:wo + 4 * k + m + 1]
                    if k == 0:
                        last[m] = ts(av[:, m, :], hb[:, m, 0:256], wk, tb("b_conv_b", 4 * l + m), ALU.mult, ALU.add,
                                     h_t)
                    else:
                        last[m] = stt(av[:, m, :], hb[:, m, k:k + 256], wk, av[:, m, :], ALU.mult, ALU.add, last[m])
                if k % 8 == 7:
                    yield
            yield
            i, fr = side()
            for m in range(4):
                p = mm(sbank(i)[:, 0:256], ones, av[:, m, :], last[m], fr, start=(m == 0), stop=(m == 3),
                       inc=(m == 3))
            a = stt(av, sbank(i)[:, 0:256].unsqueeze(1).to_broadcast([128, 4, 256]), -1.0 / 512, av,
                    ALU.mult, ALU.add, p)
            side_free[i] = a
            c_t = a
            a = act(tmp, acc, ACT.Square, a)
            yield
            i, fr = side()
            tv = tmp.rearrange("p (m c) -> p m c", m=4)
            for m in range(4):
                p = mm(sbank(i)[:, 0:256], ones, tv[:, m, :], a, fr, start=(m == 0), stop=(m == 3), inc=(m == 3))
            rs = tmp[:, 0:256]
            lnexp()
            r = act(rs, sbank(i)[:, 0:256], ACT.Ln, p, scale=1.0 / 512, bias=tb("eps"))
            side_free[i] = r
            r = act(rs, rs, ACT.Exp, r, scale=-0.5, bias=0.0)
            a = tt(av, av, rs.unsqueeze(1).to_broadcast([128, 4, 256]), ALU.mult, r, c_t)
            for m in range(4):
                r = act(av[:, m, :], av[:, m, :], ACT.Silu, a, scale=tb("b_ln_w", 4 * l + m),
                        bias=tb("b_ln_b", 4 * l + m))
            b_ready[0] = r

        QK = sc(0, 2048)
        KR = sc(2048, 1024)
        AV = sc(3072, 512)
        QT = sc(3584, 1536)
        KT2 = sc(5120, 1024)
        AS = sc(6144, 4608)
        AP_ = sc(10752, 4608)
        SQ = sc(15360, 2048)

        def attention(l, qk_t, v_t):
            qk3 = QK.rearrange("p (n d) -> p n d", d=64)
            sm = SM[:, 512:640]
            a = act(SQ, QK, ACT.Square, qk_t)
            a = dv.op(lambda e: e.tensor_reduce(sm[:, 0:32], SQ.rearrange("p (n d) -> p n d", d=64), AX.X, ALU.add), a)
            a = rstd_of(sm[:, 0:32], 64, sm[:, 0:32], a)
            a = tt(qk3, qk3, sm[:, 0:32].unsqueeze(2).to_broadcast([128, 32, 64]), ALU.mult, a)
            for t in range(2):
                for n0, n1, wn in ((0, 12, "q_norm_w"), (12, 16, "k_norm_w")):
                    v = qk3[:, 16 * t + n0:16 * t + n1, :]
                    b = tt(v, v, row(wn, l).unsqueeze(1).to_broadcast([128, n1 - n0, 64]), ALU.mult, a)
            q4 = QK.rearrange("p (t n d) -> p t n d", t=2, n=16)
            x1, x2 = q4[:, :, :, 0:8], q4[:, :, :, 8:16]
            cb = cos_t.unsqueeze(2).to_broadcast([128, 2, 16, 8])
            sb_ = sin_t.unsqueeze(2).to_broadcast([128, 2, 16, 8])
            r4 = [SQ[:, 256 * i:256 * i + 256].rearrange("p (t n d) -> p t n d", t=2, n=16) for i in range(4)]
            tt(r4[0], x1, cb, ALU.mult, b, rope_tok[0])
            tt(r4[1], x2, sb_, ALU.mult)
            tt(r4[2], x2, cb, ALU.mult)
            c = tt(r4[3], x1, sb_, ALU.mult)
            tt(x1, r4[0], r4[1], ALU.subtract, c)
            c = tt(x2, r4[2], r4[3], ALU.add)
            kr = KR.rearrange("p (t n r d) -> p t n r d", t=2, n=4, r=2)
            for t in range(2):
                d = dv.op(lambda e, t=t: e.tensor_copy(kr[:, t], q4[:, t, 12:16, :].unsqueeze(2).to_broadcast(
                    [128, 4, 2, 64])), c)
            yield
            yield
            qt = QT.rearrange("p (i t) -> p i t", i=6)
            kt2 = KT2.rearrange("p (i t) -> p i t", i=4)
            for bk in range(5):
                i, fr = side()
                for j in range(2):
                    n = 2 * bk + j
                    for t in range(2):
                        src = q4[:, t, 2 * n:2 * n + 2, :].rearrange("p a d -> p (a d)") if n < 6 else \
                            kr[:, t, n - 6, :, :].rearrange("p r d -> p (r d)")
                        p = tp(sbank(i)[:, 256 * j + 128 * t:256 * j + 128 * t + 128], src, d, fr,
                               inc=(j == 1 and t == 1))
                dst = QT[:, 512 * bk:512 * bk + 512] if bk < 3 else KT2[:, 512 * (bk - 3):512 * (bk - 3) + 512]
                a = act(dst, sbank(i), ACT.Copy, p)
                side_free[i] = a
            yield
            s3 = AS.rearrange("p (h c) -> p h c", h=12)
            p3 = AP_.rearrange("p (h c) -> p h c", h=12)
            m2 = sm[:, 32:56].rearrange("p (b h) -> p b h", b=2)
            nm = sm[:, 56:80].rearrange("p (b h) -> p b h", b=2)
            den = sm[:, 80:104].rearrange("p (b h) -> p b h", b=2)
            es = sm[:, 104:128].rearrange("p (b h) -> p b h", b=2)
            for h in range(12):
                i, fr = side()
                b0 = 64 * (h % 2)
                mm(sbank(i)[:, 0:128], qt[b0:b0 + 64, h // 2, 0:128], kt2[b0:b0 + 64, h // 3, 0:128], a, fr)
                p = mm(sbank(i)[:, 128:384], qt[b0:b0 + 64, h // 2, 128:256], kt2[b0:b0 + 64, h // 3, 0:256],
                       start=False, inc=True)
                s_t = stt(s3[:, h, :], sbank(i)[:, 0:384], 0.125, tbl("amask", 384), ALU.mult, ALU.add, p)
                side_free[i] = s_t
                if h == 5:
                    yield
            a = dv.op(lambda e: e.tensor_reduce(m2[:, 0, :], s3[:, :, 0:128], AX.X, ALU.max), s_t)
            a = dv.op(lambda e: e.tensor_reduce(m2[:, 1, :], s3[:, :, 128:384], AX.X, ALU.max), s_t)
            sk = row("sinks", l).unsqueeze(1).to_broadcast([128, 2, 12])
            a = tt(m2, m2, sk, ALU.max, a)
            e0 = tt(es, sk, m2, ALU.subtract, a)
            a = ts(nm, m2, -1.0, None, ALU.mult, None, a)
            ek = act(es, es, ACT.Exp, e0, scale=1.0, bias=0.0)
            for h in range(12):
                for b_, (c0, c1) in enumerate(((0, 128), (128, 384))):
                    e1 = act(p3[:, h, c0:c1], s3[:, h, c0:c1], ACT.Exp, a, bias=sm[:, 56 + 12 * b_ + h:57 + 12 * b_ + h],
                             scale=1.0, accum_out=sm[:, 80 + 12 * b_ + h:81 + 12 * b_ + h])
            a = tt(den, den, es, ALU.add, e1, ek)
            a = dv.op(lambda e: e.reciprocal(den, den), a)
            tt(p3[:, :, 0:128], p3[:, :, 0:128], den[:, 0, :].unsqueeze(2).to_broadcast([128, 12, 128]), ALU.mult, a)
            a = tt(p3[:, :, 128:384], p3[:, :, 128:384], den[:, 1, :].unsqueeze(2).to_broadcast([128, 12, 256]),
                   ALU.mult)
            yield
            for n in range(9):
                i, fr = side()
                for j in range(4):
                    u = 4 * n + j
                    p = tp(sbank(i)[:, 128 * j:128 * j + 128], AP_[:, 128 * u:128 * u + 128], a, fr, inc=(j == 3))
                if n % 2:
                    w = act(AS[:, 512 * n:512 * n + 512], sbank(i), ACT.Copy, p)
                else:
                    w = dv.op(lambda e, i=i, n=n: e.tensor_copy(AS[:, 512 * n:512 * n + 512], sbank(i)), p)
                side_free[i] = w
                if n % 2:
                    wa = w
                else:
                    wd = w
                if n == 4:
                    yield
            yield
            av = AV.rearrange("p (t d) -> p t d", t=2)
            for n in range(3):
                i, fr = side()
                for j in range(2):
                    for q in range(2):
                        h = 4 * n + 2 * j + q
                        b0 = 64 * q
                        kv = h // 3
                        o = sbank(i)[b0:b0 + 64, 256 * j:256 * j + 256]
                        vs = slice(64 * kv, 64 * kv + 64)
                        mm(o[:, 0:128], av[:, 0, vs], s3[:, h, 0:128], wa, wd, v_t, fr, start=(j == 0))
                        mm(o[:, 128:256], av[:, 0, vs], s3[:, h, 128:256], start=False, stop=False)
                        p = mm(o[:, 128:256], av[:, 1, vs], s3[:, h, 256:384], start=False,
                               inc=(j == 1 and q == 1))
                ya = Y[:, 2 * n:2 * n + 2, :].rearrange("p i c -> p (i c)")
                a_done[0] = tt(ya, ya, sbank(i), ALU.mult, p, za_tok[0])
                side_free[i] = a_done[0]

        rope_tok = [None]

        NBX = 8192
        sq_scr = sc(22024, 512)
        raw_pad = None
        for g in range(4):
            s_tok = sumsq(g, xt, sq_scr)
        h_all = norm_to_h("norm_w", 0, s_tok, sc(0, 4096), None)
        rope_tok[0] = rope_tables()
        raw_zero = None
        y_read = [None]
        HB = sc(19680, 1144).rearrange("p (m c) -> p m c", m=4)
        prev_x_free = h_all

        def block1(l, start_free):
            c_free[0] = start_free
            z0 = dv.op(lambda e: e.memset(RAW[:, :, 0:3], 0.0), start_free)
            wo = AT["c_conv_w"] + 72 * l
            silus = []

            def conv(i0, n, bank_ap, p):
                e_ = act(RAW[:, i0:i0 + n, 3:259], bank_ap, ACT.Copy, p, start_free)
                return e_

            def conv_taps(i0, n, e_):
                lt = [e_] * n
                for k in range(4):
                    for m in range(n):
                        wk = TB[:, wo + 18 * k + i0 + m:wo + 18 * k + i0 + m + 1]
                        if k == 0:
                            lt[m] = ts(CT[:, i0 + m, :], RAW[:, i0 + m, 0:256], wk, None, ALU.mult, None, e_, z0)
                        else:
                            lt[m] = stt(CT[:, i0 + m, :], RAW[:, i0 + m, k:k + 256], wk, CT[:, i0 + m, :],
                                        ALU.mult, ALU.add, lt[m])
                return act(CT[:, i0:i0 + n, :], CT[:, i0:i0 + n, :], ACT.Silu, lt[-1])

            pend = None
            for i in range(5):
                g = proj(512) if i < 4 else proj(256, mode="cm+")
                es = [conv(4 * i + 2 * b, 2, g.bank[b].rearrange("p (a c) -> p a c", a=2), g.tok)
                      for b in range(2 if i < 4 else 1)]
                if i == 4:
                    src = g.bank[1][:, 0:32].rearrange("p (t c) -> p t c", t=2)
                    q1 = dv.op(lambda e: e.tensor_copy(gs[:, 120:132].rearrange("p (h t) -> p h t", h=6),
                                                       src[:, :, 0:6].rearrange("p t h -> p h t")), g.tok, start_free)
                    q2 = dv.op(lambda e: e.tensor_copy(gs[:, 132:144].rearrange("p (h t) -> p h t", h=6),
                                                       src[:, :, 6:12].rearrange("p t h -> p h t")), g.tok)
                    g.free_with([es[-1], q2])
                    ba = [q1, q2]
                else:
                    g.free_with(es[-1])
                si = conv_taps(4 * i, 4 if i < 4 else 2, es[-1])
            dn = delta_net(l, si, ba, None)
            sides.append(dn)
            zt = []
            for n, t0 in ((4, 10), (2, 14)):
                g = proj(128 * n)
                for b in range(n // 2):
                    zc_tok[0] = act(Y[:, t0 + 2 * b:t0 + 2 * b + 2, :], g.bank[b].rearrange("p (a c) -> p a c", a=2),
                                    ACT.Silu, g.tok, y_read[0])
                g.free_with(zc_tok[0])
            hz = dv.op(lambda e: e.memset(HB[:, :, 0:30], 0.0), start_free)
            g1 = proj(512)
            for b in range(2):
                ea = act(HB[:, 2 * b:2 * b + 2, 30:286], g1.bank[b].rearrange("p (a c) -> p a c", a=2), ACT.Copy,
                         g1.tok, start_free)
            g1.free_with(ea)
            g2 = proj(512)
            for b in range(2):
                et = act(Y[:, 6 + 2 * b:8 + 2 * b, :], g2.bank[b].rearrange("p (a c) -> p a c", a=2), ACT.Tanh, g2.tok,
                         y_read[0], scale=0.5, bias=0.0)
            g2.free_with(et)
            yb = Y[:, 6:10, :]
            a = ts(yb, yb, 0.5, 0.5, ALU.mult, ALU.add, et)
            hb_t = tt(HB[:, :, 30:286], HB[:, :, 30:286], yb, ALU.mult, a, ea)
            g3 = proj(512)
            for b in range(2):
                zb_tok[0] = act(yb[:, 2 * b:2 * b + 2, :], g3.bank[b].rearrange("p (a c) -> p a c", a=2), ACT.Silu,
                                g3.tok, hb_t)
            g3.free_with(zb_tok[0])
            finish(dn)
            cf = conformer(l, HB, sc(17408, 1024), sc(18432, 1024), [hb_t, hz, c_done[0]])
            sides.append(cf)
            qv = QK.rearrange("p (t c) -> p t c", t=2)
            for i in range(2):
                g = proj(512, mode="tm")
                for t in range(2):
                    q_t = act(qv[:, t, 512 * i:512 * i + 512], g.bank[t], ACT.Copy, g.tok, c_done[0])
                g.free_with(q_t)
            g = proj(256, mode="tm")
            for t in range(2):
                v_t = act(AV[:, 256 * t:256 * t + 256], g.bank[t][:, 0:256], ACT.Copy, g.tok, c_done[0])
            g.free_with(v_t)
            at = attention(l, [q_t, c_done[0]], v_t)
            finish(cf)
            sides.append(at)
            acc = sc(17408, 1024).rearrange("p (m c) -> p m c", m=4)
            g = Group(lambda kt: acc[:, kt, :], lambda kt: b_ready[0], 512, "cm", 4).all()
            for m in range(4):
                b_t = stt(Y[:, 6 + m, :], g.bank[m // 2][:, 256 * (m % 2):256 * (m % 2) + 256],
                          tb("b_pw_b", 4 * l + m), Y[:, 6 + m, :], ALU.add, ALU.mult, g.tok, zb_tok[0])
            g.free_with(b_t)
            for n, t0 in ((4, 0), (2, 4)):
                g = proj(128 * n)
                for b in range(n // 2):
                    za_tok[0] = act(Y[:, t0 + 2 * b:t0 + 2 * b + 2, :], g.bank[b].rearrange("p (a c) -> p a c", a=2),
                                    ACT.Silu, g.tok, y_read[0])
                g.free_with(za_tok[0])
            h_read[0] = g.tok
            ytok = lambda kt: a_done[0] if kt < 6 else (b_t if kt < 10 else c_done[0])
            mk = lambda: Group(lambda kt: Y[:, kt, :], ytok, 512, "tm", 16)
            ga, gb = mk(), mk()
            for gg_, n in ((ga, 3), (gb, 3)):
                for _ in range(n):
                    gg_.feed()
            finish(at)
            for gg_ in (ga, gb):
                gg_.all()
            outs = [ga, gb]

            def add_x(i, g):
                for t in range(2):
                    v = X[:, t, 512 * i:512 * i + 512]
                    x_tok[i] = tt(v, v, g.bank[t], ALU.add, g.tok)
                g.free_with(x_tok[i])
                return sumsq(i, x_tok[i], sq_scr)

            add_x(0, ga)
            add_x(1, gb)
            add_x(2, mk().all())
            g = mk().all()
            y_read[0] = g.tok
            return add_x(3, g)

        s_tok = block1(0, h_all)
        free = norm_to_h("norm_w", 1, s_tok, sc(0, 4096), a_done[0])
        s_tok = block1(1, free)
        free = norm_to_h("g_pre_2", 0, s_tok, sc(0, 4096), a_done[0])

        YS = sc(0, 4096).rearrange("p (i c) -> p i c", i=16)

        def ytile(i, n=1):
            if n == 1:
                return Y[:, i, :] if i < 16 else YS[:, i - 16, :]
            return Y[:, i:i + n, :] if i < 16 else YS[:, i - 16:i - 16 + n, :]

        PO = 4096

        def pool_layer(free):
            U = sc(PO, 8 * 272).rearrange("p (i c) -> p i c", i=8)
            A = sc(PO + 2176, 2176).rearrange("p (i c) -> p i c", i=8)
            B = sc(PO + 4352, 2176).rearrange("p (i c) -> p i c", i=8)
            D = [sc(PO + 6528 + 2048 * k, 2048).rearrange("p (i c) -> p i c", i=8) for k in range(2)]
            for b in (U, A, B):
                z_ = dv.op(lambda e, b=b: e.memset(b[:, :, 0:16], 0.0), free)
            u_free, d_free = [z_], [None, None]
            d_tok = {}

            def load_u(g):
                for i in range(2):
                    q = proj(512)
                    for b in range(2):
                        t = act(U[:, 4 * i + 2 * b:4 * i + 2 * b + 2, 16:272],
                                q.bank[b].rearrange("p (a c) -> p a c", a=2), ACT.Copy, q.tok, u_free[0], free)
                    q.free_with(t)
                d = D[g % 2]
                src, k = U, 1
                tok = t
                for s in range(g + 1):
                    dst = (A, B)[s % 2]
                    tok = tt(dst[:, :, 16:272], src[:, :, 16:272], src[:, :, 16 - k:272 - k], ALU.add, tok, z_)
                    src, k = dst, 2 * k
                tok = tt(d, src[:, :, 16:272], tbl(f"cnt{g}", 256).unsqueeze(1).to_broadcast([128, 8, 256]),
                         ALU.mult, tok, d_free[g % 2], free)
                tok = tt(d, d, U[:, :, 16:272], ALU.subtract, tok)
                u_free[0] = tok
                d_tok[g] = tok

            def load_z(g):
                for i in range(2):
                    q = proj(512)
                    for b in range(2):
                        t0 = 8 * g + 4 * i + 2 * b
                        t = act(ytile(t0, 2), q.bank[b].rearrange("p (a c) -> p a c", a=2), ACT.Silu, q.tok,
                                y_read[0], free)
                    q.free_with(t)
                for j in range(8):
                    t = ts(ytile(8 * g + j), ytile(8 * g + j), tb("pool_scale_2", 8 * g + j), None, ALU.mult, None, t)
                return t

            def mix(g, zt):
                d = D[g % 2]
                for i in range(2):
                    q = Group(lambda kt: d[:, kt, :], lambda kt: d_tok[g], 512, "cm", 8).all()
                    for j in range(4):
                        n = 8 * g + 4 * i + j
                        t = stt(ytile(n), q.bank[j // 2][:, 256 * (j % 2):256 * (j % 2) + 256], tb("pool_b_2", n),
                                ytile(n), ALU.add, ALU.mult, q.tok, zt)
                    q.free_with(t)
                d_free[g % 2] = q.tok
                return t

            load_u(0)
            for g in range(4):
                zt = load_z(g)
                if g < 3:
                    load_u(g + 1)
                yt = mix(g, zt)
            return yt

        def lru_layer(free):
            o = PO
            RAWL = sc(o, 4 * 2 * 259).rearrange("p (i c) -> p i c", i=8)
            UC = sc(o + 2072, 2048)
            R, IG, TA = sc(o + 4120, 2048), sc(o + 6168, 2048), sc(o + 8216, 2048)
            ucv = UC.rearrange("p (i c) -> p i c", i=8)
            c8 = SM[:, 640:672]
            ng = SM[:, 672:704]
            a = ts(ng, TB[:, AT["lru_L_2"]:AT["lru_L_2"] + 32], -1.0, None, ALU.mult, None, free)
            a = softplus(c8, ng, SM[:, 704:800], 32, a)
            c8_t = ts(c8, c8, -8.0, None, ALU.mult, None, a)
            z_ = dv.op(lambda e: e.memset(RAWL[:, :, 0:3], 0.0), free)
            uc_free, r_free = [z_], [free]
            wo = AT["conv_w_2"]
            for g in range(4):
                for i in range(2):
                    q = proj(512)
                    for b in range(2):
                        t = act(RAWL[:, 4 * i + 2 * b:4 * i + 2 * b + 2, 3:259],
                                q.bank[b].rearrange("p (a c) -> p a c", a=2), ACT.Copy, q.tok, uc_free[0], z_, free)
                    q.free_with(t)
                    lt = [t] * 4
                    for k in range(4):
                        for m in range(4):
                            j = 4 * i + m
                            n = 8 * g + j
                            wk = TB[:, wo + 32 * k + n:wo + 32 * k + n + 1]
                            if k == 0:
                                lt[m] = ts(ucv[:, j, :], RAWL[:, j, 0:256], wk, tb("conv_b_2", n), ALU.mult, ALU.add,
                                           lt[m], uc_free[0])
                            else:
                                lt[m] = stt(ucv[:, j, :], RAWL[:, j, k:k + 256], wk, ucv[:, j, :], ALU.mult, ALU.add,
                                            lt[m])
                uc_t = lt[-1]
                raw_t = lt[-1]
                for i in range(2):
                    q = proj(512)
                    for b in range(2):
                        t0 = 8 * g + 4 * i + 2 * b
                        zt = act(ytile(t0, 2), q.bank[b].rearrange("p (a c) -> p a c", a=2), ACT.Silu, q.tok,
                                 y_read[0], free)
                    q.free_with(zt)
                for w_, dst, bias in ((0, R, "lru_ba_2"), (1, IG, "lru_bx_2")):
                    c = used[0]
                    slot = c % NSLOT
                    w = W[:, slot, :].rearrange("p (k n) -> p k n", k=8)
                    for hp in range(2):
                        q = Group(None, None, 512, "cm", 2)
                        for kl in range(2):
                            for h in range(2):
                                hd = 2 * hp + h
                                for j in range(2):
                                    last = kl == 1 and h == 1 and j == 1
                                    t = mm(q.bank[h][:, 256 * j:256 * j + 256],
                                           w[:, 2 * hd + kl, 128 * j:128 * j + 128], ucv[:, 2 * hd + kl, :],
                                           (s_slot[slot], 16 * (c // NSLOT + 1)), q.free, uc_t,
                                           start=(kl == 0 and j == 0), stop=(kl == 1), inc=last)
                        for j in range(4):
                            jj = 4 * hp + j
                            e_ = act(dst[:, 256 * jj:256 * jj + 256], q.bank[j // 2][:, 256 * (j % 2):256 * (j % 2) + 256],
                                     ACT.Sigmoid, t, r_free[0], bias=tb(bias, 8 * g + jj), scale=1.0)
                        q.free_with(e_)
                    used[0] += 1
                    released.append(t)
                r3 = R.rearrange("p (i c) -> p i c", i=8)
                cb = c8[:, 8 * g:8 * g + 8].unsqueeze(2).to_broadcast([128, 8, 256])
                la = tt(r3, r3, cb, ALU.mult, e_, c8_t)
                th = act(TA, R, ACT.Tanh, la, r_free[0], scale=-1.0, bias=0.0)
                ex = act(R, R, ACT.Exp, th, scale=1.0, bias=0.0)
                sq = sc(o + 10264, 2048)
                a = act(sq, R, ACT.Square, ex, r_free[0])
                a = stt(TA, sq, 1.0, TA, ALU.add, ALU.mult, a)
                a = ts(TA, TA, 0.0, None, ALU.max, None, a)
                a = act(TA, TA, ACT.Sqrt, a)
                b_ = tt(IG, IG, UC, ALU.mult, e_, uc_t)
                uc_free[0] = [b_, raw_t, t]
                a = tt(IG, IG, TA, ALU.mult, a, b_)
                for j in range(8):
                    js = slice(256 * j, 256 * j + 256)
                    s_ = dv.op(lambda e, js=js: e.tensor_tensor_scan(TA[:, js], R[:, js], IG[:, js], 0.0, ALU.mult,
                                                                     ALU.add), a)
                yv = ytile(8 * g, 8)
                yt = tt(yv, yv, TA.rearrange("p (i c) -> p i c", i=8), ALU.mult, s_, zt)
                r_free[0] = yt
            return yt

        g_uses = [0]

        def post(l, yt):
            h_read[0] = released[-1]
            O = sc(PO, 4096).rearrange("p (t c) -> p t c", t=2)
            GP = sc(PO + 4096, 2048)
            GL = sc(PO + 6144, 2048)
            E = sc(PO + 8192, 4096).rearrange("p (t c) -> p t c", t=2)
            junk = sc(PO + 12288, 512)
            sync_late.append((len(released), yt, [(GP, gpost_d[l:l + 1, :]), (GL, gplo_d[l:l + 1, :])]))
            g_uses[0] += 1
            gt = (s_g, 32 * g_uses[0])
            for i in range(4):
                q = Group(lambda kt: ytile(kt), lambda kt: yt, 512, "tm", 32).all()
                cs = slice(512 * i, 512 * i + 512)
                for t in range(2):
                    s1 = act(junk, q.bank[t], ACT.Square, q.tok, yt, accum_out=SM[:, 4 * t + i:4 * t + i + 1])
                    o_t = tt(O[:, t, cs], q.bank[t], GP[:, cs], ALU.mult, s1, gt, yt)
                q.free_with([s1, o_t])
            y_read[0] = q.tok
            a = dv.op(lambda e: e.tensor_reduce(SM[:, 8:10], SM[:, 0:8].rearrange("p (t g) -> p t g", t=2), AX.X,
                                                ALU.add), s1)
            r = rstd_of(SM[:, 8:10], 2048, SM[:, 12:14], a)
            for i in range(4):
                cs = slice(512 * i, 512 * i + 512)
                for t in range(2):
                    x_tok[i] = stt(X[:, t, cs], O[:, t, cs], SM[:, 12 + t:13 + t], X[:, t, cs], ALU.mult, ALU.add,
                                   r, o_t)
                s_tok = sumsq(i, x_tok[i], sq_scr)
            for i in range(4):
                q = Group(lambda kt: PTS[:, 2 * l + kt, :], lambda kt: pt_tok, 512, "tm", 2)
                q.feed(kts=range(2), col=512 * (i % 2), last_use=(i % 2 == 1))
                for t in range(2):
                    e_t = act(E[:, t, 512 * i:512 * i + 512], q.bank[t], ACT.Copy, q.tok, yt)
                q.free_with(e_t)
            ff = norm_to_h("g_ple_in_2", l, s_tok, sc(PO, 4096), [x_tok[3]])
            for i in range(4):
                q = proj(512, mode="tm")
                cs = slice(512 * i, 512 * i + 512)
                for t in range(2):
                    g_ = act(O[:, t, cs], q.bank[t], ACT.Sigmoid, q.tok, ff)
                    m_ = tt(E[:, t, cs], E[:, t, cs], O[:, t, cs], ALU.mult, g_, e_t)
                    s1 = act(junk, E[:, t, cs], ACT.Square, m_, accum_out=SM[:, 4 * t + i:4 * t + i + 1])
                    n_ = tt(E[:, t, cs], E[:, t, cs], GL[:, cs], ALU.mult, s1, gt)
                q.free_with(g_)
            h_read[0] = q.tok
            a = dv.op(lambda e: e.tensor_reduce(SM[:, 8:10], SM[:, 0:8].rearrange("p (t g) -> p t g", t=2), AX.X,
                                                ALU.add), s1)
            r = rstd_of(SM[:, 8:10], 2048, SM[:, 12:14], a)
            for i in range(4):
                cs = slice(512 * i, 512 * i + 512)
                for t in range(2):
                    x_tok[i] = stt(X[:, t, cs], E[:, t, cs], SM[:, 12 + t:13 + t], X[:, t, cs], ALU.mult, ALU.add,
                                   r, n_)
                if l == 0:
                    s_tok = sumsq(i, x_tok[i], sq_scr)
            return s_tok, x_tok[3]

        PTS = SC[:, 21000:22024].rearrange("p (k t) -> p k t", k=4)
        pt_tok = (s_tab, 48)

        yt = pool_layer(free)
        s_tok, xd = post(0, yt)
        free = norm_to_h("g_pre_2", 1, s_tok, sc(PO, 4096), [xd])
        yt = lru_layer([free, xd])
        s_tok, xd = post(1, yt)
        assert used[0] == len(chunks) == len(released)

        block = ctx.enter_context(nc.Block())

        @block.sync
        def _(e):
            e.dma_start(X[:, 0, :], xin[0:128, :]).then_inc(s_x, 16)
            e.dma_start(X[:, 1, :], xin[128:256, :]).then_inc(s_x, 16)
            e.dma_start(TB[:, :], tab).then_inc(s_tab, 16)
            e.dma_start(POSI[:, :], pos_d).then_inc(s_tab, 16)
            e.dma_start(SC[:, 21000:22024], pT_d).then_inc(s_tab, 16)
            off = 0
            late = list(sync_late)
            for c, (name, l, k0, nk, c0, n) in enumerate(chunks):
                while late and late[0][0] <= c:
                    _, tok, dmas = late.pop(0)
                    e.wait_ge(tok[0], tok[1])
                    for dst, src in dmas:
                        e.dma_start(dst, src.to_broadcast([128, 2048])).then_inc(s_g, 16)
                if c >= NSLOT:
                    e.wait_ge(released[c - NSLOT][0], released[c - NSLOT][1])
                e.dma_start(W[:, c % NSLOT, 0:nk * n], wall[off:off + 128 * nk * n].rearrange("(p f) -> p f", p=128)
                            ).then_inc(s_slot[c % NSLOT], 16)
                off += 128 * nk * n
            for t in range(2):
                e.wait_ge(x_tok[3][0], x_tok[3][1])
                e.dma_start(out[128 * t:128 * t + 128, :], X[:, t, :]).then_inc(s_out, 16)
            e.wait_ge(s_out, 32)

        @block.tensor
        def _(e):
            pe.play(e)

        @block.vector
        def _(e):
            dv.play(e)

        @block.scalar
        def _(e):
            ac.play(e)


def kernel(**inputs):
    import concourse.bacc as bacc
    from concourse.bass_utils import run_bass_kernel_spmd as run

    arr = {n: np.asarray(v) for n, v in inputs.items()}
    flat = {"lru_wa_2": arr["lru_wa_2"].reshape(1, 4096, 256), "lru_wx_2": arr["lru_wx_2"].reshape(1, 4096, 256),
            "pool_w_2": arr["pool_w_2"].reshape(4, 1024, 1024)}
    ch = plan()
    total = sum(128 * nk * n for _, _, _, nk, _, n in ch)
    wall = np.empty(total, np.float32)
    off = 0
    for name, l, k0, nk, c0, n in ch:
        a = flat.get(name, arr[name])[l][128 * k0:128 * (k0 + nk), c0:c0 + n]
        wall[off:off + 128 * nk * n] = a.reshape(nk, 128, n).transpose(1, 0, 2).ravel()
        off += 128 * nk * n
    cols = list(const_columns().values())
    for name in CHAN:
        cols.append(arr[name].reshape(-1, 128).T)
    for name in ROW:
        cols.append(np.broadcast_to(arr[name].reshape(1, -1), (128, arr[name].size)))
    tab = np.ascontiguousarray(np.concatenate(cols, axis=1))
    pT = np.ascontiguousarray(arr["p_2"][:, 0].reshape(2, 256, 2, 128).transpose(3, 0, 2, 1).reshape(128, 1024))
    arrays = {
        "wall": wall, "tab": tab, "pT": pT,
        "pos": np.ascontiguousarray(arr["positions"].reshape(2, 128).T),
        "x": np.ascontiguousarray(arr["x"].reshape(256, 2048)),
        "g_post": np.ascontiguousarray(arr["g_post_2"]), "g_ple_out": np.ascontiguousarray(arr["g_ple_out_2"]),
    }
    nc = bacc.Bacc("TRN2", target_bir_lowering=False, num_devices=1)
    d = {n: nc.dram_tensor("in_" + n, a.shape, mybir.dt.from_np(a.dtype), kind="ExternalInput").ap()
         for n, a in arrays.items()}
    out = nc.dram_tensor("out_0", (256, 2048), F32, kind="ExternalOutput").ap()
    program(nc, d["wall"], d["tab"], d["pos"], d["pT"], d["x"], d["g_post"], d["g_ple_out"], out)
    r = run(nc, [{"in_" + n: a for n, a in arrays.items()}], core_ids=[0])
    return r.results[0]["out_0"].reshape(1, 256, 2048)
```

```python
import numpy as np
import concourse.bass as bass
from concourse import mybir
from contextlib import ExitStack

F32 = mybir.dt.float32
F32R = mybir.dt.float32r
I32 = mybir.dt.int32
ALU = mybir.AluOpType
ACT = mybir.ActivationFunctionType
AX = mybir.AxisListType

T = 256
NRAW = 3
NSPL = 3
SPLIT = ("w_in", "w_out", "w_in_2", "w_out_2", "w_ple_gate_2", "pool_w_2")
SLOT = 2048
LNEXP = "natural_log_exp_and_others"



def plan():
    ch = []

    def cols(name, l, c0, n, nkt=16, step=4):
        for k in range(0, nkt, step):
            ch.append((name, l, k, min(step, nkt - k), c0, n))

    for l in range(2):
        for i in range(4):
            cols("w_in", l, 3584 + 512 * i, 512)
        cols("w_in", l, 5632, 268)
        cols("w_in", l, 5900, 512)
        cols("w_in", l, 6412, 256, step=8)
        for c in (2048, 2560, 3072, 0, 512):
            cols("w_in", l, c, 512)
        cols("w_in", l, 1024, 256, step=8)
        cols("b_pw_w", l, 0, 512, nkt=4)
        cols("w_in", l, 1280, 512)
        cols("w_in", l, 1792, 256, step=8)
        late = ((6, 4), (10, 4), (14, 2))
        soon = ((0, 4), (4, 2))
        for part, gs in ((late, (0, 1)), (soon, (0, 1)), (late + soon, (2,)), (late + soon, (3,))):
            for g in gs:
                for k, n in part:
                    ch.append(("w_out", l, k, n, 512 * g, 512))
    def u(l, g, i):
        cols("w_in_2", l, 1024 * g + 512 * i, 512)

    def z(l, g, i):
        cols("w_in_2", l, 4096 + 1024 * g + 512 * i, 512)

    def o(l, g):
        for i in range(4):
            for k in (0, 4):
                ch.append(("w_out_2", l, 8 * g + k, 4, 512 * i, 512))

    def pool(g):
        for i in range(2):
            for k in (0, 4):
                ch.append(("pool_w_2", g, k, 4, 512 * i, 512))

    def gates(n):
        ch.append(("lru_wa_2", 0, 4 * n, 4, 0, 256))
        ch.append(("lru_wx_2", 0, 4 * n, 4, 0, 256))

    def post(l):
        for g in range(2):
            ch.append(("w_ple_2", l, 0, 2, 1024 * g, 1024))
        for g in range(4):
            cols("w_ple_gate_2", l, 512 * g, 512)

    u(0, 0, 0), u(0, 0, 1)
    for g in range(4):
        z(0, g, 0), z(0, g, 1)
        if g > 0:
            o(0, g - 1)
        pool(g)
        if g < 3:
            u(0, g + 1, 0), u(0, g + 1, 1)
    o(0, 3)
    post(0)
    u(1, 0, 0)
    for n in range(8):
        z(1, n // 2, n % 2)
        if n < 7:
            u(1, (n + 1) // 2, (n + 1) % 2)
        if n % 2 == 0 and n > 0:
            o(1, n // 2 - 1)
        gates(n)
    o(1, 3)
    post(1)
    return ch



def const_columns():
    i = np.arange(128)
    c = {}
    c["ident"] = np.eye(128)
    same = (i[:, None] // 64) == (i[None, :] // 64)
    c["cum"] = same & (i[:, None] <= i[None, :])
    c["last"] = same
    c["incl"] = same & (i[:, None] <= i[None, :])
    c["strict"] = -1.0 * (same & (i[:, None] < i[None, :]))
    up = lambda m: ((i[:, None] // m) == (i[None, :] // m)) & ((i[:, None] % m) < m // 2) & ((i[None, :] % m) >= m // 2)
    c["lv2"] = up(2)
    for m in (4, 8, 16, 32, 64):
        c[f"lv{m}"] = up(m).T
    q = i[:, None]
    k = i[None, :]
    neg = np.float32(-1e30)
    c["amask"] = np.concatenate([np.where(k <= q, 0, neg), np.where(k > q, 0, neg), np.where(k <= q, 0, neg)], axis=1)
    c["ones"] = np.ones((128, 128))
    c["eps"] = np.full((128, 1), 1e-6)
    c["zero"] = np.zeros((128, 1))
    inv = np.float32(500000.0) ** (-np.arange(0, 16, 2, dtype=np.float32) / np.float32(16))
    c["invf"] = np.broadcast_to(inv, (128, 8))
    for g, w in enumerate((2, 4, 8, 16)):
        cnt = np.minimum(np.arange(1, 17), w)
        c[f"cnt{g}"] = np.broadcast_to(1.0 / cnt.astype(np.float32), (128, 16))
    return {n: np.ascontiguousarray(v, dtype=np.float32) for n, v in c.items()}


CHAN = ["norm_w", "b_conv_w", "b_conv_b", "b_ln_w", "b_ln_b", "b_pw_b", "c_conv_w", "c_onorm_w", "g_pre_2",
        "pool_b_2", "pool_scale_2", "conv_w_2", "conv_b_2", "lru_ba_2", "lru_bx_2", "lru_L_2", "g_ple_in_2"]
ROW = ["q_norm_w", "k_norm_w", "sinks", "c_a_log", "c_dt_bias"]
SHAPE = {"norm_w": (2, 2048), "b_conv_w": (2, 31, 512), "b_conv_b": (2, 512), "b_ln_w": (2, 512), "b_ln_b": (2, 512),
         "b_pw_b": (2, 512), "c_conv_w": (2, 4, 2304), "c_onorm_w": (2, 128), "g_pre_2": (2, 2048),
         "pool_b_2": (1, 4096), "pool_scale_2": (1, 4096), "conv_w_2": (1, 4, 4096), "conv_b_2": (1, 4096),
         "lru_ba_2": (1, 4096), "lru_bx_2": (1, 4096), "lru_L_2": (1, 4096), "g_ple_in_2": (2, 2048),
         "q_norm_w": (2, 64), "k_norm_w": (2, 64), "sinks": (2, 12), "c_a_log": (2, 6), "c_dt_bias": (2, 6)}


def column_table():
    at, n = {}, 0
    for name, v in const_columns().items():
        at[name] = n
        n += v.shape[1]
    for name in CHAN:
        at[name] = n
        n += int(np.prod(SHAPE[name])) // 128
    for name in ROW:
        at[name] = n
        n += int(np.prod(SHAPE[name]))
    return at, n


def NQ_BASE(nc, n):
    return nc.sbuf_base - 4 * n


PE_STREAMS = ("main",)
DV_STREAMS = ("prep", "main")
AC_STREAMS = ("prep", "main")


class Unit:

    def __init__(self):
        self.items, self.cost, self.sem, self.value, self.done, self.dma = [], 0.0, None, None, None, False


class Eng:

    def __init__(self, sem=None, chain=False, streams=("main",)):
        self.sem, self.chain = sem, chain
        self.q = {s: [] for s in streams}
        self.open = {s: None for s in streams}
        self.tail = {s: None for s in streams}
        self.order = []

    def op(self, fn, *toks, inc=True, free=False, stream="main", cost=500.0, sem=None, value=None):
        if stream not in self.q:
            stream = "main"
        u = self.open[stream] or Unit()
        waits = flat(toks)
        if self.chain and not free and self.tail[stream] is not None:
            waits.append(self.tail[stream])
        u.items.append((waits, fn, cost))
        if not inc:
            self.open[stream] = u
            return None
        self.open[stream] = None
        u.sem, u.value = sem or self.sem, value
        self.q[stream].append(u)
        if not free:
            self.tail[stream] = u
        return u

    def play(self, e):
        seen = {}
        for u in self.order:
            for k, (waits, fn, _) in enumerate(u.items):
                for w in waits:
                    if seen.get(id(w.sem), 0) < w.value:
                        seen[id(w.sem)] = w.value
                        e.wait_ge(w.sem, w.value)
                r = fn(e)
                if k == len(u.items) - 1:
                    r.then_inc(u.sem, 16 if u.dma else 1)


def flat(toks):
    out = []
    for t in toks:
        if isinstance(t, (list, tuple)):
            out += flat(t)
        elif t is not None:
            out.append(t)
    return out


def arrange(engines):
    free = [0.0] * len(engines)
    while True:
        best = None
        for n, (en, _) in enumerate(engines):
            cand = None
            for pr, (s, q) in enumerate(en.q.items()):
                if not q:
                    continue
                u, t, ok = q[0], free[n], True
                for waits, _, cost in u.items:
                    for w in waits:
                        if w.done is None:
                            ok = False
                            break
                        t = max(t, w.done)
                    if not ok:
                        break
                if not ok:
                    continue
                key = (max(t - free[n] - 50.0, 0.0), pr)
                if cand is None or key < cand[0]:
                    cand = (key, t, s)
            if cand is not None and (best is None or cand[1] < best[0]):
                best = (cand[1], n, cand[2])
        if best is None:
            break
        _, n, s = best
        en, stall = engines[n]
        u = en.q[s].pop(0)
        t = free[n]
        for waits, _, cost in u.items:
            for w in waits:
                t = max(t, w.done)
            t += cost
        free[n] = t
        u.done = t + stall
        en.order.append(u)
        if u.value is None:
            u.value = len(en.order)
    for en, _ in engines:
        assert not any(en.q.values())


def size(ap):
    n = 1
    for k in ap.shape[1:]:
        n *= int(k)
    return n


def program(nc, wall, tab, pos_d, pT_d, xin, gpost_d, gplo_d, xsave, out):
    chunks = plan()
    AT, NT = column_table()
    ctx = ExitStack()
    with ctx:
        TB = ctx.enter_context(nc.sbuf_tensor("TB", [128, NT], F32))
        SM = ctx.enter_context(nc.sbuf_tensor("SM", [128, 800], F32))
        POSI = ctx.enter_context(nc.sbuf_tensor("POSI", [128, 8], I32))
        W = ctx.enter_context(nc.sbuf_tensor("W", [128, NRAW, SLOT], F32))
        WH = ctx.enter_context(nc.sbuf_tensor("WH", [128, NSPL, SLOT], F32R))
        WL = ctx.enter_context(nc.sbuf_tensor("WL", [128, NSPL, SLOT], F32R))
        HH = ctx.enter_context(nc.sbuf_tensor("HH", [128, 16, 256], F32R))
        HL = ctx.enter_context(nc.sbuf_tensor("HL", [128, 16, 256], F32R))
        NQ = 22320
        Q = ctx.enter_context(nc.sbuf_tensor("Q", [128, NQ], F32))
        q_at = NQ_BASE(nc, NQ)

        def over(name, off, shape, dt=F32):
            return nc.alloc_sbuf_tensor_at(name, shape, dt, offset=q_at + 4 * off)

        X = over("X", 10240, [128, 2, 2048])
        Y = over("Y", 0, [128, 16, 256])
        O = over("O", 0, [128, 2, 2048])
        YH = over("YH", 4096, [128, 8, 256], F32R)
        YL = over("YL", 6144, [128, 8, 256], F32R)
        DH = over("DH", 14336, [128, 8, 256], F32R)
        DL = over("DL", 16384, [128, 8, 256], F32R)
        E = over("E", 14336, [128, 2, 2048])
        PS = ctx.enter_context(nc.psum_tensor("PS", [128, 4096], F32))

        def sem(n):
            return ctx.enter_context(nc.semaphore(n))

        pe = Eng(sem("s_pe"), streams=PE_STREAMS)
        dv = Eng(sem("s_dv"), chain=True, streams=DV_STREAMS)
        ac = Eng(sem("s_ac"), chain=True, streams=AC_STREAMS)
        sy, po = Eng(), Eng()
        at = ["main"]

        def dma(q, dst, src, s, value, *toks):
            u = q.op(lambda e: e.dma_start(dst, src), *toks, sem=s, value=value, cost=size(dst) * 512 / 360.0)
            u.dma = True
            return u

        s_slot = [sem(f"s_w{i}") for i in range(NRAW)]
        s_tab, s_x, s_xr, s_g, s_out, s_sp = sem("s_tab"), sem("s_x"), sem("s_xr"), sem("s_g"), sem("s_out"), sem("s_sp")

        def pool_dma(dst, src, s, count, *toks):
            count[0] += 16
            return dma(po, dst, src, s, count[0], *toks)

        def tb(name, off=0, n=1):
            return TB[:, AT[name] + off:AT[name] + off + n]

        def tbl(name, n=128):
            return TB[:, AT[name]:AT[name] + n]

        def row(name, l):
            w = SHAPE[name][1]
            return TB[:, AT[name] + l * w:AT[name] + (l + 1) * w]

        ident, ones = tbl("ident"), tbl("ones")
        dma(sy, X[:, 0, :], xin[0:128, :], s_x, 16)
        xt = dma(sy, X[:, 1, :], xin[128:256, :], s_x, 32)
        dma(sy, TB[:, :], tab, s_tab, 16)
        tabt = dma(sy, POSI[:, 0:2], pos_d, s_tab, 32)
        n_xr, n_sp, n_g = [0], [0], [0]

        def sc(off, n):
            assert off + n <= NQ - 4096, (off, n)
            return Q[:, 4096 + off:4096 + off + n]

        def dop(o, fn, *w, **k):
            return dv.op(fn, *w, stream=at[0], cost=60 + size(o) / 0.96, **k)

        def dop0(fn, *w, **k):
            return dv.op(fn, *w, stream=at[0], **k)

        def tt(o, a, b, op, *w):
            return dop(o, lambda e: e.tensor_tensor(o, a, b, op), *w)

        def stt(o, a, s, b, op0, op1, *w):
            return dop(o, lambda e: e.scalar_tensor_tensor(out=o, in0=a, scalar=s, in1=b, op0=op0, op1=op1), *w)

        def ts(o, a, s1, s2, op0, op1, *w):
            if s2 is None:
                return dop(o, lambda e: e.tensor_scalar(o, a, s1, None, op0), *w)
            return dop(o, lambda e: e.tensor_scalar(o, a, s1, s2, op0, op1), *w)

        def act(o, a, f, *w, **k):
            return ac.op(lambda e: e.activation(o, a, f, **k), *w, stream=at[0], cost=190 + size(o) / 1.2)

        def lnexp():
            ac.op(lambda e: e.preload_act_table_set(LNEXP), inc=False, stream=at[0], cost=1300)

        def mm(o, l, r, *w, start=True, stop=True, inc=False):
            return pe.op(lambda e: e.matmul(o, l, r, start=start, stop=stop, skip_group_check=True), *w, inc=inc,
                         stream=at[0], cost=size(r) * (1 if r.dtype == F32R else 4) / 2.4)

        def tp(o, a, *w, inc=False):
            return pe.op(lambda e: e.transpose(o, a, ident), *w, inc=inc, stream=at[0], cost=size(o) * 4 / 2.4)

        side_free = [None] * 4
        side_at = [0]

        def side():
            i = side_at[0] % 4
            side_at[0] += 1
            return i, side_free[i]

        def sbank(i):
            return PS[:, 2048 + 512 * i:2560 + 512 * i]

        main_free = [None, None]
        main_at = [0]
        sides = []

        def pump():
            at[0] = "side"
            for g in list(sides):
                try:
                    next(g)
                except StopIteration:
                    sides.remove(g)
            at[0] = "main"

        def finish(g):
            while g in sides:
                pump()

        used = [0]
        released = []
        raw_free = []
        part_tok = []

        arrived = []
        wall_at = [0]

        def fetch():
            while len(arrived) < len(chunks):
                c = len(arrived)
                before = None
                if c >= NRAW:
                    if len(raw_free) <= c - NRAW or raw_free[c - NRAW] is None:
                        return
                    before = raw_free[c - NRAW]
                m, off = chunks[c][3] * chunks[c][5], wall_at[0]
                arrived.append(dma(sy, W[:, c % NRAW, 0:m], wall[off:off + 128 * m].rearrange("(p f) -> p f", p=128),
                                   s_slot[c % NRAW], 16 * (c // NRAW + 1), before))
                wall_at[0] += 128 * m

        def prep():
            c = len(part_tok)
            if c >= len(chunks):
                return
            name, l, k0, nk, c0, n = chunks[c]
            if name not in SPLIT:
                part_tok.append([arrived[c]])
                raw_free.append(None)
                return
            sl, m = c % NSPL, nk * n
            before = released[c - NSPL] if c >= NSPL else None
            raw, wh, wl = W[:, c % NRAW, 0:m], WH[:, sl, 0:m], WL[:, sl, 0:m]
            a = ac.op(lambda e: e.activation(wh, raw, ACT.Copy), arrived[c], before, free=True, stream="prep",
                      cost=190 + m / 1.2)
            b = dv.op(lambda e: e.tensor_tensor(wl, raw, wh.bitcast(F32), ALU.subtract), a, free=True, stream="prep",
                      cost=60 + m / 0.96)
            part_tok.append([a, b])
            raw_free.append(b)
            fetch()

        def split(hi, lo, src, *toks):
            a = act(hi, src, ACT.Copy, *toks)
            b = tt(lo, src, hi.bitcast(F32), ALU.subtract, a)
            return [a, b]

        def use(c, t):
            used[0] += 1
            released.append(t)
            if raw_free[c] is None:
                raw_free[c] = t
                fetch()
            prep()

        class Group:

            def __init__(self, src, src_toks, ncols, mode, nk):
                self.i = main_at[0] % 2
                main_at[0] += 1
                self.bank = [PS[:, 1024 * self.i + 512 * b:1024 * self.i + 512 * b + 512] for b in range(2)]
                self.free = main_free[self.i]
                self.src, self.src_toks, self.ncols, self.mode, self.nk, self.done = src, src_toks, ncols, mode, nk, 0

            def feed(self, kts=None, col=0, last_use=True, stride=None):
                c = used[0]
                name, l, k0, nk, c0, n = chunks[c]
                shape = lambda v: v.rearrange("p (k n) -> p k n", k=nk)
                if name in SPLIT:
                    hi, lo = shape(WH[:, c % NSPL, 0:nk * n]), shape(WL[:, c % NSPL, 0:nk * n])
                else:
                    raw = shape(W[:, c % NRAW, 0:nk * n])
                lead = [part_tok[c], self.free]
                kts = range(k0, k0 + nk) if kts is None else kts
                for kl, kt in enumerate(kts):
                    tok = self.src_toks(kt)
                    x = self.src(kt)
                    passes = ((lo, x[0]), (hi, x[1]), (hi, x[0])) if name in SPLIT else ((raw, x),)
                    for n_p, (w, s) in enumerate(passes):
                        first = self.done == 0 and n_p == 0
                        last = self.done == self.nk - 1 and n_p == len(passes) - 1
                        end = kl == nk - 1 and n_p == len(passes) - 1
                        if self.mode == "cm":
                            m = self.ncols // 128
                            for j in range(m):
                                t = mm(self.bank[j // 2][:, 256 * (j % 2):256 * (j % 2) + 256],
                                       w[:, kl, col + 128 * j:col + 128 * j + 128], s, tok, lead,
                                       start=first and j % 2 == 0, stop=last, inc=end and j == m - 1)
                        elif self.mode == "cm+":
                            for j in range(2):
                                mm(self.bank[0][:, 256 * j:256 * j + 256], w[:, kl, 128 * j:128 * j + 128], s, tok, lead,
                                   start=first and j == 0, stop=last)
                            for j in range(2):
                                t = mm(self.bank[1][:, 16 * j:16 * j + 12], s[:, 128 * j:128 * j + 128],
                                       w[:, kl, 256:268], tok, lead, start=first and j == 0, stop=last, inc=end and j == 1)
                        else:
                            for j in range(2):
                                t = mm(self.bank[j][:, 0:self.ncols], s[:, 128 * j:128 * j + 128],
                                       w[:, kl, col:col + self.ncols], tok, lead, start=first, stop=last,
                                       inc=end and j == 1)
                    self.done += 1
                self.tok = t
                if last_use:
                    use(c, t)
                pump()

            def all(self):
                while self.done < self.nk:
                    self.feed()
                return self

            def free_with(self, toks):
                main_free[self.i] = toks

        def from_h(kt):
            return HH[:, kt, :], HL[:, kt, :]

        h_tok = [None] * 16

        def ht(kt):
            return h_tok[kt]

        def proj(ncols, mode="cm", nk=16):
            return Group(from_h, ht, ncols, mode, nk).all()

        x_tok = [xt] * 4
        h_read = [None]
        NXN = 0

        sq_war = [None]

        def sumsq(g, tok, scratch):
            for t in range(2):
                r = act(scratch, X[:, t, 512 * g:512 * g + 512], ACT.Square, tok, sq_war[0],
                        accum_out=SM[:, 4 * t + g:4 * t + g + 1])
            sq_war[0] = None
            return r

        def rstd_of(ssum, n, o, tok, eps="eps"):
            lnexp()
            a = act(o, ssum, ACT.Ln, tok, tabt, scale=1.0 / n, bias=tb(eps))
            return act(o, o, ACT.Exp, a, scale=-0.5, bias=0.0)

        def norm_to_h(gname, l, ss_tok, xn, xn_war):
            a = dop0(lambda e: e.tensor_reduce(SM[:, 8:10], SM[:, 0:8].rearrange("p (t g) -> p t g", t=2), AX.X,
                                                ALU.add), ss_tok)
            r = rstd_of(SM[:, 8:10], 2048, SM[:, 10:12], a)
            xv = xn.rearrange("p (t c) -> p t c", t=2)
            xtk = {}
            for g in range(4):
                for t in range(2):
                    xtk[g] = ts(xv[:, t, 512 * g:512 * g + 512], X[:, t, 512 * g:512 * g + 512], SM[:, 10 + t:11 + t],
                                None, ALU.mult, None, r, x_tok[g], xn_war)
            off = AT[gname] + 16 * l
            for k in range(0, 16, 2):
                i, fr = side()
                for j in range(2):
                    for t in range(2):
                        c = 128 * (k + j)
                        p = tp(sbank(i)[:, 256 * j + 128 * t:256 * j + 128 * t + 128], xv[:, t, c:c + 128],
                               fr, xtk[k // 4], tabt, inc=(j == 1 and t == 1))
                for j in range(2):
                    g_ap = TB[:, off + k + j:off + k + j + 1]
                    src = sbank(i)[:, 256 * j:256 * j + 256]
                    hh, hl = HH[:, k + j, :], HL[:, k + j, :]
                    t0 = act(hh, src, ACT.Copy, p, h_read[0], t1 if j else None, scale=g_ap)
                    t1 = stt(hl, src, g_ap, hh.bitcast(F32), ALU.mult, ALU.subtract, t0)
                    h_tok[k + j] = [t0, t1]
                side_free[i] = t1
            return [t0, t1]

        ROPE = SM[:, 64:64 + 32]
        sin_t = ROPE[:, 0:16].rearrange("p (t c) -> p t c", t=2)
        cos_t = ROPE[:, 16:32].rearrange("p (t c) -> p t c", t=2)

        def rope_tables():
            posf = SM[:, 12:14]
            ang = SM[:, 16:32]
            kk = SM[:, 32:48]
            a = dop0(lambda e: e.tensor_copy(posf, POSI[:, 0:2]), tabt)
            for t in range(2):
                b = ts(ang[:, 8 * t:8 * t + 8], tbl("invf", 8), posf[:, t:t + 1], None, ALU.mult, None, a)
            C1, C2 = 6.28125, float(np.float32(2 * np.pi - 6.28125))
            C3 = float(np.float32(2 * np.pi - 6.28125 - float(np.float32(2 * np.pi - 6.28125))))
            MAGIC = 12582912.0
            lim = 3.1415925
            for shift, add, dst in ((0.0, 0.0, ROPE[:, 0:16]), (0.25, float(np.float32(np.pi / 2)), ROPE[:, 16:32])):
                b = ts(kk, ang, float(1 / (2 * np.pi)), shift, ALU.mult, ALU.add, b)
                b = ts(kk, kk, MAGIC, None, ALU.add, None, b)
                b = ts(kk, kk, -MAGIC, None, ALU.add, None, b)
                b = stt(dst, kk, -C1, ang, ALU.mult, ALU.add, b)
                b = stt(dst, kk, -C2, dst, ALU.mult, ALU.add, b)
                b = stt(dst, kk, -C3, dst, ALU.mult, ALU.add, b)
                b = ts(dst, dst, add, lim, ALU.add, ALU.min, b)
                b = ts(dst, dst, -lim, None, ALU.max, None, b)
            return act(ROPE, ROPE, ACT.Sin, b)

        def softplus(o, x, s, n, tok):
            e_, z, q = s[:, 0:n], s[:, n:2 * n], s[:, 2 * n:3 * n]
            a = act(e_, x, ACT.Abs, tok)
            a = act(e_, e_, ACT.Exp, a, scale=-1.0, bias=0.0)
            a = ts(z, e_, 2.0, None, ALU.add, None, a)
            a = dop0(lambda e: e.reciprocal(z, z), a)
            a = tt(z, z, e_, ALU.mult, a)
            a = tt(q, z, z, ALU.mult, a)
            a = ts(e_, q, 1.0 / 17, None, ALU.mult, None, a)
            for k in (15, 13, 11, 9, 7, 5, 3):
                a = stt(e_, e_, 1.0 / k, q, ALU.add, ALU.mult, a)
            a = stt(e_, e_, 1.0, z, ALU.add, ALU.mult, a)
            a = ts(e_, e_, 2.0, None, ALU.mult, None, a)
            return stt(o, x, 0.0, e_, ALU.max, ALU.add, a)

        RAW = sc(0, 18 * 259).rearrange("p (i c) -> p i c", i=18)
        CT = sc(4662, 4608).rearrange("p (i c) -> p i c", i=18)
        CQ, CK, CV = sc(4662, 1536), sc(4662 + 1536, 1536), sc(4662 + 3072, 1536)
        o0 = 4662 + 4608
        KB, EG, DS, DI, KD = (sc(o0, 1536), sc(o0 + 1536, 1536), sc(o0 + 3072, 1536), sc(o0 + 4608, 1536),
                              sc(o0 + 6144, 1536))
        SS, VN = CK, KB[:, 0:768]
        UU, TT_, XX = sc(0, 1536), sc(1536, 1536), sc(3072, 1536)
        RV, RW, U2, WT, OC = KB, CV, TT_, XX, DS

        def heads(ap):
            return ap.rearrange("p (h t c) -> p h t c", h=6, t=2)

        gs = SM[:, 128:512]
        c_free = [None]

        def delta_net(l, silu_tok, ba_tok, ba_bank_free):
            bt = gs[:, 0:12].rearrange("p (h t) -> p h t", h=6)
            gg = gs[:, 12:24].rearrange("p (h t) -> p h t", h=6)
            ea = gs[:, 24:30]
            gcs, gls = gs[:, 36:48], gs[:, 48:60]
            bw, kdw = gs[:, 60:72], gs[:, 72:84]
            th = gs[:, 84:96]
            a = act(th, gs[:, 120:132], ACT.Tanh, ba_tok, scale=0.5, bias=0.0)
            b1 = ts(gs[:, 0:12], th, 0.5, 0.5, ALU.mult, ALU.add, a)
            e1 = act(ea, row("c_a_log", l), ACT.Exp, tabt, scale=1.0, bias=0.0)
            a = tt(gs[:, 132:144].rearrange("p (h t) -> p h t", h=6), gs[:, 132:144].rearrange("p (h t) -> p h t", h=6),
                   row("c_dt_bias", l).unsqueeze(2).to_broadcast([128, 6, 2]), ALU.add, ba_tok)
            a = softplus(gs[:, 12:24], gs[:, 132:144], gs[:, 144:180], 12, a)
            a = ts(gs[:, 12:24], gs[:, 12:24], -1.0, None, ALU.mult, None, a)
            g_t = tt(gg, gg, ea.unsqueeze(2).to_broadcast([128, 6, 2]), ALU.mult, a, e1)
            sq = sc(0, 3072)
            q1 = act(sq, sc(4662, 3072), ACT.Square, silu_tok)
            yield
            yield
            i, fr = side()
            b = sbank(i)
            mm(b[:, 0:12], tbl("cum"), gs[:, 12:24], g_t, fr)
            p = mm(b[:, 16:28], tbl("last"), gs[:, 12:24], start=False, inc=True)
            a = dop0(lambda e: e.tensor_copy(gs[:, 36:60].rearrange("p (a c) -> p a c", a=2),
                                              b[:, 0:32].rearrange("p (a c) -> p a c", a=2)[:, :, 0:12]), p)
            side_free[i] = a
            gc_t = a
            a1 = act(bw, gcs, ACT.Exp, a, scale=1.0, bias=0.0)
            bw_t = tt(bw, bw, gs[:, 0:12], ALU.mult, a1, b1)
            a2 = tt(kdw, gls, gcs, ALU.subtract, a)
            kd_t = act(kdw, kdw, ACT.Exp, a2, scale=1.0, bias=0.0)
            dsts = []
            for bk in range(3):
                i, fr = side()
                bnk = sbank(i)
                for j in range(4):
                    u = 4 * bk + j
                    p = mm(bnk[:, 128 * j:128 * j + 128], gs[:, 12 + u:13 + u].to_broadcast([128, 128]), tbl("cum"),
                           g_t, fr, start=(j == 0), inc=(j == 3))
                cs = slice(512 * bk, 512 * bk + 512)
                for j in range(4):
                    u = 4 * bk + j
                    d1 = ts(DI[:, 128 * u:128 * u + 128], bnk[:, 128 * j:128 * j + 128], gcs[:, u:u + 1], 0.0,
                            ALU.subtract, ALU.min, p, gc_t, c_free[0])
                e2 = act(EG[:, cs], bnk, ACT.Exp, p, d1, c_free[0], scale=1.0, bias=0.0)
                e3 = act(DI[:, cs], DI[:, cs], ACT.Exp, d1, scale=1.0, bias=0.0)
                side_free[i] = [d1, e2]
                dsts.append((e2, e3))
            eg_t, di_t = dsts[-1]
            yield
            lnexp()
            rn = sc(0, 3072)
            rt = []
            for k in range(6):
                i, fr = side()
                p = mm(sbank(i), ones, sq[:, 512 * k:512 * k + 512], q1, fr, inc=True)
                a = act(rn[:, 512 * k:512 * k + 512], sbank(i), ACT.Ln, p, scale=1.0, bias=tb("eps"))
                side_free[i] = a
                rt.append(a)
            a = act(rn, rn, ACT.Exp, a, scale=-0.5, bias=0.0)
            q_t = stt(CQ, CQ, float(128 ** -0.5), rn[:, 0:1536], ALU.mult, ALU.mult, a)
            k_t = tt(CK, CK, rn[:, 1536:3072], ALU.mult, a)
            yield
            for bk in range(3):
                i, fr = side()
                bnk = sbank(i)
                for j in range(4):
                    u = 4 * bk + j
                    p = mm(bnk[:, 128 * j:128 * j + 128], gs[:, u:u + 1].to_broadcast([128, 128]), ident,
                           b1, fr, start=(j == 0), inc=(j == 3))
                cs = slice(512 * bk, 512 * bk + 512)
                kb_t = tt(KB[:, cs], CK[:, cs], bnk, ALU.mult, p, k_t)
                side_free[i] = kb_t
            ds_t = tt(DS.rearrange("p (u c) -> p u c", u=12), DI.rearrange("p (u c) -> p u c", u=12),
                      tbl("strict").unsqueeze(1).to_broadcast([128, 12, 128]), ALU.mult, di_t)
            dm_t = tt(DI.rearrange("p (u c) -> p u c", u=12), DI.rearrange("p (u c) -> p u c", u=12),
                      tbl("incl").unsqueeze(1).to_broadcast([128, 12, 128]), ALU.mult, ds_t)
            yield
            for bk in range(3):
                cs = slice(512 * bk, 512 * bk + 512)
                for dst, rhs_, tok in ((DS, KB, kb_t), (DI, CQ, q_t)):
                    i, fr = side()
                    bnk = sbank(i)
                    for j in range(4):
                        u = 4 * bk + j
                        us = slice(128 * u, 128 * u + 128)
                        p = mm(bnk[:, 128 * j:128 * j + 128], CK[:, us], rhs_[:, us], k_t, tok, fr, start=(j == 0),
                               inc=(j == 3))
                    a = tt(dst[:, cs], bnk, dst[:, cs], ALU.mult, p, ds_t, dm_t)
                    side_free[i] = a
                    if dst is DS:
                        v3 = UU[:, cs].rearrange("p (u c) -> p u c", u=4)
                        b_ = tt(v3, DS[:, cs].rearrange("p (u c) -> p u c", u=4),
                                tbl("lv2").unsqueeze(1).to_broadcast([128, 4, 128]), ALU.mult, a, k_t, q_t)
                        u_t = tt(v3, v3, ident.unsqueeze(1).to_broadcast([128, 4, 128]), ALU.add, b_)
                        ns_t = a
                    else:
                        in_t = a
            yield
            for bk in range(3):
                i, fr = side()
                bnk = sbank(i)
                cs = slice(512 * bk, 512 * bk + 512)
                for j in range(4):
                    u = 4 * bk + j
                    p = tp(bnk[:, 128 * j:128 * j + 128], UU[:, 128 * u:128 * u + 128], u_t, fr, inc=(j == 3))
                t_t = act(TT_[:, cs], bnk, ACT.Copy, p, q_t, k_t)
                side_free[i] = t_t
            lastk = None
            for src, which in ((CV, "v"), (CK, "k")):
                for bk in range(3):
                    i, fr = side()
                    bnk = sbank(i)
                    cs = slice(512 * bk, 512 * bk + 512)
                    for j in range(4):
                        u = 4 * bk + j
                        p = tp(bnk[:, 128 * j:128 * j + 128], src[:, 128 * u:128 * u + 128], fr, silu_tok, k_t,
                               inc=(j == 3))
                    b3 = bnk.rearrange("p (u c) -> p u c", u=4)

                    def per(v):
                        return v[:, 4 * bk:4 * bk + 4].unsqueeze(2).to_broadcast([128, 4, 128])
                    r3 = lambda v: v[:, cs].rearrange("p (u c) -> p u c", u=4)
                    if which == "v":
                        a = tt(r3(RV), b3, per(gs[:, 0:12]), ALU.mult, p, b1, ns_t, in_t)
                        side_free[i] = a
                        vtp = p
                        rv_t = a
                    else:
                        a = tt(r3(RW), b3, per(bw), ALU.mult, p, bw_t, vtp)
                        a2 = tt(r3(KD), b3, per(kdw), ALU.mult, kd_t, c_free[0])
                        side_free[i] = [a, a2]
                        rw_t, kdt = a, a2
            qg_t = tt(CQ, CQ, EG, ALU.mult, eg_t, in_t)
            yield
            for m in (4, 8, 16, 32, 64):
                for bk in range(3):
                    i, fr = side()
                    bnk = sbank(i)
                    cs = slice(512 * bk, 512 * bk + 512)
                    for j in range(4):
                        u = 4 * bk + j
                        us = slice(128 * u, 128 * u + 128)
                        p = mm(bnk[:, 128 * j:128 * j + 128], DS[:, us], TT_[:, us], t_t, ns_t, fr, start=(j == 0),
                               inc=(j == 3))
                    a = tt(XX[:, cs].rearrange("p (u c) -> p u c", u=4), bnk.rearrange("p (u c) -> p u c", u=4),
                           tbl(f"lv{m}").unsqueeze(1).to_broadcast([128, 4, 128]), ALU.mult, p, u_t)
                    side_free[i] = a
                    x_t = a
                yield
                ups = []
                for bk in range(3):
                    cs = slice(512 * bk, 512 * bk + 512)
                    for which in (0, 1) if m < 64 else (0,):
                        i, fr = side()
                        bnk = sbank(i)
                        for j in range(4):
                            u = 4 * bk + j
                            us = slice(128 * u, 128 * u + 128)
                            l_, r_ = (XX[:, us], UU[:, us]) if which == 0 else (UU[:, us], XX[:, us])
                            p = mm(bnk[:, 128 * j:128 * j + 128], l_, r_, x_t, u_t, fr, start=(j == 0), inc=(j == 3))
                        ups.append((which, cs, bnk, i))
                    for which, cs2, bnk, i in ups:
                        dst = UU if which == 0 else TT_
                        a = tt(dst[:, cs2], dst[:, cs2], bnk, ALU.add, p)
                        side_free[i] = a
                        if which == 0:
                            u_t2 = a
                        else:
                            t_t = a
                    ups = []
                u_t = u_t2
                yield
            for bk in range(3):
                cs = slice(512 * bk, 512 * bk + 512)
                for which in (0, 1):
                    i, fr = side()
                    bnk = sbank(i)
                    for j in range(4):
                        u = 4 * bk + j
                        us = slice(128 * u, 128 * u + 128)
                        l_, r_ = (UU[:, us], RV[:, us]) if which == 0 else (RW[:, us], UU[:, us])
                        p = mm(bnk[:, 128 * j:128 * j + 128], l_, r_, u_t, rv_t, rw_t, fr, start=(j == 0),
                               inc=(j == 3))
                    dst = (U2, WT)[which]
                    a = act(dst[:, cs], bnk, ACT.Copy, p, u_t, t_t)
                    side_free[i] = a
                    uw_t = a
            s_t = dop0(lambda e: e.memset(SS[:, 0:768], 0.0), u_t, uw_t)
            yield
            EG4 = EG.rearrange("p (h t) -> p h t", h=6)
            o_rd = [None, None]
            for c in range(4):
                half, p0 = c // 2, 64 * (c % 2)
                S = SS[:, 768 * (c % 2):768 * (c % 2) + 768]
                S2 = SS[:, 768 * ((c + 1) % 2):768 * ((c + 1) % 2) + 768]
                (i1, f1), (i2, f2) = side(), side()
                for h in range(6):
                    bnk = sbank(i1) if h < 4 else sbank(i2)
                    hh = h % 4
                    us = 256 * h + 128 * half + p0
                    p = mm(bnk[p0:p0 + 64, 128 * hh:128 * hh + 128], WT[:, us:us + 64], S[:, 128 * h:128 * h + 128],
                           s_t, uw_t, f1, f2, start=(hh == 0), inc=(h in (3, 5)))
                for n_, i_, h0, nh in ((0, i1, 0, 4), (1, i2, 4, 2)):
                    v_t = tt(VN[p0:p0 + 64, 128 * h0:128 * (h0 + nh)].rearrange("p (h c) -> p h c", h=nh),
                             heads(U2)[p0:p0 + 64, h0:h0 + nh, half, :],
                             sbank(i_)[p0:p0 + 64, 0:128 * nh].rearrange("p (h c) -> p h c", h=nh),
                             ALU.subtract, p, uw_t, o_rd[c % 2])
                    side_free[i_] = v_t
                yield
                if c < 3:
                    (i1, f1), (i2, f2) = side(), side()
                    for h in range(6):
                        bnk = sbank(i1) if h < 4 else sbank(i2)
                        hh = h % 4
                        us = 256 * h + 128 * half
                        p = mm(bnk[:, 128 * hh:128 * hh + 128], KD[p0:p0 + 64, us:us + 128],
                               VN[p0:p0 + 64, 128 * h:128 * h + 128], v_t, kdt, f1, f2, start=(hh == 0),
                               inc=(h in (3, 5)))
                    for h in range(6):
                        i_ = i1 if h < 4 else i2
                        hh = h % 4
                        s_n = stt(S2[:, 128 * h:128 * h + 128], S[:, 128 * h:128 * h + 128],
                                  EG4[:, h, 64 * c + 63:64 * c + 64], sbank(i_)[:, 128 * hh:128 * hh + 128],
                                  ALU.mult, ALU.add, p, o_rd[(c + 1) % 2], eg_t)
                        side_free[i_] = s_n
                i, fr = side()
                for h in range(6):
                    ob = sbank(i)[:, 64 * h:64 * h + 64]
                    cs = slice(256 * h + 64 * c, 256 * h + 64 * c + 64)
                    mm(ob, S[:, 128 * h:128 * h + 128], CQ[:, cs], fr, qg_t, start=(h == 0), stop=False)
                    u0 = 256 * h + 128 * half + p0
                    p = mm(ob, VN[p0:p0 + 64, 128 * h:128 * h + 128], DI[p0:p0 + 64, u0:u0 + 64], v_t, in_t,
                           start=False, inc=(h == 5))
                o_t = act(OC.rearrange("p (h t) -> p h t", h=6)[:, :, 64 * c:64 * c + 64],
                          sbank(i)[:, 0:384].rearrange("p (h t) -> p h t", h=6), ACT.Copy, p, u_t)
                side_free[i] = o_t
                o_rd[c % 2] = p
                if c < 3:
                    s_t = s_n
                yield
            a = act(XX, OC, ACT.Square, o_t)
            yield
            lnexp()
            for k in range(3):
                i, fr = side()
                p = mm(sbank(i), ones, XX[:, 512 * k:512 * k + 512], a, fr, inc=True)
                r = act(TT_[:, 512 * k:512 * k + 512], sbank(i), ACT.Ln, p, scale=1.0 / 128, bias=tb("eps"))
                side_free[i] = r
            r = act(TT_, TT_, ACT.Exp, r, scale=-0.5, bias=0.0)
            a = stt(OC, OC, TB[:, AT["c_onorm_w"] + l:AT["c_onorm_w"] + l + 1], TT_, ALU.mult, ALU.mult, r)
            yc = Y[:, 10:16, :].rearrange("p i c -> p (i c)")
            c_done[0] = tt(yc, yc, OC, ALU.mult, a, zc_tok[0])

        c_done, zc_tok, zb_tok, za_tok, b_ready, a_done = [None], [None], [None], [None], [None], [None]

        def conformer(l, hb, acc, tmp, h_t):
            wo = AT["b_conv_w"] + 124 * l
            av = acc.rearrange("p (m c) -> p m c", m=4)
            last = [None] * 4
            for k in range(31):
                for m in range(4):
                    wk = TB[:, wo + 4 * k + m:wo + 4 * k + m + 1]
                    if k == 0:
                        last[m] = ts(av[:, m, :], hb[:, m, 0:256], wk, tb("b_conv_b", 4 * l + m), ALU.mult, ALU.add,
                                     h_t)
                    else:
                        last[m] = stt(av[:, m, :], hb[:, m, k:k + 256], wk, av[:, m, :], ALU.mult, ALU.add, last[m])
                if k % 8 == 7:
                    yield
            yield
            i, fr = side()
            for m in range(4):
                p = mm(sbank(i)[:, 0:256], ones, av[:, m, :], last[m], fr, start=(m == 0), stop=(m == 3),
                       inc=(m == 3))
            a = stt(av, sbank(i)[:, 0:256].unsqueeze(1).to_broadcast([128, 4, 256]), -1.0 / 512, av,
                    ALU.mult, ALU.add, p)
            side_free[i] = a
            c_t = a
            a = act(tmp, acc, ACT.Square, a)
            yield
            i, fr = side()
            tv = tmp.rearrange("p (m c) -> p m c", m=4)
            for m in range(4):
                p = mm(sbank(i)[:, 0:256], ones, tv[:, m, :], a, fr, start=(m == 0), stop=(m == 3), inc=(m == 3))
            rs = tmp[:, 0:256]
            lnexp()
            r = act(rs, sbank(i)[:, 0:256], ACT.Ln, p, scale=1.0 / 512, bias=tb("eps"))
            side_free[i] = r
            r = act(rs, rs, ACT.Exp, r, scale=-0.5, bias=0.0)
            a = tt(av, av, rs.unsqueeze(1).to_broadcast([128, 4, 256]), ALU.mult, r, c_t)
            for m in range(4):
                r = act(av[:, m, :], av[:, m, :], ACT.Silu, a, scale=tb("b_ln_w", 4 * l + m),
                        bias=tb("b_ln_b", 4 * l + m))
            b_ready[0] = r

        QK = sc(0, 2048)
        KR = sc(2048, 1024)
        AV = sc(3072, 512)
        QT = sc(3584, 1536)
        KT2 = sc(5120, 1024)
        AP_ = sc(6144, 4608)
        AS = sc(10752, 4608)
        SQ = sc(10752, 2048)

        def attention(l, qk_t, v_t):
            qk3 = QK.rearrange("p (n d) -> p n d", d=64)
            sm = SM[:, 512:640]
            a = act(SQ, QK, ACT.Square, qk_t)
            a = dop0(lambda e: e.tensor_reduce(sm[:, 0:32], SQ.rearrange("p (n d) -> p n d", d=64), AX.X, ALU.add), a)
            a = rstd_of(sm[:, 0:32], 64, sm[:, 0:32], a)
            a = tt(qk3, qk3, sm[:, 0:32].unsqueeze(2).to_broadcast([128, 32, 64]), ALU.mult, a)
            for t in range(2):
                for n0, n1, wn in ((0, 12, "q_norm_w"), (12, 16, "k_norm_w")):
                    v = qk3[:, 16 * t + n0:16 * t + n1, :]
                    b = tt(v, v, row(wn, l).unsqueeze(1).to_broadcast([128, n1 - n0, 64]), ALU.mult, a)
            q4 = QK.rearrange("p (t n d) -> p t n d", t=2, n=16)
            x1, x2 = q4[:, :, :, 0:8], q4[:, :, :, 8:16]
            cb = cos_t.unsqueeze(2).to_broadcast([128, 2, 16, 8])
            sb_ = sin_t.unsqueeze(2).to_broadcast([128, 2, 16, 8])
            r4 = [SQ[:, 256 * i:256 * i + 256].rearrange("p (t n d) -> p t n d", t=2, n=16) for i in range(4)]
            tt(r4[0], x1, cb, ALU.mult, b, rope_tok[0])
            tt(r4[1], x2, sb_, ALU.mult)
            tt(r4[2], x2, cb, ALU.mult)
            c = tt(r4[3], x1, sb_, ALU.mult)
            tt(x1, r4[0], r4[1], ALU.subtract, c)
            c = tt(x2, r4[2], r4[3], ALU.add)
            kr = KR.rearrange("p (t n r d) -> p t n r d", t=2, n=4, r=2)
            for t in range(2):
                d = dop0(lambda e, t=t: e.tensor_copy(kr[:, t], q4[:, t, 12:16, :].unsqueeze(2).to_broadcast(
                    [128, 4, 2, 64])), c)
            yield
            yield
            qt = QT.rearrange("p (i t) -> p i t", i=6)
            kt2 = KT2.rearrange("p (i t) -> p i t", i=4)
            for bk in range(5):
                i, fr = side()
                for j in range(2):
                    n = 2 * bk + j
                    for t in range(2):
                        src = q4[:, t, 2 * n:2 * n + 2, :].rearrange("p a d -> p (a d)") if n < 6 else \
                            kr[:, t, n - 6, :, :].rearrange("p r d -> p (r d)")
                        p = tp(sbank(i)[:, 256 * j + 128 * t:256 * j + 128 * t + 128], src, d, fr,
                               inc=(j == 1 and t == 1))
                dst = QT[:, 512 * bk:512 * bk + 512] if bk < 3 else KT2[:, 512 * (bk - 3):512 * (bk - 3) + 512]
                a = act(dst, sbank(i), ACT.Copy, p)
                side_free[i] = a
            yield
            s3 = AS.rearrange("p (h c) -> p h c", h=12)
            p3 = AP_.rearrange("p (h c) -> p h c", h=12)
            m2 = sm[:, 32:56].rearrange("p (b h) -> p b h", b=2)
            nm = sm[:, 56:80].rearrange("p (b h) -> p b h", b=2)
            den = sm[:, 80:104].rearrange("p (b h) -> p b h", b=2)
            es = sm[:, 104:128].rearrange("p (b h) -> p b h", b=2)
            for h in range(12):
                i, fr = side()
                b0 = 64 * (h % 2)
                mm(sbank(i)[:, 0:128], qt[b0:b0 + 64, h // 2, 0:128], kt2[b0:b0 + 64, h // 3, 0:128], a, fr)
                p = mm(sbank(i)[:, 128:384], qt[b0:b0 + 64, h // 2, 128:256], kt2[b0:b0 + 64, h // 3, 0:256],
                       start=False, inc=True)
                s_t = stt(s3[:, h, :], sbank(i)[:, 0:384], 0.125, tbl("amask", 384), ALU.mult, ALU.add, p)
                side_free[i] = s_t
                if h == 5:
                    yield
            a = dop0(lambda e: e.tensor_reduce(m2[:, 0, :], s3[:, :, 0:128], AX.X, ALU.max), s_t)
            a = dop0(lambda e: e.tensor_reduce(m2[:, 1, :], s3[:, :, 128:384], AX.X, ALU.max), s_t)
            sk = row("sinks", l).unsqueeze(1).to_broadcast([128, 2, 12])
            a = tt(m2, m2, sk, ALU.max, a)
            e0 = tt(es, sk, m2, ALU.subtract, a)
            a = ts(nm, m2, -1.0, None, ALU.mult, None, a)
            ek = act(es, es, ACT.Exp, e0, scale=1.0, bias=0.0)
            for h in range(12):
                for b_, (c0, c1) in enumerate(((0, 128), (128, 384))):
                    e1 = act(p3[:, h, c0:c1], s3[:, h, c0:c1], ACT.Exp, a, bias=sm[:, 56 + 12 * b_ + h:57 + 12 * b_ + h],
                             scale=1.0, accum_out=sm[:, 80 + 12 * b_ + h:81 + 12 * b_ + h])
            a = tt(den, den, es, ALU.add, e1, ek)
            a = dop0(lambda e: e.reciprocal(den, den), a)
            tt(p3[:, :, 0:128], p3[:, :, 0:128], den[:, 0, :].unsqueeze(2).to_broadcast([128, 12, 128]), ALU.mult, a)
            a = tt(p3[:, :, 128:384], p3[:, :, 128:384], den[:, 1, :].unsqueeze(2).to_broadcast([128, 12, 256]),
                   ALU.mult)
            yield
            for n in range(9):
                i, fr = side()
                for j in range(4):
                    u = 4 * n + j
                    p = tp(sbank(i)[:, 128 * j:128 * j + 128], AP_[:, 128 * u:128 * u + 128], a, fr, inc=(j == 3))
                if n % 2:
                    w = act(AS[:, 512 * n:512 * n + 512], sbank(i), ACT.Copy, p)
                else:
                    w = dop0(lambda e, i=i, n=n: e.tensor_copy(AS[:, 512 * n:512 * n + 512], sbank(i)), p)
                side_free[i] = w
                if n % 2:
                    wa = w
                else:
                    wd = w
                if n == 4:
                    yield
            x_tok[:] = [pool_dma(X[:, :, :], xsave.rearrange("(t p) c -> p t c", t=2), s_xr, n_xr, p)] * 4
            yield
            av = AV.rearrange("p (t d) -> p t d", t=2)
            for n in range(3):
                i, fr = side()
                for j in range(2):
                    for q in range(2):
                        h = 4 * n + 2 * j + q
                        b0 = 64 * q
                        kv = h // 3
                        o = sbank(i)[b0:b0 + 64, 256 * j:256 * j + 256]
                        vs = slice(64 * kv, 64 * kv + 64)
                        mm(o[:, 0:128], av[:, 0, vs], s3[:, h, 0:128], wa, wd, v_t, fr, start=(j == 0))
                        mm(o[:, 128:256], av[:, 0, vs], s3[:, h, 128:256], start=False, stop=False)
                        p = mm(o[:, 128:256], av[:, 1, vs], s3[:, h, 256:384], start=False,
                               inc=(j == 1 and q == 1))
                ya = Y[:, 2 * n:2 * n + 2, :].rearrange("p i c -> p (i c)")
                a_done[0] = tt(ya, ya, sbank(i), ALU.mult, p, za_tok[0])
                side_free[i] = a_done[0]

        rope_tok = [None]

        fetch()
        for _ in range(NSPL - 1):
            prep()
        sq_scr = sc(0, 512)
        for g in range(4):
            s_tok = sumsq(g, xt, sq_scr)
        XN = sc(0, 4096)
        h_all = norm_to_h("norm_w", 0, s_tok, XN, None)
        rope_tok[0] = rope_tables()
        y_read = [None]
        HB = sc(16950, 1144).rearrange("p (m c) -> p m c", m=4)

        def block1(l, start_free):
            c_free[0] = start_free
            z0 = dop0(lambda e: e.memset(RAW[:, :, 0:3], 0.0), start_free)
            wo = AT["c_conv_w"] + 72 * l
            silus = []

            def conv(i0, n, bank_ap, p):
                e_ = act(RAW[:, i0:i0 + n, 3:259], bank_ap, ACT.Copy, p, start_free)
                return e_

            def conv_taps(i0, n, e_):
                lt = [e_] * n
                for k in range(4):
                    for m in range(n):
                        wk = TB[:, wo + 18 * k + i0 + m:wo + 18 * k + i0 + m + 1]
                        if k == 0:
                            lt[m] = ts(CT[:, i0 + m, :], RAW[:, i0 + m, 0:256], wk, None, ALU.mult, None, e_, z0)
                        else:
                            lt[m] = stt(CT[:, i0 + m, :], RAW[:, i0 + m, k:k + 256], wk, CT[:, i0 + m, :],
                                        ALU.mult, ALU.add, lt[m])
                return act(CT[:, i0:i0 + n, :], CT[:, i0:i0 + n, :], ACT.Silu, lt[-1])

            pend = None
            for i in range(5):
                g = proj(512) if i < 4 else proj(256, mode="cm+")
                es = [conv(4 * i + 2 * b, 2, g.bank[b].rearrange("p (a c) -> p a c", a=2), g.tok)
                      for b in range(2 if i < 4 else 1)]
                if i == 4:
                    src = g.bank[1][:, 0:32].rearrange("p (t c) -> p t c", t=2)
                    q1 = dop0(lambda e: e.tensor_copy(gs[:, 120:132].rearrange("p (h t) -> p h t", h=6),
                                                       src[:, :, 0:6].rearrange("p t h -> p h t")), g.tok, start_free)
                    q2 = dop0(lambda e: e.tensor_copy(gs[:, 132:144].rearrange("p (h t) -> p h t", h=6),
                                                       src[:, :, 6:12].rearrange("p t h -> p h t")), g.tok)
                    g.free_with([es[-1], q2])
                    ba = [q1, q2]
                else:
                    g.free_with(es[-1])
                si = conv_taps(4 * i, 4 if i < 4 else 2, es[-1])
            dn = delta_net(l, si, ba, None)
            sides.append(dn)
            zt = []
            for n, t0 in ((4, 10), (2, 14)):
                g = proj(128 * n)
                for b in range(n // 2):
                    zc_tok[0] = act(Y[:, t0 + 2 * b:t0 + 2 * b + 2, :], g.bank[b].rearrange("p (a c) -> p a c", a=2),
                                    ACT.Silu, g.tok, y_read[0])
                g.free_with(zc_tok[0])
            hz = dop0(lambda e: e.memset(HB[:, :, 0:30], 0.0), start_free)
            g1 = proj(512)
            for b in range(2):
                ea = act(HB[:, 2 * b:2 * b + 2, 30:286], g1.bank[b].rearrange("p (a c) -> p a c", a=2), ACT.Copy,
                         g1.tok, start_free)
            g1.free_with(ea)
            g2 = proj(512)
            for b in range(2):
                et = act(Y[:, 6 + 2 * b:8 + 2 * b, :], g2.bank[b].rearrange("p (a c) -> p a c", a=2), ACT.Tanh, g2.tok,
                         y_read[0], scale=0.5, bias=0.0)
            g2.free_with(et)
            yb = Y[:, 6:10, :]
            a = ts(yb, yb, 0.5, 0.5, ALU.mult, ALU.add, et)
            hb_t = tt(HB[:, :, 30:286], HB[:, :, 30:286], yb, ALU.mult, a, ea)
            g3 = proj(512)
            for b in range(2):
                zb_tok[0] = act(yb[:, 2 * b:2 * b + 2, :], g3.bank[b].rearrange("p (a c) -> p a c", a=2), ACT.Silu,
                                g3.tok, hb_t)
            g3.free_with(zb_tok[0])
            finish(dn)
            acc = sc(15360, 1024)
            cf = conformer(l, HB, acc, sc(16950, 1024), [hb_t, hz, c_done[0]])
            sides.append(cf)
            qv = QK.rearrange("p (t c) -> p t c", t=2)
            for i in range(2):
                g = proj(512, mode="tm")
                for t in range(2):
                    q_t = act(qv[:, t, 512 * i:512 * i + 512], g.bank[t], ACT.Copy, g.tok, c_done[0])
                g.free_with(q_t)
            g = proj(256, mode="tm")
            for t in range(2):
                v_t = act(AV[:, 256 * t:256 * t + 256], g.bank[t][:, 0:256], ACT.Copy, g.tok, c_done[0])
            g.free_with(v_t)
            att = attention(l, [q_t, c_done[0]], v_t)
            finish(cf)
            sides.append(att)
            acc = acc.rearrange("p (m c) -> p m c", m=4)
            g = Group(lambda kt: acc[:, kt, :], lambda kt: b_ready[0], 512, "cm", 4).all()
            for m in range(4):
                b_t = stt(Y[:, 6 + m, :], g.bank[m // 2][:, 256 * (m % 2):256 * (m % 2) + 256],
                          tb("b_pw_b", 4 * l + m), Y[:, 6 + m, :], ALU.add, ALU.mult, g.tok, zb_tok[0])
            g.free_with(b_t)
            for n, t0 in ((4, 0), (2, 4)):
                g = proj(128 * n)
                for b in range(n // 2):
                    za_tok[0] = act(Y[:, t0 + 2 * b:t0 + 2 * b + 2, :], g.bank[b].rearrange("p (a c) -> p a c", a=2),
                                    ACT.Silu, g.tok, y_read[0])
                g.free_with(za_tok[0])
            h_read[0] = g.tok
            y_tok = {}

            def ysplit(k, n, tok):
                t = split(HH[:, k:k + n, :], HL[:, k:k + n, :], Y[:, k:k + n, :], tok, h_read[0])
                for j in range(n):
                    y_tok[k + j] = t

            for k in (6, 8):
                ysplit(k, 2, b_t)
            for k in (10, 12, 14):
                ysplit(k, 2, c_done[0])
            mk = lambda: Group(from_h, lambda kt: y_tok[kt], 512, "tm", 16)
            ga, gb = mk(), mk()
            for gg_ in (ga, gb):
                for _ in range(3):
                    gg_.feed()
            finish(att)
            for k in (0, 2, 4):
                ysplit(k, 2, a_done[0])
            for gg_ in (ga, gb):
                gg_.all()

            def add_x(i, g):
                for t in range(2):
                    v = X[:, t, 512 * i:512 * i + 512]
                    x_tok[i] = tt(v, v, g.bank[t], ALU.add, g.tok, x_tok[i])
                g.free_with(x_tok[i])
                return sumsq(i, x_tok[i], sq_scr)

            add_x(0, ga)
            add_x(1, gb)
            add_x(2, mk().all())
            g = mk().all()
            h_read[0] = g.tok
            y_read[0] = y_tok[0]
            return add_x(3, g)

        def save_x():
            return pool_dma(xsave.rearrange("(t p) c -> p t c", t=2), X[:, :, :], s_sp, n_sp, x_tok[3])

        sp = save_x()
        s_tok = block1(0, [h_all, sp])
        sp = save_x()
        free = norm_to_h("norm_w", 1, s_tok, XN, a_done[0])
        s_tok = block1(1, [free, sp])
        free = norm_to_h("g_pre_2", 0, s_tok, XN, a_done[0])

        ZT = Q[:, 8192:10240].rearrange("p (i c) -> p i c", i=8)
        o_tok = [None]

        def out_part(g, y_t):
            for i in range(4):
                q = Group(lambda kt: (YH[:, kt - 8 * g, :], YL[:, kt - 8 * g, :]), lambda kt: y_t[kt - 8 * g], 512,
                          "tm", 8).all()
                for t in range(2):
                    o = O[:, t, 512 * i:512 * i + 512]
                    if g == 0:
                        o_tok[0] = act(o, q.bank[t], ACT.Copy, q.tok, y_read[0])
                    else:
                        o_tok[0] = tt(o, o, q.bank[t], ALU.add, q.tok, o_tok[0])
                q.free_with(o_tok[0])
            y_read[0] = q.tok

        def pool_layer(free):
            U = Q[:, 18432:19520].rearrange("p (i c) -> p i c", i=4)
            A = Q[:, 19520:20608].rearrange("p (i c) -> p i c", i=4)
            B = Q[:, 20608:21696].rearrange("p (i c) -> p i c", i=4)
            for b in (U, A, B):
                z_ = dop0(lambda e, b=b: e.memset(b[:, :, 0:16], 0.0), free)
            u_free, d_free, z_free = [z_], [free], [free]
            d_tok, y_tok = {}, {}

            def load_u(g):
                for i in range(2):
                    q = proj(512)
                    for b in range(2):
                        t = act(U[:, 2 * b:2 * b + 2, 16:272], q.bank[b].rearrange("p (a c) -> p a c", a=2), ACT.Copy,
                                q.tok, u_free[0], free)
                    q.free_with(t)
                    src, k = U, 1
                    tok = t
                    for s in range(g + 1):
                        dst = (A, B)[s % 2]
                        tok = tt(dst[:, :, 16:272], src[:, :, 16:272], src[:, :, 16 - k:272 - k], ALU.add, tok, z_)
                        src, k = dst, 2 * k
                    other = B if src is A else A
                    tok = ts(other[:, :, 16:272], src[:, :, 16:272], 1.0 / k, None, ALU.mult, None, tok)
                    tok = tt(other[:, :, 16:32], src[:, :, 16:32],
                             tbl(f"cnt{g}", 16).unsqueeze(1).to_broadcast([128, 4, 16]), ALU.mult, tok)
                    tok = tt(src[:, :, 16:272], other[:, :, 16:272], U[:, :, 16:272], ALU.subtract, tok)
                    d = split(DH[:, 4 * i:4 * i + 4, :], DL[:, 4 * i:4 * i + 4, :], src[:, :, 16:272], tok, d_free[0])
                    u_free[0] = d
                    for j in range(4):
                        d_tok[4 * i + j] = d

            def load_z(g):
                for i in range(2):
                    q = proj(512)
                    for b in range(2):
                        t0 = 4 * i + 2 * b
                        t = act(ZT[:, t0:t0 + 2, :], q.bank[b].rearrange("p (a c) -> p a c", a=2), ACT.Silu, q.tok,
                                z_free[0])
                    q.free_with(t)
                for j in range(8):
                    t = ts(ZT[:, j, :], ZT[:, j, :], tb("pool_scale_2", 8 * g + j), None, ALU.mult, None, t)
                return t

            def mix(g, zt):
                for i in range(2):
                    q = Group(lambda kt: (DH[:, kt, :], DL[:, kt, :]), lambda kt: d_tok[kt], 512, "cm", 8).all()
                    for j in range(4):
                        n = 4 * i + j
                        t = stt(ZT[:, n, :], q.bank[j // 2][:, 256 * (j % 2):256 * (j % 2) + 256],
                                tb("pool_b_2", 8 * g + n), ZT[:, n, :], ALU.add, ALU.mult, q.tok, zt)
                    q.free_with(t)
                    y = split(YH[:, 4 * i:4 * i + 4, :], YL[:, 4 * i:4 * i + 4, :], ZT[:, 4 * i:4 * i + 4, :], t,
                              y_read[0], free)
                    for j in range(4):
                        y_tok[4 * i + j] = y
                z_free[0] = y
                d_free[0] = q.tok

            load_u(0)
            for g in range(4):
                zt = load_z(g)
                if g > 0:
                    out_part(g - 1, dict(y_tok))
                mix(g, zt)
                if g < 3:
                    load_u(g + 1)
            out_part(3, dict(y_tok))

        def lru_layer(free):
            RAWL = Q[:, 14336:15372].rearrange("p (i c) -> p i c", i=4)
            UC = Q[:, 15372:16396]
            R, IG, TA, SQ2 = (Q[:, 16396 + 1024 * k:17420 + 1024 * k] for k in range(4))
            ucv = UC.rearrange("p (i c) -> p i c", i=4)
            c8 = SM[:, 640:672]
            ng = SM[:, 672:704]
            a = ts(ng, TB[:, AT["lru_L_2"]:AT["lru_L_2"] + 32], -1.0, None, ALU.mult, None, free)
            a = softplus(c8, ng, SM[:, 704:800], 32, a)
            c8_t = ts(c8, c8, -8.0, None, ALU.mult, None, a)
            z_ = dop0(lambda e: e.memset(RAWL[:, :, 0:3], 0.0), free)
            raw_rd, uc_rd, z_rd = [z_], [free], {0: free, 1: free}
            wo = AT["conv_w_2"]
            y_tok = {}
            uct = {}

            def load_u(n):
                q = proj(512)
                for b in range(2):
                    t = act(RAWL[:, 2 * b:2 * b + 2, 3:259], q.bank[b].rearrange("p (a c) -> p a c", a=2), ACT.Copy,
                            q.tok, raw_rd[0], free)
                q.free_with(t)
                return t

            def conv(n, t):
                lt = [t] * 4
                for k in range(4):
                    for m in range(4):
                        i = 4 * n + m
                        wk = TB[:, wo + 32 * k + i:wo + 32 * k + i + 1]
                        if k == 0:
                            lt[m] = ts(ucv[:, m, :], RAWL[:, m, 0:256], wk, tb("conv_b_2", i), ALU.mult, ALU.add,
                                       lt[m], uc_rd[0])
                        else:
                            lt[m] = stt(ucv[:, m, :], RAWL[:, m, k:k + 256], wk, ucv[:, m, :], ALU.mult, ALU.add,
                                        lt[m])
                raw_rd[0] = lt[-1]
                uct[n] = lt[-1]

            def load_z(n):
                q = proj(512)
                for b in range(2):
                    t0 = 4 * (n % 2) + 2 * b
                    zt = act(ZT[:, t0:t0 + 2, :], q.bank[b].rearrange("p (a c) -> p a c", a=2), ACT.Silu, q.tok,
                             z_rd[n % 2])
                q.free_with(zt)
                return zt

            def gates(n, zt):
                for dst, bias in ((R, "lru_ba_2"), (IG, "lru_bx_2")):
                    c = used[0]
                    w = W[:, c % NRAW, 0:1024].rearrange("p (k n) -> p k n", k=4)
                    q = Group(None, None, 512, "cm", 2)
                    for kl in range(2):
                        for h in range(2):
                            for j in range(2):
                                last = kl == 1 and h == 1 and j == 1
                                t = mm(q.bank[h][:, 256 * j:256 * j + 256], w[:, 2 * h + kl, 128 * j:128 * j + 128],
                                       ucv[:, 2 * h + kl, :], part_tok[c], q.free, uct[n],
                                       start=(kl == 0 and j == 0), stop=(kl == 1), inc=last)
                    for j in range(4):
                        e_ = act(dst[:, 256 * j:256 * j + 256], q.bank[j // 2][:, 256 * (j % 2):256 * (j % 2) + 256],
                                 ACT.Sigmoid, t, free, y_tok.get(0), y_tok.get(4), bias=tb(bias, 4 * n + j), scale=1.0)
                    q.free_with(e_)
                    use(c, t)
                r3 = R.rearrange("p (i c) -> p i c", i=4)
                cb = c8[:, 4 * n:4 * n + 4].unsqueeze(2).to_broadcast([128, 4, 256])
                la = tt(r3, r3, cb, ALU.mult, e_, c8_t)
                th = act(TA, R, ACT.Tanh, la, scale=-1.0, bias=0.0)
                ex = act(R, R, ACT.Exp, th, scale=1.0, bias=0.0)
                a = act(SQ2, R, ACT.Square, ex)
                b_ = tt(IG, IG, UC, ALU.mult, e_, uct[n])
                uc_rd[0] = [b_, t]
                a = stt(TA, SQ2, 1.0, TA, ALU.add, ALU.mult, a)
                a = ts(TA, TA, 0.0, None, ALU.max, None, a)
                a = act(TA, TA, ACT.Sqrt, a)
                a = tt(IG, IG, TA, ALU.mult, a, b_)
                for j in range(4):
                    js = slice(256 * j, 256 * j + 256)
                    s_ = dop0(lambda e, js=js: e.tensor_tensor_scan(TA[:, js], R[:, js], IG[:, js], 0.0, ALU.mult,
                                                                     ALU.add), a)
                j0 = 4 * (n % 2)
                zv = ZT[:, j0:j0 + 4, :]
                t = tt(zv, zv, TA.rearrange("p (i c) -> p i c", i=4), ALU.mult, s_, zt)
                y = split(YH[:, j0:j0 + 4, :], YL[:, j0:j0 + 4, :], zv, t, y_read[0], free)
                z_rd[n % 2] = y
                for j in range(4):
                    y_tok[j0 + j] = y

            conv(0, load_u(0))
            for n in range(8):
                zt = load_z(n)
                if n < 7:
                    nxt = load_u(n + 1)
                if n % 2 == 0 and n > 0:
                    out_part(n // 2 - 1, dict(y_tok))
                gates(n, zt)
                if n < 7:
                    conv(n + 1, nxt)
            out_part(3, dict(y_tok))

        def post(l, free):
            GP, GL, junk = Q[:, 8192:10240], Q[:, 18432:20480], Q[:, 20480:20992]
            PT = Q[:, 21760:22272].rearrange("p (k t) -> p k t", k=2)
            done = [o_tok[0], y_read[0]]
            h_read[0] = y_read[0]
            gt1 = pool_dma(GP, gpost_d[l:l + 1, :].to_broadcast([128, 2048]), s_g, n_g, o_tok[0])
            gt2 = pool_dma(GL, gplo_d[l:l + 1, :].to_broadcast([128, 2048]), s_g, n_g)
            gt = pool_dma(Q[:, 21760:22272], pT_d[:, 512 * l:512 * l + 512], s_g, n_g)
            for i in range(4):
                cs = slice(512 * i, 512 * i + 512)
                for t in range(2):
                    s1 = act(junk, O[:, t, cs], ACT.Square, done, accum_out=SM[:, 4 * t + i:4 * t + i + 1])
            a = dop0(lambda e: e.tensor_reduce(SM[:, 8:10], SM[:, 0:8].rearrange("p (t g) -> p t g", t=2), AX.X,
                                                ALU.add), s1)
            r = rstd_of(SM[:, 8:10], 2048, SM[:, 12:14], a)
            for i in range(4):
                q = Group(lambda kt: PT[:, kt, :], lambda kt: gt, 512, "tm", 2)
                q.feed(kts=range(2), col=512 * (i % 2), last_use=(i % 2 == 1))
                for t in range(2):
                    e_t = act(E[:, t, 512 * i:512 * i + 512], q.bank[t], ACT.Copy, q.tok, done)
                q.free_with(e_t)
            for i in range(4):
                cs = slice(512 * i, 512 * i + 512)
                for t in range(2):
                    o_ = stt(O[:, t, cs], O[:, t, cs], SM[:, 12 + t:13 + t], GP[:, cs], ALU.mult, ALU.mult, r, gt)
                    x_tok[i] = tt(X[:, t, cs], X[:, t, cs], O[:, t, cs], ALU.add, o_)
                s_tok = sumsq(i, x_tok[i], junk)
            ff = norm_to_h("g_ple_in_2", l, s_tok, XN, [x_tok[3]])
            for i in range(4):
                q = proj(512, mode="tm")
                cs = slice(512 * i, 512 * i + 512)
                for t in range(2):
                    g_ = act(O[:, t, cs], q.bank[t], ACT.Sigmoid, q.tok, ff)
                    m_ = tt(E[:, t, cs], E[:, t, cs], O[:, t, cs], ALU.mult, g_, e_t)
                    s1 = act(junk, E[:, t, cs], ACT.Square, m_, accum_out=SM[:, 4 * t + i:4 * t + i + 1])
                    n_ = tt(E[:, t, cs], E[:, t, cs], GL[:, cs], ALU.mult, s1, gt)
                q.free_with(g_)
            h_read[0] = q.tok
            a = dop0(lambda e: e.tensor_reduce(SM[:, 8:10], SM[:, 0:8].rearrange("p (t g) -> p t g", t=2), AX.X,
                                                ALU.add), s1)
            r = rstd_of(SM[:, 8:10], 2048, SM[:, 12:14], a)
            for i in range(4):
                cs = slice(512 * i, 512 * i + 512)
                for t in range(2):
                    x_tok[i] = stt(X[:, t, cs], E[:, t, cs], SM[:, 12 + t:13 + t], X[:, t, cs], ALU.mult, ALU.add,
                                   r, n_)
                if l == 0:
                    s_tok = sumsq(i, x_tok[i], junk)
            return s_tok

        pool_layer([free, a_done[0]])
        s_tok = post(0, None)
        free = norm_to_h("g_pre_2", 1, s_tok, XN, [x_tok[3]])
        lru_layer([free, x_tok[3]])
        s_tok = post(1, None)
        assert used[0] == len(chunks) == len(released)

        arrange([(pe, 60.0), (dv, 60.0), (ac, 60.0), (sy, 2000.0), (po, 2500.0)])
        block = ctx.enter_context(nc.Block())

        @block.sync
        def _(e):
            sy.play(e)
            for t in range(2):
                e.wait_ge(x_tok[3].sem, x_tok[3].value)
                e.dma_start(out[128 * t:128 * t + 128, :], X[:, t, :]).then_inc(s_out, 16)
            e.wait_ge(s_out, 32)

        @block.gpsimd
        def _(e):
            po.play(e)
            e.wait_ge(s_sp, n_sp[0])

        @block.tensor
        def _(e):
            pe.play(e)

        @block.vector
        def _(e):
            dv.play(e)

        @block.scalar
        def _(e):
            ac.play(e)


def kernel(**inputs):
    import concourse.bacc as bacc
    from concourse.bass_utils import run_bass_kernel_spmd as run

    arr = {n: np.asarray(v) for n, v in inputs.items()}
    flat = {"lru_wa_2": arr["lru_wa_2"].reshape(1, 4096, 256), "lru_wx_2": arr["lru_wx_2"].reshape(1, 4096, 256),
            "pool_w_2": arr["pool_w_2"].reshape(4, 1024, 1024)}
    ch = plan()
    total = sum(128 * nk * n for _, _, _, nk, _, n in ch)
    wall = np.empty(total, np.float32)
    off = 0
    for name, l, k0, nk, c0, n in ch:
        a = flat.get(name, arr[name])[l][128 * k0:128 * (k0 + nk), c0:c0 + n]
        wall[off:off + 128 * nk * n] = a.reshape(nk, 128, n).transpose(1, 0, 2).ravel()
        off += 128 * nk * n
    cols = list(const_columns().values())
    for name in CHAN:
        cols.append(arr[name].reshape(-1, 128).T)
    for name in ROW:
        cols.append(np.broadcast_to(arr[name].reshape(1, -1), (128, arr[name].size)))
    tab = np.ascontiguousarray(np.concatenate(cols, axis=1))
    pT = np.ascontiguousarray(arr["p_2"][:, 0].reshape(2, 256, 2, 128).transpose(3, 0, 2, 1).reshape(128, 1024))
    arrays = {
        "wall": wall, "tab": tab, "pT": pT,
        "pos": np.ascontiguousarray(arr["positions"].reshape(2, 128).T),
        "x": np.ascontiguousarray(arr["x"].reshape(256, 2048)),
        "g_post": np.ascontiguousarray(arr["g_post_2"]), "g_ple_out": np.ascontiguousarray(arr["g_ple_out_2"]),
    }
    nc = bacc.Bacc("TRN2", target_bir_lowering=False, num_devices=1)
    d = {n: nc.dram_tensor("in_" + n, a.shape, mybir.dt.from_np(a.dtype), kind="ExternalInput").ap()
         for n, a in arrays.items()}
    out = nc.dram_tensor("out_0", (256, 2048), F32, kind="ExternalOutput").ap()
    xsave = nc.dram_tensor("xsave", (256, 2048), F32, kind="Internal").ap()
    program(nc, d["wall"], d["tab"], d["pos"], d["pT"], d["x"], d["g_post"], d["g_ple_out"], xsave, out)
    r = run(nc, [{"in_" + n: a for n, a in arrays.items()}], core_ids=[0])
    return r.results[0]["out_0"].reshape(1, 256, 2048)
```

```python
import numpy as np
import concourse.bass as bass
from concourse import mybir
from contextlib import ExitStack

F32 = mybir.dt.float32
F32R = mybir.dt.float32r
I32 = mybir.dt.int32
ALU = mybir.AluOpType
ACT = mybir.ActivationFunctionType
AX = mybir.AxisListType

T = 256
NRAW = 3
NSPL = 3
SPLIT = ("w_in", "w_out", "w_in_2", "w_out_2", "w_ple_gate_2", "pool_w_2")
SLOT = 2048
TABLE = {ACT.Copy: None, ACT.Square: None, ACT.Abs: None, ACT.Ln: "lnexp", ACT.Exp: "lnexp"}
LNEXP = "natural_log_exp_and_others"



def plan():
    ch = []

    def cols(name, l, c0, n, nkt=16, step=4):
        for k in range(0, nkt, step):
            ch.append((name, l, k, min(step, nkt - k), c0, n))

    for l in range(2):
        for i in range(4):
            cols("w_in", l, 3584 + 512 * i, 512)
        cols("w_in", l, 5632, 268)
        cols("w_in", l, 5900, 512)
        cols("w_in", l, 6412, 256, step=8)
        for c in (2048, 2560, 3072, 0, 512):
            cols("w_in", l, c, 512)
        cols("w_in", l, 1024, 256, step=8)
        cols("b_pw_w", l, 0, 512, nkt=4)
        cols("w_in", l, 1280, 512)
        cols("w_in", l, 1792, 256, step=8)
        late = ((6, 4), (10, 4), (14, 2))
        soon = ((0, 4), (4, 2))
        for part, gs in ((late, (0, 1)), (soon, (0, 1)), (late + soon, (2,)), (late + soon, (3,))):
            for g in gs:
                for k, n in part:
                    ch.append(("w_out", l, k, n, 512 * g, 512))
    def u(l, g, i):
        cols("w_in_2", l, 1024 * g + 512 * i, 512)

    def z(l, g, i):
        cols("w_in_2", l, 4096 + 1024 * g + 512 * i, 512)

    def o(l, g):
        for i in range(4):
            for k in (0, 4):
                ch.append(("w_out_2", l, 8 * g + k, 4, 512 * i, 512))

    def pool(g):
        for i in range(2):
            for k in (0, 4):
                ch.append(("pool_w_2", g, k, 4, 512 * i, 512))

    def gates(n):
        ch.append(("lru_w", 0, 8 * n, 8, 0, 256))

    def post(l):
        for g in range(2):
            ch.append(("w_ple_2", l, 0, 2, 1024 * g, 1024))
        for g in range(4):
            cols("w_ple_gate_2", l, 512 * g, 512)

    u(0, 0, 0), u(0, 0, 1)
    for g in range(4):
        z(0, g, 0), z(0, g, 1)
        if g > 0:
            o(0, g - 1)
        pool(g)
        if g < 3:
            u(0, g + 1, 0), u(0, g + 1, 1)
    o(0, 3)
    post(0)
    u(1, 0, 0)
    for n in range(8):
        z(1, n // 2, n % 2)
        if n < 7:
            u(1, (n + 1) // 2, (n + 1) % 2)
        if n % 2 == 0 and n > 0:
            o(1, n // 2 - 1)
        gates(n)
    for k in (0, 4):
        for i in range(4):
            ch.append(("w_out_2", 1, 24 + k, 4, 512 * i, 512))
    post(1)
    return ch



def const_columns():
    i = np.arange(128)
    c = {}
    c["ident"] = np.eye(128)
    same = (i[:, None] // 64) == (i[None, :] // 64)
    c["cum"] = same & (i[:, None] <= i[None, :])
    c["last"] = same
    c["incl"] = same & (i[:, None] <= i[None, :])
    c["strict"] = -1.0 * (same & (i[:, None] < i[None, :]))
    up = lambda m: ((i[:, None] // m) == (i[None, :] // m)) & ((i[:, None] % m) < m // 2) & ((i[None, :] % m) >= m // 2)
    c["lv2"] = up(2)
    for m in (4, 8, 16, 32, 64):
        c[f"lv{m}"] = up(m).T
    q = i[:, None]
    k = i[None, :]
    neg = np.float32(-1e30)
    c["amask"] = np.concatenate([np.where(k <= q, 0, neg), np.where(k > q, 0, neg), np.where(k <= q, 0, neg)], axis=1)
    c["ones"] = np.ones((128, 128))
    c["eps"] = np.full((128, 1), 1e-6)
    c["zero"] = np.zeros((128, 1))
    inv = np.float32(500000.0) ** (-np.arange(0, 16, 2, dtype=np.float32) / np.float32(16))
    c["invf"] = np.broadcast_to(inv, (128, 8))
    for g, w in enumerate((2, 4, 8, 16)):
        cnt = np.minimum(np.arange(1, 17), w)
        c[f"cnt{g}"] = np.broadcast_to(1.0 / cnt.astype(np.float32), (128, 16))
    return {n: np.ascontiguousarray(v, dtype=np.float32) for n, v in c.items()}


CHAN = ["norm_w", "b_conv_w", "b_conv_b", "b_ln_w", "b_ln_b", "b_pw_b", "c_conv_w", "c_onorm_w", "g_pre_2",
        "pool_b_2", "pool_scale_2", "conv_w_2", "conv_b_2", "lru_ba_2", "lru_bx_2", "lru_L_2", "g_ple_in_2"]
ROW = ["q_norm_w", "k_norm_w", "sinks", "c_a_log", "c_dt_bias"]
SHAPE = {"norm_w": (2, 2048), "b_conv_w": (2, 31, 512), "b_conv_b": (2, 512), "b_ln_w": (2, 512), "b_ln_b": (2, 512),
         "b_pw_b": (2, 512), "c_conv_w": (2, 4, 2304), "c_onorm_w": (2, 128), "g_pre_2": (2, 2048),
         "pool_b_2": (1, 4096), "pool_scale_2": (1, 4096), "conv_w_2": (1, 4, 4096), "conv_b_2": (1, 4096),
         "lru_ba_2": (1, 4096), "lru_bx_2": (1, 4096), "lru_L_2": (1, 4096), "g_ple_in_2": (2, 2048),
         "q_norm_w": (2, 64), "k_norm_w": (2, 64), "sinks": (2, 12), "c_a_log": (2, 6), "c_dt_bias": (2, 6)}


def table_order():
    first = ["ident", "eps", "norm_w"]
    return first + [n for n in list(const_columns()) + CHAN + ROW if n not in first]


def column_table():
    at, n = {}, 0
    const = const_columns()
    for name in table_order():
        at[name] = n
        n += const[name].shape[1] if name in const else int(np.prod(SHAPE[name])) // (128 if name in CHAN else 1)
    return at, n


def NQ_BASE(nc, n):
    return nc.sbuf_base - 4 * n


PE_STREAMS = ("side", "main", "conv")
DV_STREAMS = ("main", "prep", "side", "conv")
AC_STREAMS = ("main", "prep", "side", "conv")


class Unit:

    def __init__(self):
        self.items, self.cost, self.sem, self.value, self.done, self.dma = [], 0.0, None, None, None, False
        self.kind = None


class Eng:

    def __init__(self, sem=None, chain=False, streams=("main",)):
        self.sem, self.chain = sem, chain
        self.q = {s: [] for s in streams}
        self.open = {s: None for s in streams}
        self.tail = {s: None for s in streams}
        self.order = []

    def op(self, fn, *toks, inc=True, free=False, stream="main", cost=500.0, sem=None, value=None,
           kind=None):
        if stream not in self.q:
            stream = "main"
        u = self.open[stream] or Unit()
        waits = flat(toks)
        if self.chain and not free and self.tail[stream] is not None:
            waits.append(self.tail[stream])
        u.items.append((waits, fn, cost))
        u.kind = kind or u.kind
        if not inc:
            self.open[stream] = u
            return None
        self.open[stream] = None
        u.sem, u.value = sem or self.sem, value
        self.q[stream].append(u)
        if not free:
            self.tail[stream] = u
        return u

    def play(self, e):
        seen = {}
        for u in self.order:
            for k, (waits, fn, _) in enumerate(u.items):
                for w in waits:
                    if seen.get(id(w.sem), 0) < w.value:
                        seen[id(w.sem)] = w.value
                        e.wait_ge(w.sem, w.value)
                r = fn(e)
                if k == len(u.items) - 1:
                    r.then_inc(u.sem, 16 if u.dma else 1)


def flat(toks):
    out = []
    for t in toks:
        if isinstance(t, (list, tuple)):
            out += flat(t)
        elif t is not None:
            out.append(t)
    return out


def arrange(engines):
    free = [0.0] * len(engines)
    table = None
    while True:
        best = None
        for n, (en, _) in enumerate(engines):
            cand = None
            for pr, (s, q) in enumerate(en.q.items()):
                if not q:
                    continue
                u, t, ok = q[0], free[n], True
                for waits, _, cost in u.items:
                    for w in waits:
                        if w.done is None:
                            ok = False
                            break
                        t = max(t, w.done)
                    if not ok:
                        break
                if not ok:
                    continue
                key = (max(t - free[n] - 50.0, 0.0), pr)
                if cand is None or key < cand[0]:
                    cand = (key, t, s)
            if cand is not None and (best is None or cand[1] < best[0]):
                best = (cand[1], n, cand[2])
        if best is None:
            break
        _, n, s = best
        en, stall = engines[n]
        u = en.q[s].pop(0)
        t = free[n]
        if u.kind not in (None, table):
            table, t = u.kind, t + 1300.0
        for waits, _, cost in u.items:
            for w in waits:
                t = max(t, w.done)
            t += cost
        free[n] = t
        u.done = t + stall
        en.order.append(u)
        if u.value is None:
            u.value = len(en.order)
    for en, _ in engines:
        assert not any(en.q.values())


def size(ap):
    n = 1
    for k in ap.shape[1:]:
        n *= int(k)
    return n


def program(nc, wall, tab, pos_d, pT_d, xin, gpost_d, gplo_d, xsave, out):
    chunks = plan()
    AT, NT = column_table()
    ctx = ExitStack()
    with ctx:
        TB = ctx.enter_context(nc.sbuf_tensor("TB", [128, NT], F32))
        SM = ctx.enter_context(nc.sbuf_tensor("SM", [128, 1056], F32))
        POSI = ctx.enter_context(nc.sbuf_tensor("POSI", [128, 8], I32))
        W = ctx.enter_context(nc.sbuf_tensor("W", [128, NRAW, SLOT], F32))
        WH = ctx.enter_context(nc.sbuf_tensor("WH", [128, NSPL, SLOT], F32R))
        WL = ctx.enter_context(nc.sbuf_tensor("WL", [128, NSPL, SLOT], F32R))
        HH = ctx.enter_context(nc.sbuf_tensor("HH", [128, 16, 256], F32R))
        HL = ctx.enter_context(nc.sbuf_tensor("HL", [128, 16, 256], F32R))
        NQ = 22320
        Q = ctx.enter_context(nc.sbuf_tensor("Q", [128, NQ], F32))
        q_at = NQ_BASE(nc, NQ)

        def over(name, off, shape, dt=F32):
            return nc.alloc_sbuf_tensor_at(name, shape, dt, offset=q_at + 4 * off)

        X = over("X", 10240, [128, 2, 2048])
        Y = over("Y", 0, [128, 16, 256])
        O = over("O", 0, [128, 2, 2048])
        YH = over("YH", 4096, [128, 8, 256], F32R)
        YL = over("YL", 6144, [128, 8, 256], F32R)
        DH = over("DH", 14336, [128, 8, 256], F32R)
        DL = over("DL", 16384, [128, 8, 256], F32R)
        E = over("E", 14336, [128, 2, 2048])
        PS = ctx.enter_context(nc.psum_tensor("PS", [128, 4096], F32))

        def sem(n):
            return ctx.enter_context(nc.semaphore(n))

        pe = Eng(sem("s_pe"), streams=PE_STREAMS)
        dv = Eng(sem("s_dv"), chain=True, streams=DV_STREAMS)
        ac = Eng(sem("s_ac"), chain=True, streams=AC_STREAMS)
        sy, po = Eng(), Eng()
        at = ["main"]

        def dma(q, dst, src, s, value, *toks):
            u = q.op(lambda e: e.dma_start(dst, src), *toks, sem=s, value=value, cost=size(dst) * 512 / 360.0)
            u.dma = True
            return u

        s_slot = [sem(f"s_w{i}") for i in range(NRAW)]
        s_tabh = sem("s_tabh")
        s_xg = [sem(f"s_x{g}") for g in range(4)]
        s_tab, s_xr, s_g, s_out, s_sp = sem("s_tab"), sem("s_xr"), sem("s_g"), sem("s_out"), sem("s_sp")

        def pool_dma(dst, src, s, count, *toks):
            count[0] += 16
            return dma(po, dst, src, s, count[0], *toks)

        def tb(name, off=0, n=1):
            return TB[:, AT[name] + off:AT[name] + off + n]

        def tbl(name, n=128):
            return TB[:, AT[name]:AT[name] + n]

        def row(name, l):
            w = SHAPE[name][1]
            return TB[:, AT[name] + l * w:AT[name] + (l + 1) * w]

        ident, ones = tbl("ident"), tbl("ones")
        NH = AT["norm_w"] + 32
        head_tok = [dma(sy, TB[:, 0:NH], tab[:, 0:NH], s_tabh, 16)]
        xv_d = xin.rearrange("(t p) c -> p t c", t=2)
        x_tok = [dma(sy, X[:, :, 512 * g:512 * g + 512], xv_d[:, :, 512 * g:512 * g + 512], s_xg[g], 16)
                 for g in range(4)]
        n_xr, n_sp, n_g, n_gp, n_pt = [0], [0], [0], [0], [0]
        s_gp, s_pt = sem("s_gp"), sem("s_pt")

        def sc(off, n):
            assert off + n <= NQ - 4096, (off, n)
            return Q[:, 4096 + off:4096 + off + n]

        def dop(o, fn, *w, base=65.0, rate=0.96):
            return dv.op(fn, *w, stream=at[0], cost=base + size(o) / rate)

        def dop0(fn, *w, **k):
            return dv.op(fn, *w, stream=at[0], **k)

        def tt(o, a, b, op, *w):
            return dop(o, lambda e: e.tensor_tensor(o, a, b, op), *w)

        def stt(o, a, s, b, op0, op1, *w):
            return dop(o, lambda e: e.scalar_tensor_tensor(out=o, in0=a, scalar=s, in1=b, op0=op0, op1=op1), *w,
                       base=130.0)

        def ts(o, a, s1, s2, op0, op1, *w):
            fn = ((lambda e: e.tensor_scalar(o, a, s1, None, op0)) if s2 is None else
                  (lambda e: e.tensor_scalar(o, a, s1, s2, op0, op1)))
            return dop(o, fn, *w, base=65.0 if isinstance(s1, float) else 130.0, rate=1.92)

        def act(o, a, f, *w, **k):
            return ac.op(lambda e: e.activation(o, a, f, **k), *w, stream=at[0], kind=TABLE.get(f, f),
                         cost=45 + size(o) / 1.2 + 100 * ("bias" in k or "scale" in k) + 140 * ("accum_out" in k))

        def lnexp():
            ac.op(lambda e: e.preload_act_table_set(LNEXP), inc=False, stream=at[0], cost=0.0)

        def mm(o, l, r, *w, start=True, stop=True, inc=False):
            return pe.op(lambda e: e.matmul(o, l, r, start=start, stop=stop, skip_group_check=True), *w, inc=inc,
                         stream=at[0], cost=max(size(r) * (1 if r.dtype == F32R else 4), 128) / 2.4)

        def tp(o, a, *w, inc=False):
            return pe.op(lambda e: e.transpose(o, a, ident), *w, inc=inc, stream=at[0], cost=size(o) * 2 / 2.4)

        side_free = [None] * 4
        side_at = [0]

        def side():
            i = side_at[0] % 4
            side_at[0] += 1
            return i, side_free[i]

        def sbank(i):
            return PS[:, 2048 + 512 * i:2560 + 512 * i]

        main_free = [None, None]
        main_at = [0]
        sides = []

        def pump():
            before = at[0]
            for g, stream in list(sides):
                at[0] = stream
                try:
                    next(g)
                except StopIteration:
                    sides.remove((g, stream))
            at[0] = before

        def finish(g):
            while any(g is h for h, _ in sides):
                pump()

        used = [0]
        released = []
        raw_free = []
        spl_of, spl_read = [], []
        part_tok = []

        arrived = []
        wall_at = [0]

        def fetch():
            while len(arrived) < len(chunks):
                c = len(arrived)
                before = None
                if c >= NRAW:
                    if len(raw_free) <= c - NRAW or raw_free[c - NRAW] is None:
                        return
                    before = raw_free[c - NRAW]
                m, off = chunks[c][3] * chunks[c][5], wall_at[0]
                arrived.append(dma(sy, W[:, c % NRAW, 0:m], wall[off:off + 128 * m].rearrange("(p f) -> p f", p=128),
                                   s_slot[c % NRAW], 16 * (c // NRAW + 1), before))
                wall_at[0] += 128 * m

        fetch()
        dma(sy, TB[:, NH:], tab[:, NH:], s_tab, 16)
        tabt = dma(sy, POSI[:, 0:2], pos_d, s_tab, 32)

        def prep():
            c = len(part_tok)
            if c >= len(chunks):
                return
            name, l, k0, nk, c0, n = chunks[c]
            if name not in SPLIT:
                part_tok.append([arrived[c]])
                spl_of.append(None)
                raw_free.append(None)
                return
            s, m = len(spl_read), nk * n
            sl = s % NSPL
            before = released[spl_read[s - NSPL]] if s >= NSPL else None
            spl_read.append(c)
            spl_of.append(sl)
            raw, wh, wl = W[:, c % NRAW, 0:m], WH[:, sl, 0:m], WL[:, sl, 0:m]
            a = ac.op(lambda e: e.activation(wh, raw, ACT.Copy), arrived[c], before, free=True, stream="prep",
                      cost=45 + m / 1.2)
            b = dv.op(lambda e: e.tensor_tensor(wl, raw, wh.bitcast(F32), ALU.subtract), a, free=True, stream="prep",
                      cost=60 + m / 0.96)
            part_tok.append([a, b])
            raw_free.append(b)
            fetch()

        def split(hi, lo, src, *toks):
            a = act(hi, src, ACT.Copy, *toks)
            b = tt(lo, src, hi.bitcast(F32), ALU.subtract, a)
            return [a, b]

        def use(c, t):
            used[0] += 1
            released.append(t)
            if raw_free[c] is None:
                raw_free[c] = t
                fetch()
            prep()

        class Group:

            def __init__(self, src, src_toks, ncols, mode, nk):
                self.i = main_at[0] % 2
                main_at[0] += 1
                self.bank = [PS[:, 1024 * self.i + 512 * b:1024 * self.i + 512 * b + 512] for b in range(2)]
                self.free = main_free[self.i]
                self.src, self.src_toks, self.ncols, self.mode, self.nk, self.done = src, src_toks, ncols, mode, nk, 0

            def feed(self, kts=None, col=0, last_use=True, stride=None):
                c = used[0]
                name, l, k0, nk, c0, n = chunks[c]
                shape = lambda v: v.rearrange("p (k n) -> p k n", k=nk)
                if name in SPLIT:
                    hi, lo = shape(WH[:, spl_of[c], 0:nk * n]), shape(WL[:, spl_of[c], 0:nk * n])
                else:
                    raw = shape(W[:, c % NRAW, 0:nk * n])
                lead = [part_tok[c], self.free]
                kts = range(k0, k0 + nk) if kts is None else kts
                for kl, kt in enumerate(kts):
                    tok = self.src_toks(kt)
                    x = self.src(kt)
                    passes = ((lo, x[0]), (hi, x[1]), (hi, x[0])) if name in SPLIT else ((raw, x),)
                    for n_p, (w, s) in enumerate(passes):
                        first = self.done == 0 and n_p == 0
                        last = self.done == self.nk - 1 and n_p == len(passes) - 1
                        end = kl == nk - 1 and n_p == len(passes) - 1
                        if self.mode == "cm":
                            m = self.ncols // 128
                            for j in range(m):
                                t = mm(self.bank[j // 2][:, 256 * (j % 2):256 * (j % 2) + 256],
                                       w[:, kl, col + 128 * j:col + 128 * j + 128], s, tok, lead,
                                       start=first and j % 2 == 0, stop=last, inc=end and j == m - 1)
                        elif self.mode == "cm+":
                            for j in range(2):
                                mm(self.bank[0][:, 256 * j:256 * j + 256], w[:, kl, 128 * j:128 * j + 128], s, tok, lead,
                                   start=first and j == 0, stop=last)
                            for j in range(2):
                                t = mm(self.bank[1][:, 16 * j:16 * j + 12], s[:, 128 * j:128 * j + 128],
                                       w[:, kl, 256:268], tok, lead, start=first and j == 0, stop=last, inc=end and j == 1)
                        else:
                            for j in range(2):
                                t = mm(self.bank[j][:, 0:self.ncols], s[:, 128 * j:128 * j + 128],
                                       w[:, kl, col:col + self.ncols], tok, lead, start=first, stop=last,
                                       inc=end and j == 1)
                    self.done += 1
                self.tok = t
                if last_use:
                    use(c, t)
                pump()

            def all(self):
                while self.done < self.nk:
                    self.feed()
                return self

            def free_with(self, toks):
                main_free[self.i] = toks

        def from_h(kt):
            return HH[:, kt, :], HL[:, kt, :]

        h_tok = [None] * 16

        def ht(kt):
            return h_tok[kt]

        def proj(ncols, mode="cm", nk=16):
            return Group(from_h, ht, ncols, mode, nk).all()

        h_read = [None]

        DIAG = SM[:, 704:960].rearrange("p (t c) -> p t c", t=2)
        diag_rd = [None]

        def sumsq(g, tok, scratch, v=None):
            if g == 3:
                lnexp()
            v = X if v is None else v
            for t in range(2):
                r = act(scratch, v[:, t, 512 * g:512 * g + 512], ACT.Square, tok,
                        accum_out=SM[:, 4 * t + g:4 * t + g + 1])
            return r

        def rstd_of(ssum, n, o, tok, table=True):
            if table:
                lnexp()
            a = act(o, ssum, ACT.Ln, tok, head_tok[0], scale=1.0 / n, bias=tb("eps"))
            return act(o, o, ACT.Exp, a, scale=-0.5, bias=0.0)

        def norm_to_h(gname, l, ss_tok):
            a = dop(SM[:, 8:10], lambda e: e.tensor_reduce(SM[:, 8:10], SM[:, 0:8].rearrange("p (t g) -> p t g", t=2),
                                                           AX.X, ALU.add), ss_tok)
            r = rstd_of(SM[:, 8:10], 2048, SM[:, 10:12], a, table=False)
            for t in range(2):
                dg = ts(DIAG[:, t, :], ident, SM[:, 10 + t:11 + t], None, ALU.mult, None, r, head_tok[0], diag_rd[0])
            off = AT[gname] + 16 * l
            at[0] = "side"
            for k in range(0, 16, 2):
                i, fr = side()
                for j in range(2):
                    for t in range(2):
                        c = 128 * (k + j)
                        p = mm(sbank(i)[:, 256 * j + 128 * t:256 * j + 128 * t + 128], X[:, t, c:c + 128],
                               DIAG[:, t, :], fr, x_tok[k // 4], dg, start=(j == 0 and t == 0),
                               inc=(j == 1 and t == 1))
                for j in range(2):
                    g_ap = TB[:, off + k + j:off + k + j + 1]
                    src = sbank(i)[:, 256 * j:256 * j + 256]
                    hh, hl = HH[:, k + j, :], HL[:, k + j, :]
                    t0 = act(hh, src, ACT.Copy, p, h_read[0], t1 if j else None, scale=g_ap)
                    t1 = stt(hl, src, g_ap, hh.bitcast(F32), ALU.mult, ALU.subtract, t0)
                    h_tok[k + j] = [t0, t1]
                side_free[i] = t1
            diag_rd[0] = p
            at[0] = "main"
            head_tok[0] = tabt
            return [t0, t1]

        ROPE = SM[:, 64:64 + 32]
        sin_t = ROPE[:, 0:16].rearrange("p (t c) -> p t c", t=2)
        cos_t = ROPE[:, 16:32].rearrange("p (t c) -> p t c", t=2)

        def rope_tables():
            posf = SM[:, 12:14]
            ang = SM[:, 16:32]
            kk = SM[:, 32:48]
            a = dop0(lambda e: e.tensor_copy(posf, POSI[:, 0:2]), tabt)
            for t in range(2):
                b = ts(ang[:, 8 * t:8 * t + 8], tbl("invf", 8), posf[:, t:t + 1], None, ALU.mult, None, a)
            C1, C2 = 6.28125, float(np.float32(2 * np.pi - 6.28125))
            C3 = float(np.float32(2 * np.pi - 6.28125 - float(np.float32(2 * np.pi - 6.28125))))
            MAGIC = 12582912.0
            lim = 3.1415925
            for shift, add, dst in ((0.0, 0.0, ROPE[:, 0:16]), (0.25, float(np.float32(np.pi / 2)), ROPE[:, 16:32])):
                b = ts(kk, ang, float(1 / (2 * np.pi)), shift, ALU.mult, ALU.add, b)
                b = ts(kk, kk, MAGIC, None, ALU.add, None, b)
                b = ts(kk, kk, -MAGIC, None, ALU.add, None, b)
                b = stt(dst, kk, -C1, ang, ALU.mult, ALU.add, b)
                b = stt(dst, kk, -C2, dst, ALU.mult, ALU.add, b)
                b = stt(dst, kk, -C3, dst, ALU.mult, ALU.add, b)
                b = ts(dst, dst, add, lim, ALU.add, ALU.min, b)
                b = ts(dst, dst, -lim, None, ALU.max, None, b)
            return act(ROPE, ROPE, ACT.Sin, b)

        def softplus(o, x, s, n, tok):
            e_, z, q = s[:, 0:n], s[:, n:2 * n], s[:, 2 * n:3 * n]
            a = act(e_, x, ACT.Abs, tok)
            a = act(e_, e_, ACT.Exp, a, scale=-1.0, bias=0.0)
            a = ts(z, e_, 2.0, None, ALU.add, None, a)
            a = dop0(lambda e: e.reciprocal(z, z), a)
            a = tt(z, z, e_, ALU.mult, a)
            a = tt(q, z, z, ALU.mult, a)
            a = ts(e_, q, 1.0 / 17, None, ALU.mult, None, a)
            for k in (15, 13, 11, 9, 7, 5, 3):
                a = stt(e_, e_, 1.0 / k, q, ALU.add, ALU.mult, a)
            a = stt(e_, e_, 1.0, z, ALU.add, ALU.mult, a)
            a = ts(e_, e_, 2.0, None, ALU.mult, None, a)
            return stt(o, x, 0.0, e_, ALU.max, ALU.add, a)

        RAW = sc(0, 18 * 259).rearrange("p (i c) -> p i c", i=18)
        CT = sc(4662, 4608).rearrange("p (i c) -> p i c", i=18)
        CQ, CK, CV = sc(4662, 1536), sc(4662 + 1536, 1536), sc(4662 + 3072, 1536)
        o0 = 4662 + 4608
        KB, EG, DS, DI, KD = (sc(o0, 1536), sc(o0 + 1536, 1536), sc(o0 + 3072, 1536), sc(o0 + 4608, 1536),
                              sc(o0 + 6144, 1536))
        SS, VN = CK, KB[:, 0:768]
        UU, TT_, XX = sc(0, 1536), sc(1536, 1536), sc(3072, 1536)
        RV, RW, U2, WT, OC = KB, CV, TT_, XX, DS

        def heads(ap):
            return ap.rearrange("p (h t c) -> p h t c", h=6, t=2)

        gs = SM[:, 128:512]
        c_free = [None]

        def delta_net(l, silu_tok, ba_tok, ba_bank_free):
            bt = gs[:, 0:12].rearrange("p (h t) -> p h t", h=6)
            gg = gs[:, 12:24].rearrange("p (h t) -> p h t", h=6)
            ea = gs[:, 24:30]
            gcs, gls = gs[:, 36:48], gs[:, 48:60]
            bw, kdw = gs[:, 60:72], gs[:, 72:84]
            th = gs[:, 84:96]
            a = act(th, gs[:, 120:132], ACT.Tanh, ba_tok, scale=0.5, bias=0.0)
            b1 = ts(gs[:, 0:12], th, 0.5, 0.5, ALU.mult, ALU.add, a)
            e1 = act(ea, row("c_a_log", l), ACT.Exp, tabt, scale=1.0, bias=0.0)
            a = tt(gs[:, 132:144].rearrange("p (h t) -> p h t", h=6), gs[:, 132:144].rearrange("p (h t) -> p h t", h=6),
                   row("c_dt_bias", l).unsqueeze(2).to_broadcast([128, 6, 2]), ALU.add, ba_tok)
            a = softplus(gs[:, 12:24], gs[:, 132:144], gs[:, 144:180], 12, a)
            a = ts(gs[:, 12:24], gs[:, 12:24], -1.0, None, ALU.mult, None, a)
            g_t = tt(gg, gg, ea.unsqueeze(2).to_broadcast([128, 6, 2]), ALU.mult, a, e1)
            sq = sc(0, 3072)
            q1 = act(sq, sc(4662, 3072), ACT.Square, silu_tok)
            yield
            yield
            i, fr = side()
            b = sbank(i)
            mm(b[:, 0:12], tbl("cum"), gs[:, 12:24], g_t, fr)
            p = mm(b[:, 16:28], tbl("last"), gs[:, 12:24], start=False, inc=True)
            a = dop0(lambda e: e.tensor_copy(gs[:, 36:60].rearrange("p (a c) -> p a c", a=2),
                                              b[:, 0:32].rearrange("p (a c) -> p a c", a=2)[:, :, 0:12]), p)
            side_free[i] = a
            gc_t = a
            a1 = act(bw, gcs, ACT.Exp, a, scale=1.0, bias=0.0)
            bw_t = tt(bw, bw, gs[:, 0:12], ALU.mult, a1, b1)
            a2 = tt(kdw, gls, gcs, ALU.subtract, a)
            kd_t = act(kdw, kdw, ACT.Exp, a2, scale=1.0, bias=0.0)
            dsts = []
            for bk in range(3):
                i, fr = side()
                bnk = sbank(i)
                for j in range(4):
                    u = 4 * bk + j
                    p = mm(bnk[:, 128 * j:128 * j + 128], gs[:, 12 + u:13 + u].to_broadcast([128, 128]), tbl("cum"),
                           g_t, fr, start=(j == 0), inc=(j == 3))
                cs = slice(512 * bk, 512 * bk + 512)
                for j in range(4):
                    u = 4 * bk + j
                    d1 = ts(DI[:, 128 * u:128 * u + 128], bnk[:, 128 * j:128 * j + 128], gcs[:, u:u + 1], 0.0,
                            ALU.subtract, ALU.min, p, gc_t, c_free[0])
                e2 = act(EG[:, cs], bnk, ACT.Exp, p, d1, c_free[0], scale=1.0, bias=0.0)
                e3 = act(DI[:, cs], DI[:, cs], ACT.Exp, d1, scale=1.0, bias=0.0)
                side_free[i] = [d1, e2]
                dsts.append((e2, e3))
            eg_t, di_t = dsts[-1]
            yield
            lnexp()
            rn = sc(0, 3072)
            rt = []
            for k in range(6):
                i, fr = side()
                p = mm(sbank(i), ones, sq[:, 512 * k:512 * k + 512], q1, fr, inc=True)
                a = act(rn[:, 512 * k:512 * k + 512], sbank(i), ACT.Ln, p, scale=1.0, bias=tb("eps"))
                side_free[i] = a
                rt.append(a)
            a = act(rn, rn, ACT.Exp, a, scale=-0.5, bias=0.0)
            q_t = stt(CQ, CQ, float(128 ** -0.5), rn[:, 0:1536], ALU.mult, ALU.mult, a)
            k_t = tt(CK, CK, rn[:, 1536:3072], ALU.mult, a)
            yield
            for bk in range(3):
                i, fr = side()
                bnk = sbank(i)
                for j in range(4):
                    u = 4 * bk + j
                    p = mm(bnk[:, 128 * j:128 * j + 128], gs[:, u:u + 1].to_broadcast([128, 128]), ident,
                           b1, fr, start=(j == 0), inc=(j == 3))
                cs = slice(512 * bk, 512 * bk + 512)
                kb_t = tt(KB[:, cs], CK[:, cs], bnk, ALU.mult, p, k_t)
                side_free[i] = kb_t
            ds_t = tt(DS.rearrange("p (u c) -> p u c", u=12), DI.rearrange("p (u c) -> p u c", u=12),
                      tbl("strict").unsqueeze(1).to_broadcast([128, 12, 128]), ALU.mult, di_t)
            dm_t = tt(DI.rearrange("p (u c) -> p u c", u=12), DI.rearrange("p (u c) -> p u c", u=12),
                      tbl("incl").unsqueeze(1).to_broadcast([128, 12, 128]), ALU.mult, ds_t)
            yield
            for bk in range(3):
                cs = slice(512 * bk, 512 * bk + 512)
                for dst, rhs_, tok in ((DS, KB, kb_t), (DI, CQ, q_t)):
                    i, fr = side()
                    bnk = sbank(i)
                    for j in range(4):
                        u = 4 * bk + j
                        us = slice(128 * u, 128 * u + 128)
                        p = mm(bnk[:, 128 * j:128 * j + 128], CK[:, us], rhs_[:, us], k_t, tok, fr, start=(j == 0),
                               inc=(j == 3))
                    a = tt(dst[:, cs], bnk, dst[:, cs], ALU.mult, p, ds_t, dm_t)
                    side_free[i] = a
                    if dst is DS:
                        v3 = UU[:, cs].rearrange("p (u c) -> p u c", u=4)
                        b_ = tt(v3, DS[:, cs].rearrange("p (u c) -> p u c", u=4),
                                tbl("lv2").unsqueeze(1).to_broadcast([128, 4, 128]), ALU.mult, a, k_t, q_t)
                        u_t = tt(v3, v3, ident.unsqueeze(1).to_broadcast([128, 4, 128]), ALU.add, b_)
                        ns_t = a
                    else:
                        in_t = a
            yield
            for bk in range(3):
                i, fr = side()
                bnk = sbank(i)
                cs = slice(512 * bk, 512 * bk + 512)
                for j in range(4):
                    u = 4 * bk + j
                    p = tp(bnk[:, 128 * j:128 * j + 128], UU[:, 128 * u:128 * u + 128], u_t, fr, inc=(j == 3))
                t_t = act(TT_[:, cs], bnk, ACT.Copy, p, q_t, k_t)
                side_free[i] = t_t
            lastk = None
            for src, which in ((CV, "v"), (CK, "k")):
                for bk in range(3):
                    i, fr = side()
                    bnk = sbank(i)
                    cs = slice(512 * bk, 512 * bk + 512)
                    for j in range(4):
                        u = 4 * bk + j
                        p = tp(bnk[:, 128 * j:128 * j + 128], src[:, 128 * u:128 * u + 128], fr, silu_tok, k_t,
                               inc=(j == 3))
                    b3 = bnk.rearrange("p (u c) -> p u c", u=4)

                    def per(v):
                        return v[:, 4 * bk:4 * bk + 4].unsqueeze(2).to_broadcast([128, 4, 128])
                    r3 = lambda v: v[:, cs].rearrange("p (u c) -> p u c", u=4)
                    if which == "v":
                        a = tt(r3(RV), b3, per(gs[:, 0:12]), ALU.mult, p, b1, ns_t, in_t)
                        side_free[i] = a
                        vtp = p
                        rv_t = a
                    else:
                        a = tt(r3(RW), b3, per(bw), ALU.mult, p, bw_t, vtp)
                        a2 = tt(r3(KD), b3, per(kdw), ALU.mult, kd_t, c_free[0])
                        side_free[i] = [a, a2]
                        rw_t, kdt = a, a2
            qg_t = tt(CQ, CQ, EG, ALU.mult, eg_t, in_t)
            yield
            for m in (4, 8, 16, 32, 64):
                for bk in range(3):
                    i, fr = side()
                    bnk = sbank(i)
                    cs = slice(512 * bk, 512 * bk + 512)
                    for j in range(4):
                        u = 4 * bk + j
                        us = slice(128 * u, 128 * u + 128)
                        p = mm(bnk[:, 128 * j:128 * j + 128], DS[:, us], TT_[:, us], t_t, ns_t, fr, start=(j == 0),
                               inc=(j == 3))
                    a = tt(XX[:, cs].rearrange("p (u c) -> p u c", u=4), bnk.rearrange("p (u c) -> p u c", u=4),
                           tbl(f"lv{m}").unsqueeze(1).to_broadcast([128, 4, 128]), ALU.mult, p, u_t)
                    side_free[i] = a
                    x_t = a
                yield
                ups = []
                for bk in range(3):
                    cs = slice(512 * bk, 512 * bk + 512)
                    for which in (0, 1) if m < 64 else (0,):
                        i, fr = side()
                        bnk = sbank(i)
                        for j in range(4):
                            u = 4 * bk + j
                            us = slice(128 * u, 128 * u + 128)
                            l_, r_ = (XX[:, us], UU[:, us]) if which == 0 else (UU[:, us], XX[:, us])
                            p = mm(bnk[:, 128 * j:128 * j + 128], l_, r_, x_t, u_t, fr, start=(j == 0), inc=(j == 3))
                        ups.append((which, cs, bnk, i))
                    for which, cs2, bnk, i in ups:
                        dst = UU if which == 0 else TT_
                        a = tt(dst[:, cs2], dst[:, cs2], bnk, ALU.add, p)
                        side_free[i] = a
                        if which == 0:
                            u_t2 = a
                        else:
                            t_t = a
                    ups = []
                u_t = u_t2
                yield
            for bk in range(3):
                cs = slice(512 * bk, 512 * bk + 512)
                for which in (0, 1):
                    i, fr = side()
                    bnk = sbank(i)
                    for j in range(4):
                        u = 4 * bk + j
                        us = slice(128 * u, 128 * u + 128)
                        l_, r_ = (UU[:, us], RV[:, us]) if which == 0 else (RW[:, us], UU[:, us])
                        p = mm(bnk[:, 128 * j:128 * j + 128], l_, r_, u_t, rv_t, rw_t, fr, start=(j == 0),
                               inc=(j == 3))
                    dst = (U2, WT)[which]
                    a = act(dst[:, cs], bnk, ACT.Copy, p, u_t, t_t)
                    side_free[i] = a
                    uw_t = a
            s_t = dop0(lambda e: e.memset(SS[:, 0:768], 0.0), u_t, uw_t)
            yield
            EG4 = EG.rearrange("p (h t) -> p h t", h=6)
            o_rd = [None, None]
            for c in range(4):
                half, p0 = c // 2, 64 * (c % 2)
                S = SS[:, 768 * (c % 2):768 * (c % 2) + 768]
                S2 = SS[:, 768 * ((c + 1) % 2):768 * ((c + 1) % 2) + 768]
                (i1, f1), (i2, f2) = side(), side()
                for h in range(6):
                    bnk = sbank(i1) if h < 4 else sbank(i2)
                    hh = h % 4
                    us = 256 * h + 128 * half + p0
                    p = mm(bnk[p0:p0 + 64, 128 * hh:128 * hh + 128], WT[:, us:us + 64], S[:, 128 * h:128 * h + 128],
                           s_t, uw_t, f1, f2, start=(hh == 0), inc=(h in (3, 5)))
                for n_, i_, h0, nh in ((0, i1, 0, 4), (1, i2, 4, 2)):
                    v_t = tt(VN[p0:p0 + 64, 128 * h0:128 * (h0 + nh)].rearrange("p (h c) -> p h c", h=nh),
                             heads(U2)[p0:p0 + 64, h0:h0 + nh, half, :],
                             sbank(i_)[p0:p0 + 64, 0:128 * nh].rearrange("p (h c) -> p h c", h=nh),
                             ALU.subtract, p, uw_t, o_rd[c % 2])
                    side_free[i_] = v_t
                yield
                if c < 3:
                    (i1, f1), (i2, f2) = side(), side()
                    for h in range(6):
                        bnk = sbank(i1) if h < 4 else sbank(i2)
                        hh = h % 4
                        us = 256 * h + 128 * half
                        p = mm(bnk[:, 128 * hh:128 * hh + 128], KD[p0:p0 + 64, us:us + 128],
                               VN[p0:p0 + 64, 128 * h:128 * h + 128], v_t, kdt, f1, f2, start=(hh == 0),
                               inc=(h in (3, 5)))
                    for h in range(6):
                        i_ = i1 if h < 4 else i2
                        hh = h % 4
                        s_n = stt(S2[:, 128 * h:128 * h + 128], S[:, 128 * h:128 * h + 128],
                                  EG4[:, h, 64 * c + 63:64 * c + 64], sbank(i_)[:, 128 * hh:128 * hh + 128],
                                  ALU.mult, ALU.add, p, o_rd[(c + 1) % 2], eg_t)
                        side_free[i_] = s_n
                i, fr = side()
                for h in range(6):
                    ob = sbank(i)[:, 64 * h:64 * h + 64]
                    cs = slice(256 * h + 64 * c, 256 * h + 64 * c + 64)
                    mm(ob, S[:, 128 * h:128 * h + 128], CQ[:, cs], fr, qg_t, start=(h == 0), stop=False)
                    u0 = 256 * h + 128 * half + p0
                    p = mm(ob, VN[p0:p0 + 64, 128 * h:128 * h + 128], DI[p0:p0 + 64, u0:u0 + 64], v_t, in_t,
                           start=False, inc=(h == 5))
                o_t = act(OC.rearrange("p (h t) -> p h t", h=6)[:, :, 64 * c:64 * c + 64],
                          sbank(i)[:, 0:384].rearrange("p (h t) -> p h t", h=6), ACT.Copy, p, u_t)
                side_free[i] = o_t
                o_rd[c % 2] = p
                if c < 3:
                    s_t = s_n
                yield
            low_free[0], mid_free[0] = v_t, o_rd[:]
            a = act(DI, OC, ACT.Square, o_t, o_rd[:])
            yield
            lnexp()
            for k in range(3):
                i, fr = side()
                p = mm(sbank(i), ones, DI[:, 512 * k:512 * k + 512], a, fr, inc=True)
                r = act(KD[:, 512 * k:512 * k + 512], sbank(i), ACT.Ln, p, scale=1.0 / 128, bias=tb("eps"))
                side_free[i] = r
            r = act(KD, KD, ACT.Exp, r, scale=-0.5, bias=0.0)
            a = stt(OC, OC, TB[:, AT["c_onorm_w"] + l:AT["c_onorm_w"] + l + 1], KD, ALU.mult, ALU.mult, r)
            yc = Y[:, 10:16, :].rearrange("p i c -> p (i c)")
            c_done[0] = tt(yc, yc, OC, ALU.mult, a, zc_tok[0])

        low_free, mid_free = [None], [None]
        c_done, zc_tok, zb_tok, za_tok, b_ready, a_done = [None], [None], [None], [None], [None], [None]

        def conformer(l, hb, acc, tmp, h_t):
            wo = AT["b_conv_w"] + 124 * l
            av = acc.rearrange("p (m c) -> p m c", m=4)
            last = [None] * 4
            for k in range(31):
                for m in range(4):
                    wk = TB[:, wo + 4 * k + m:wo + 4 * k + m + 1]
                    if k == 0:
                        last[m] = ts(av[:, m, :], hb[:, m, 0:256], wk, tb("b_conv_b", 4 * l + m), ALU.mult, ALU.add,
                                     h_t)
                    else:
                        last[m] = stt(av[:, m, :], hb[:, m, k:k + 256], wk, av[:, m, :], ALU.mult, ALU.add, last[m])
                if k % 8 == 7:
                    yield
            yield
            i, fr = side()
            for m in range(4):
                p = mm(sbank(i)[:, 0:256], ones, av[:, m, :], last[m], fr, start=(m == 0), stop=(m == 3),
                       inc=(m == 3))
            a = stt(av, sbank(i)[:, 0:256].unsqueeze(1).to_broadcast([128, 4, 256]), -1.0 / 512, av,
                    ALU.mult, ALU.add, p)
            side_free[i] = a
            c_t = a
            a = act(tmp, acc, ACT.Square, a)
            yield
            i, fr = side()
            tv = tmp.rearrange("p (m c) -> p m c", m=4)
            for m in range(4):
                p = mm(sbank(i)[:, 0:256], ones, tv[:, m, :], a, fr, start=(m == 0), stop=(m == 3), inc=(m == 3))
            rs = tmp[:, 0:256]
            lnexp()
            r = act(rs, sbank(i)[:, 0:256], ACT.Ln, p, scale=1.0 / 512, bias=tb("eps"))
            side_free[i] = r
            r = act(rs, rs, ACT.Exp, r, scale=-0.5, bias=0.0)
            a = tt(av, av, rs.unsqueeze(1).to_broadcast([128, 4, 256]), ALU.mult, r, c_t)
            for m in range(4):
                r = act(av[:, m, :], av[:, m, :], ACT.Silu, a, scale=tb("b_ln_w", 4 * l + m),
                        bias=tb("b_ln_b", 4 * l + m))
            b_ready[0] = r

        QK = sc(0, 2048)
        KR = sc(2048, 1024)
        AV = sc(3072, 512)
        QT = sc(3584, 1536)
        KT2 = sc(5120, 1024)
        AP_ = sc(6144, 4608)
        AS = sc(10752, 4608)
        SQ = sc(5120, 2048)

        def attention(l, qk_t, v_t):
            qk3 = QK.rearrange("p (n d) -> p n d", d=64)
            sm = SM[:, 512:640]
            a = act(SQ, QK, ACT.Square, qk_t)
            a = dop0(lambda e: e.tensor_reduce(sm[:, 0:32], SQ.rearrange("p (n d) -> p n d", d=64), AX.X, ALU.add), a)
            a = rstd_of(sm[:, 0:32], 64, sm[:, 0:32], a)
            a = tt(qk3, qk3, sm[:, 0:32].unsqueeze(2).to_broadcast([128, 32, 64]), ALU.mult, a)
            for t in range(2):
                for n0, n1, wn in ((0, 12, "q_norm_w"), (12, 16, "k_norm_w")):
                    v = qk3[:, 16 * t + n0:16 * t + n1, :]
                    b = tt(v, v, row(wn, l).unsqueeze(1).to_broadcast([128, n1 - n0, 64]), ALU.mult, a)
            q4 = QK.rearrange("p (t n d) -> p t n d", t=2, n=16)
            x1, x2 = q4[:, :, :, 0:8], q4[:, :, :, 8:16]
            cb = cos_t.unsqueeze(2).to_broadcast([128, 2, 16, 8])
            sb_ = sin_t.unsqueeze(2).to_broadcast([128, 2, 16, 8])
            r4 = [SQ[:, 256 * i:256 * i + 256].rearrange("p (t n d) -> p t n d", t=2, n=16) for i in range(4)]
            tt(r4[0], x1, cb, ALU.mult, b, rope_tok[0])
            tt(r4[1], x2, sb_, ALU.mult)
            tt(r4[2], x2, cb, ALU.mult)
            c = tt(r4[3], x1, sb_, ALU.mult)
            tt(x1, r4[0], r4[1], ALU.subtract, c)
            c = tt(x2, r4[2], r4[3], ALU.add)
            kr = KR.rearrange("p (t n r d) -> p t n r d", t=2, n=4, r=2)
            for t in range(2):
                d = dop0(lambda e, t=t: e.tensor_copy(kr[:, t], q4[:, t, 12:16, :].unsqueeze(2).to_broadcast(
                    [128, 4, 2, 64])), c)
            yield
            yield
            qt = QT.rearrange("p (i t) -> p i t", i=6)
            kt2 = KT2.rearrange("p (i t) -> p i t", i=4)
            for bk in range(5):
                i, fr = side()
                for j in range(2):
                    n = 2 * bk + j
                    for t in range(2):
                        src = q4[:, t, 2 * n:2 * n + 2, :].rearrange("p a d -> p (a d)") if n < 6 else \
                            kr[:, t, n - 6, :, :].rearrange("p r d -> p (r d)")
                        p = tp(sbank(i)[:, 256 * j + 128 * t:256 * j + 128 * t + 128], src, d, fr,
                               inc=(j == 1 and t == 1))
                dst = QT[:, 512 * bk:512 * bk + 512] if bk < 3 else KT2[:, 512 * (bk - 3):512 * (bk - 3) + 512]
                a = act(dst, sbank(i), ACT.Copy, p)
                side_free[i] = a
            yield
            s3 = AS.rearrange("p (h c) -> p h c", h=12)
            p3 = AP_.rearrange("p (h c) -> p h c", h=12)
            m2 = sm[:, 32:56].rearrange("p (b h) -> p b h", b=2)
            nm = sm[:, 56:80].rearrange("p (b h) -> p b h", b=2)
            den = sm[:, 80:104].rearrange("p (b h) -> p b h", b=2)
            es = sm[:, 104:128].rearrange("p (b h) -> p b h", b=2)
            wt = {}

            def scores(q):
                hs = slice(4 * q, 4 * q + 4)
                for h in range(4 * q, 4 * q + 4):
                    i, fr = side()
                    b0 = 64 * (h % 2)
                    mm(sbank(i)[:, 0:128], qt[b0:b0 + 64, h // 2, 0:128], kt2[b0:b0 + 64, h // 3, 0:128], qk_done, fr)
                    p = mm(sbank(i)[:, 128:384], qt[b0:b0 + 64, h // 2, 128:256], kt2[b0:b0 + 64, h // 3, 0:256],
                           start=False, inc=True)
                    s_t = stt(s3[:, h, :], sbank(i)[:, 0:384], 0.125, tbl("amask", 384), ALU.mult, ALU.add, p,
                              c_done[0])
                    side_free[i] = s_t
                for b_, (c0, c1) in enumerate(((0, 128), (128, 384))):
                    a = dop(s3[:, hs, c0:c1].rearrange("p h c -> p c h"),
                            lambda e, b_=b_, c0=c0, c1=c1: e.tensor_reduce(m2[:, b_, hs], s3[:, hs, c0:c1], AX.X,
                                                                           ALU.max), s_t)
                sk = row("sinks", l)[:, hs].unsqueeze(1).to_broadcast([128, 2, 4])
                a = tt(m2[:, :, hs], m2[:, :, hs], sk, ALU.max, a)
                a = ts(nm[:, :, hs], m2[:, :, hs], -1.0, None, ALU.mult, None, a)
                e0 = tt(es[:, :, hs], sk, m2[:, :, hs], ALU.subtract)
                for h in range(4 * q, 4 * q + 4):
                    for b_, (c0, c1) in enumerate(((0, 128), (128, 384))):
                        k = 12 * b_ + h
                        e1 = act(p3[:, h, c0:c1], s3[:, h, c0:c1], ACT.Exp, a, bias=sm[:, 56 + k:57 + k],
                                 scale=1.0, accum_out=sm[:, 80 + k:81 + k])
                return act(es[:, :, hs], es[:, :, hs], ACT.Exp, e0, scale=1.0, bias=0.0)

            def turned(q, e_t):
                hs = slice(4 * q, 4 * q + 4)
                a = tt(den[:, :, hs], den[:, :, hs], es[:, :, hs], ALU.add, e_t)
                a = dop(den[:, :, hs], lambda e: e.reciprocal(den[:, :, hs], den[:, :, hs]), a)
                for b_, (c0, c1) in enumerate(((0, 128), (128, 384))):
                    v = p3[:, hs, c0:c1]
                    a = tt(v, v, den[:, b_, hs].unsqueeze(2).to_broadcast([128, 4, c1 - c0]), ALU.mult)
                for n in range(3 * q, 3 * q + 3):
                    i, fr = side()
                    for j in range(4):
                        u = 4 * n + j
                        p = tp(sbank(i)[:, 128 * j:128 * j + 128], AP_[:, 128 * u:128 * u + 128], a, fr, inc=(j == 3))
                    dst = AS[:, 512 * n:512 * n + 512]
                    if n % 2:
                        wt[1] = act(dst, sbank(i), ACT.Copy, p)
                    else:
                        wt[0] = dop(dst, lambda e, i=i, dst=dst: e.tensor_copy(dst, sbank(i)), p)
                    side_free[i] = wt[n % 2]
                return p

            qk_done = a
            e0_ = scores(0)
            yield
            e1_ = scores(1)
            yield
            turned(0, e0_)
            e2_ = scores(2)
            yield
            turned(1, e1_)
            yield
            p = turned(2, e2_)
            wa, wd = wt[1], wt[0]
            x_tok[:] = [pool_dma(X[:, :, :], xsave.rearrange("(t p) c -> p t c", t=2), s_xr, n_xr, p)] * 4
            yield
            av = AV.rearrange("p (t d) -> p t d", t=2)
            for n in range(3):
                i, fr = side()
                for j in range(2):
                    for q in range(2):
                        h = 4 * n + 2 * j + q
                        b0 = 64 * q
                        kv = h // 3
                        o = sbank(i)[b0:b0 + 64, 256 * j:256 * j + 256]
                        vs = slice(64 * kv, 64 * kv + 64)
                        mm(o[:, 0:128], av[:, 0, vs], s3[:, h, 0:128], wa, wd, v_t, fr, start=(j == 0))
                        mm(o[:, 128:256], av[:, 0, vs], s3[:, h, 128:256], start=False, stop=False)
                        p = mm(o[:, 128:256], av[:, 1, vs], s3[:, h, 256:384], start=False,
                               inc=(j == 1 and q == 1))
                ya = Y[:, 2 * n:2 * n + 2, :].rearrange("p i c -> p (i c)")
                a_done[0] = tt(ya, ya, sbank(i), ALU.mult, p, za_tok[0])
                side_free[i] = a_done[0]

        rope_tok = [None]

        for _ in range(NSPL - 1):
            prep()
        sq_scr = sc(0, 512)
        for g in range(4):
            s_tok = sumsq(g, x_tok[g], sq_scr)
        h_all = norm_to_h("norm_w", 0, s_tok)
        rope_tok[0] = rope_tables()
        y_read = [None]
        HB = sc(16950, 1144).rearrange("p (m c) -> p m c", m=4)

        def block1(l, start_free):
            c_free[0] = start_free
            z0 = dop0(lambda e: e.memset(RAW[:, :, 0:3], 0.0), start_free)
            wo = AT["c_conv_w"] + 72 * l
            silus = []

            def conv(i0, n, bank_ap, p):
                e_ = act(RAW[:, i0:i0 + n, 3:259], bank_ap, ACT.Copy, p, start_free)
                return e_

            def conv_taps(i0, n, e_):
                lt = [e_] * n
                for k in range(4):
                    for m in range(n):
                        wk = TB[:, wo + 18 * k + i0 + m:wo + 18 * k + i0 + m + 1]
                        if k == 0:
                            lt[m] = ts(CT[:, i0 + m, :], RAW[:, i0 + m, 0:256], wk, None, ALU.mult, None, e_, z0)
                        else:
                            lt[m] = stt(CT[:, i0 + m, :], RAW[:, i0 + m, k:k + 256], wk, CT[:, i0 + m, :],
                                        ALU.mult, ALU.add, lt[m])
                return act(CT[:, i0:i0 + n, :], CT[:, i0:i0 + n, :], ACT.Silu, lt[-1])

            pend = None
            for i in range(5):
                g = proj(512) if i < 4 else proj(256, mode="cm+")
                es = [conv(4 * i + 2 * b, 2, g.bank[b].rearrange("p (a c) -> p a c", a=2), g.tok)
                      for b in range(2 if i < 4 else 1)]
                if i == 4:
                    src = g.bank[1][:, 0:32].rearrange("p (t c) -> p t c", t=2)
                    q1 = dop0(lambda e: e.tensor_copy(gs[:, 120:132].rearrange("p (h t) -> p h t", h=6),
                                                       src[:, :, 0:6].rearrange("p t h -> p h t")), g.tok, start_free)
                    q2 = dop0(lambda e: e.tensor_copy(gs[:, 132:144].rearrange("p (h t) -> p h t", h=6),
                                                       src[:, :, 6:12].rearrange("p t h -> p h t")), g.tok)
                    g.free_with([es[-1], q2])
                    ba = [q1, q2]
                else:
                    g.free_with(es[-1])
                si = conv_taps(4 * i, 4 if i < 4 else 2, es[-1])
            dn = delta_net(l, si, ba, None)
            sides.append((dn, "side"))
            zt = []
            for n, t0 in ((4, 10), (2, 14)):
                g = proj(128 * n)
                for b in range(n // 2):
                    zc_tok[0] = act(Y[:, t0 + 2 * b:t0 + 2 * b + 2, :], g.bank[b].rearrange("p (a c) -> p a c", a=2),
                                    ACT.Silu, g.tok, y_read[0])
                g.free_with(zc_tok[0])
            hz = dop0(lambda e: e.memset(HB[:, :, 0:30], 0.0), start_free)
            g1 = proj(512)
            for b in range(2):
                ea = act(HB[:, 2 * b:2 * b + 2, 30:286], g1.bank[b].rearrange("p (a c) -> p a c", a=2), ACT.Copy,
                         g1.tok, start_free)
            g1.free_with(ea)
            g2 = proj(512)
            for b in range(2):
                et = act(Y[:, 6 + 2 * b:8 + 2 * b, :], g2.bank[b].rearrange("p (a c) -> p a c", a=2), ACT.Tanh, g2.tok,
                         y_read[0], scale=0.5, bias=0.0)
            g2.free_with(et)
            yb = Y[:, 6:10, :]
            a = ts(yb, yb, 0.5, 0.5, ALU.mult, ALU.add, et)
            hb_t = tt(HB[:, :, 30:286], HB[:, :, 30:286], yb, ALU.mult, a, ea)
            g3 = proj(512)
            for b in range(2):
                zb_tok[0] = act(yb[:, 2 * b:2 * b + 2, :], g3.bank[b].rearrange("p (a c) -> p a c", a=2), ACT.Silu,
                                g3.tok, hb_t)
            g3.free_with(zb_tok[0])
            acc = Y[:, 0:4, :].rearrange("p m c -> p (m c)")
            cf = conformer(l, HB, acc, sc(16950, 1024), [hb_t, hz, y_read[0]])
            sides.append((cf, "conv"))
            finish(dn)
            qv = QK.rearrange("p (t c) -> p t c", t=2)
            for i in range(2):
                g = proj(512, mode="tm")
                for t in range(2):
                    q_t = act(qv[:, t, 512 * i:512 * i + 512], g.bank[t], ACT.Copy, g.tok, low_free[0])
                g.free_with(q_t)
            g = proj(256, mode="tm")
            for t in range(2):
                v_t = act(AV[:, 256 * t:256 * t + 256], g.bank[t][:, 0:256], ACT.Copy, g.tok, low_free[0])
            g.free_with(v_t)
            att = attention(l, [q_t, mid_free[0]], v_t)
            finish(cf)
            sides.append((att, "side"))
            acc = Y[:, 0:4, :]
            g = Group(lambda kt: acc[:, kt, :], lambda kt: b_ready[0], 512, "cm", 4).all()
            b_read = g.tok
            for m in range(4):
                b_t = stt(Y[:, 6 + m, :], g.bank[m // 2][:, 256 * (m % 2):256 * (m % 2) + 256],
                          tb("b_pw_b", 4 * l + m), Y[:, 6 + m, :], ALU.add, ALU.mult, g.tok, zb_tok[0])
            g.free_with(b_t)
            for n, t0 in ((4, 0), (2, 4)):
                g = proj(128 * n)
                for b in range(n // 2):
                    za_tok[0] = act(Y[:, t0 + 2 * b:t0 + 2 * b + 2, :], g.bank[b].rearrange("p (a c) -> p a c", a=2),
                                    ACT.Silu, g.tok, b_read)
                g.free_with(za_tok[0])
            h_read[0] = g.tok
            y_tok = {}

            def ysplit(k, n, tok):
                t = split(HH[:, k:k + n, :], HL[:, k:k + n, :], Y[:, k:k + n, :], tok, h_read[0])
                for j in range(n):
                    y_tok[k + j] = t

            for k in (6, 8):
                ysplit(k, 2, b_t)
            for k in (10, 12, 14):
                ysplit(k, 2, c_done[0])
            mk = lambda: Group(from_h, lambda kt: y_tok[kt], 512, "tm", 16)
            ga, gb = mk(), mk()
            for gg_ in (ga, gb):
                for _ in range(3):
                    gg_.feed()
            finish(att)
            for k in (0, 2, 4):
                ysplit(k, 2, a_done[0])
            for gg_ in (ga, gb):
                gg_.all()

            def add_x(i, g):
                for t in range(2):
                    v = X[:, t, 512 * i:512 * i + 512]
                    x_tok[i] = tt(v, v, g.bank[t], ALU.add, g.tok, x_tok[i])
                g.free_with(x_tok[i])
                return sumsq(i, x_tok[i], sq_scr)

            add_x(0, ga)
            add_x(1, gb)
            add_x(2, mk().all())
            g = mk().all()
            h_read[0] = g.tok
            y_read[0] = y_tok[0]
            return add_x(3, g)

        def save_x():
            return pool_dma(xsave.rearrange("(t p) c -> p t c", t=2), X[:, :, :], s_sp, n_sp, x_tok[3])

        sp = save_x()
        s_tok = block1(0, [h_all, sp])
        sp = save_x()
        free = norm_to_h("norm_w", 1, s_tok)
        s_tok = block1(1, [free, sp])
        free = norm_to_h("g_pre_2", 0, s_tok)

        ZT = Q[:, 8192:10240].rearrange("p (i c) -> p i c", i=8)
        o_tok = [None] * 4

        def out_part(g, y_t, halves=1):
            for hf in range(halves):
                for i in range(4):
                    q = Group(lambda kt: (YH[:, kt - 8 * g, :], YL[:, kt - 8 * g, :]), lambda kt: y_t[kt - 8 * g],
                              512, "tm", 8 // halves).all()
                    cs = slice(512 * i, 512 * i + 512)
                    for t in range(2):
                        o = O[:, t, cs]
                        if g == 0:
                            o_tok[i] = act(o, q.bank[t], ACT.Copy, q.tok, y_read[0])
                        else:
                            o_tok[i] = tt(o, o, q.bank[t], ALU.add, q.tok, o_tok[i])
                    q.free_with(o_tok[i])
                    if g == 3 and hf == halves - 1:
                        os_tok[0] = sumsq(i, o_tok[i], JUNK, O)
                        for t in range(2):
                            o_tok[i] = tt(O[:, t, cs], O[:, t, cs], GP[:, cs], ALU.mult, os_tok[0], post_t["gp"])
            y_read[0] = q.tok

        GP, GL, JUNK = Q[:, 8192:10240], Q[:, 18432:20480], Q[:, 20480:20992]
        PT = Q[:, 21760:22272].rearrange("p (k t) -> p k t", k=2)
        post_t, os_tok = {}, [None]

        def load_pt(l, tok):
            post_t["pt"] = pool_dma(Q[:, 21760:22272], pT_d[:, 512 * l:512 * l + 512], s_pt, n_pt, tok)

        def pre_post(l, free):
            post_t["gp"] = pool_dma(GP, gpost_d[l:l + 1, :].to_broadcast([128, 2048]), s_gp, n_gp, free)
            post_t["gl"] = pool_dma(GL, gplo_d[l:l + 1, :].to_broadcast([128, 2048]), s_g, n_g)
            post_t["free"] = free

        def pool_layer(free):
            U = Q[:, 18432:19520].rearrange("p (i c) -> p i c", i=4)
            A = Q[:, 19520:20608].rearrange("p (i c) -> p i c", i=4)
            B = Q[:, 20608:21696].rearrange("p (i c) -> p i c", i=4)
            for b in (U, A, B):
                z_ = dop0(lambda e, b=b: e.memset(b[:, :, 0:16], 0.0), free)
            u_free, d_free, z_free = [z_], [free], [free]
            d_tok, y_tok = {}, {}

            def load_u(g):
                for i in range(2):
                    q = proj(512)
                    for b in range(2):
                        t = act(U[:, 2 * b:2 * b + 2, 16:272], q.bank[b].rearrange("p (a c) -> p a c", a=2), ACT.Copy,
                                q.tok, u_free[0], free)
                    q.free_with(t)
                    src, k = U, 1
                    tok = t
                    for s in range(g + 1):
                        dst = (A, B)[s % 2]
                        tok = tt(dst[:, :, 16:272], src[:, :, 16:272], src[:, :, 16 - k:272 - k], ALU.add, tok, z_)
                        src, k = dst, 2 * k
                    other = B if src is A else A
                    tok = ts(other[:, :, 16:272], src[:, :, 16:272], 1.0 / k, None, ALU.mult, None, tok)
                    tok = tt(other[:, :, 16:32], src[:, :, 16:32],
                             tbl(f"cnt{g}", 16).unsqueeze(1).to_broadcast([128, 4, 16]), ALU.mult, tok)
                    tok = tt(src[:, :, 16:272], other[:, :, 16:272], U[:, :, 16:272], ALU.subtract, tok)
                    d = split(DH[:, 4 * i:4 * i + 4, :], DL[:, 4 * i:4 * i + 4, :], src[:, :, 16:272], tok, d_free[0])
                    u_free[0] = d
                    for j in range(4):
                        d_tok[4 * i + j] = d

            def load_z(g):
                for i in range(2):
                    q = proj(512)
                    for b in range(2):
                        t0 = 4 * i + 2 * b
                        t = act(ZT[:, t0:t0 + 2, :], q.bank[b].rearrange("p (a c) -> p a c", a=2), ACT.Silu, q.tok,
                                z_free[0])
                    q.free_with(t)
                for j in range(8):
                    t = ts(ZT[:, j, :], ZT[:, j, :], tb("pool_scale_2", 8 * g + j), None, ALU.mult, None, t)
                return t

            def mix(g, zt):
                for i in range(2):
                    q = Group(lambda kt: (DH[:, kt, :], DL[:, kt, :]), lambda kt: d_tok[kt], 512, "cm", 8).all()
                    for j in range(4):
                        n = 4 * i + j
                        t = stt(ZT[:, n, :], q.bank[j // 2][:, 256 * (j % 2):256 * (j % 2) + 256],
                                tb("pool_b_2", 8 * g + n), ZT[:, n, :], ALU.add, ALU.mult, q.tok, zt)
                    q.free_with(t)
                    y = split(YH[:, 4 * i:4 * i + 4, :], YL[:, 4 * i:4 * i + 4, :], ZT[:, 4 * i:4 * i + 4, :], t,
                              y_read[0], free)
                    for j in range(4):
                        y_tok[4 * i + j] = y
                z_free[0] = y
                d_free[0] = q.tok

            load_u(0)
            for g in range(4):
                zt = load_z(g)
                if g > 0:
                    out_part(g - 1, dict(y_tok))
                mix(g, zt)
                if g < 3:
                    load_u(g + 1)
            pre_post(0, list(y_tok.values()) + flat([d_free[0]]))
            out_part(3, dict(y_tok))

        def lru_layer(free):
            RAWL = Q[:, 14336:15372].rearrange("p (i c) -> p i c", i=4)
            UCS = (Q[:, 15372:16396], Q[:, 20512:21536])
            R, IG, TA, SQ2 = (Q[:, 16396 + 1024 * k:17420 + 1024 * k] for k in range(4))
            ucs = [v.rearrange("p (i c) -> p i c", i=4) for v in UCS]
            c8 = SM[:, 640:672]
            ng = SM[:, 672:704]
            a = ts(ng, TB[:, AT["lru_L_2"]:AT["lru_L_2"] + 32], -1.0, None, ALU.mult, None, free)
            a = softplus(c8, ng, SM[:, 960:1056], 32, a)
            c8_t = ts(c8, c8, -8.0, None, ALU.mult, None, a)
            z_ = dop0(lambda e: e.memset(RAWL[:, :, 0:3], 0.0), free)
            raw_rd, uc_rd, z_rd = [z_], {0: free, 1: free}, {0: free, 1: free}
            wo = AT["conv_w_2"]
            y_tok = {}
            uct = {}

            def load_u(n):
                q = proj(512)
                for b in range(2):
                    t = act(RAWL[:, 2 * b:2 * b + 2, 3:259], q.bank[b].rearrange("p (a c) -> p a c", a=2), ACT.Copy,
                            q.tok, raw_rd[0], free)
                q.free_with(t)
                return t

            def conv(n, t):
                lt = [t] * 4
                ucv = ucs[n % 2]
                for k in range(4):
                    for m in range(4):
                        i = 4 * n + m
                        wk = TB[:, wo + 32 * k + i:wo + 32 * k + i + 1]
                        if k == 0:
                            lt[m] = ts(ucv[:, m, :], RAWL[:, m, 0:256], wk, tb("conv_b_2", i), ALU.mult, ALU.add,
                                       lt[m], uc_rd[n % 2])
                        else:
                            lt[m] = stt(ucv[:, m, :], RAWL[:, m, k:k + 256], wk, ucv[:, m, :], ALU.mult, ALU.add,
                                        lt[m])
                raw_rd[0] = lt[-1]
                uct[n] = lt[-1]

            def load_z(n):
                q = proj(512)
                for b in range(2):
                    t0 = 4 * (n % 2) + 2 * b
                    zt = act(ZT[:, t0:t0 + 2, :], q.bank[b].rearrange("p (a c) -> p a c", a=2), ACT.Silu, q.tok,
                             z_rd[n % 2])
                q.free_with(zt)
                return zt

            def gates(n, zt):
                ucv, UC = ucs[n % 2], UCS[n % 2]
                c = used[0]
                for k0, dst, bias in ((0, R, "lru_ba_2"), (4, IG, "lru_bx_2")):
                    w = W[:, c % NRAW, :].rearrange("p (k n) -> p k n", k=8)[:, k0:k0 + 4, :]
                    q = Group(None, None, 512, "cm", 2)
                    for kl in range(2):
                        for h in range(2):
                            for j in range(2):
                                last = kl == 1 and h == 1 and j == 1
                                t = mm(q.bank[h][:, 256 * j:256 * j + 256], w[:, 2 * h + kl, 128 * j:128 * j + 128],
                                       ucv[:, 2 * h + kl, :], part_tok[c], q.free, uct[n],
                                       start=(kl == 0 and j == 0), stop=(kl == 1), inc=last)
                    for j in range(4):
                        e_ = act(dst[:, 256 * j:256 * j + 256], q.bank[j // 2][:, 256 * (j % 2):256 * (j % 2) + 256],
                                 ACT.Sigmoid, t, free, y_tok.get(0), y_tok.get(4), bias=tb(bias, 4 * n + j), scale=1.0)
                    q.free_with(e_)
                use(c, t)
                parts = 2 if n == 7 else 1
                m = 4 // parts
                j0 = 4 * (n % 2)
                cut = [slice(256 * m * k, 256 * m * (k + 1)) for k in range(parts)]
                rng = range(parts)

                def each(f, prev):
                    return [f(cut[k], k, prev[k]) for k in rng]

                def v3(ap):
                    return ap.rearrange("p (i c) -> p i c", i=m)

                def cb(k):
                    i = 4 * n + m * k
                    return c8[:, i:i + m].unsqueeze(2).to_broadcast([128, m, 256])
                at[0] = "side"
                la = each(lambda c_, k, w: tt(v3(R[:, c_]), v3(R[:, c_]), cb(k), ALU.mult, w, c8_t), [e_] * parts)
                th = each(lambda c_, k, w: act(TA[:, c_], R[:, c_], ACT.Tanh, w, scale=-1.0, bias=0.0), la)
                ex = each(lambda c_, k, w: act(R[:, c_], R[:, c_], ACT.Exp, w, scale=1.0, bias=0.0), th)
                a = each(lambda c_, k, w: act(SQ2[:, c_], R[:, c_], ACT.Square, w), ex)
                b_ = tt(IG, IG, UC, ALU.mult, e_, uct[n])
                uc_rd[n % 2] = [b_, t]
                a = each(lambda c_, k, w: stt(TA[:, c_], SQ2[:, c_], 1.0, TA[:, c_], ALU.add, ALU.mult, w), a)
                a = each(lambda c_, k, w: ts(TA[:, c_], TA[:, c_], 0.0, None, ALU.max, None, w), a)
                a = each(lambda c_, k, w: act(TA[:, c_], TA[:, c_], ACT.Sqrt, w), a)
                a = each(lambda c_, k, w: tt(IG[:, c_], IG[:, c_], TA[:, c_], ALU.mult, w, b_), a)
                for k in rng:
                    for j in range(m * k, m * (k + 1)):
                        js = slice(256 * j, 256 * j + 256)
                        s_ = dop(TA[:, js], lambda e, js=js: e.tensor_tensor_scan(TA[:, js], R[:, js], IG[:, js], 0.0,
                                                                                  ALU.mult, ALU.add), a[k])
                    zv = ZT[:, j0 + m * k:j0 + m * (k + 1), :]
                    t = tt(zv, zv, v3(TA[:, cut[k]]), ALU.mult, s_, zt)
                    y = split(YH[:, j0 + m * k:j0 + m * (k + 1), :], YL[:, j0 + m * k:j0 + m * (k + 1), :], zv, t,
                              y_read[0], free)
                    for j in range(m * k, m * (k + 1)):
                        y_tok[j0 + j] = y
                z_rd[n % 2] = y
                at[0] = "main"

            conv(0, load_u(0))
            for n in range(8):
                zt = load_z(n)
                if n < 7:
                    nxt = load_u(n + 1)
                if n % 2 == 0 and n > 0:
                    out_part(n // 2 - 1, dict(y_tok))
                if n < 7:
                    conv(n + 1, nxt)
                gates(n, zt)
            fr = list(y_tok.values())
            pre_post(1, fr)
            out_part(3, dict(y_tok), halves=2)

        def post(l):
            junk, fr = JUNK, post_t["free"]
            gt = post_t["gl"]
            h_read[0] = y_read[0]
            a = dop(SM[:, 8:10], lambda e: e.tensor_reduce(SM[:, 8:10], SM[:, 0:8].rearrange("p (t g) -> p t g", t=2),
                                                           AX.X, ALU.add), os_tok[0])
            r = rstd_of(SM[:, 8:10], 2048, SM[:, 12:14], a, table=False)
            for i in range(4):
                cs = slice(512 * i, 512 * i + 512)
                for t in range(2):
                    x_tok[i] = stt(X[:, t, cs], O[:, t, cs], SM[:, 12 + t:13 + t], X[:, t, cs], ALU.mult, ALU.add,
                                   r, o_tok[i], x_tok[i], diag_rd[0])
                s_tok = sumsq(i, x_tok[i], junk)
            for i in range(4):
                at[0] = "conv"
                q = Group(lambda kt: PT[:, kt, :], lambda kt: post_t["pt"], 512, "tm", 2)
                q.feed(kts=range(2), col=512 * (i % 2), last_use=(i % 2 == 1))
                at[0] = "prep"
                for t in range(2):
                    e_t = act(E[:, t, 512 * i:512 * i + 512], q.bank[t], ACT.Copy, q.tok, fr)
                q.free_with(e_t)
                at[0] = "main"
            pt_read = q.tok
            norm_to_h("g_ple_in_2", l, s_tok)
            if l == 0:
                load_pt(1, pt_read)
            ff = flat(x_tok)
            for i in range(4):
                q = proj(512, mode="tm")
                cs = slice(512 * i, 512 * i + 512)
                for t in range(2):
                    g_ = act(O[:, t, cs], q.bank[t], ACT.Sigmoid, q.tok, ff)
                    m_ = tt(E[:, t, cs], E[:, t, cs], O[:, t, cs], ALU.mult, g_, e_t)
                    s1 = act(junk, E[:, t, cs], ACT.Square, m_, accum_out=SM[:, 4 * t + i:4 * t + i + 1])
                    n_ = tt(E[:, t, cs], E[:, t, cs], GL[:, cs], ALU.mult, s1, gt)
                q.free_with(g_)
            h_read[0] = q.tok
            a = dop0(lambda e: e.tensor_reduce(SM[:, 8:10], SM[:, 0:8].rearrange("p (t g) -> p t g", t=2), AX.X,
                                                ALU.add), s1)
            r = rstd_of(SM[:, 8:10], 2048, SM[:, 12:14], a)
            for i in range(4):
                cs = slice(512 * i, 512 * i + 512)
                for t in range(2):
                    x_tok[i] = stt(X[:, t, cs], E[:, t, cs], SM[:, 12 + t:13 + t], X[:, t, cs], ALU.mult, ALU.add,
                                   r, n_, diag_rd[0])
                if l == 0:
                    s_tok = sumsq(i, x_tok[i], junk)
            return s_tok

        load_pt(0, [free, a_done[0]])
        pool_layer([free, a_done[0]])
        s_tok = post(0)
        free = norm_to_h("g_pre_2", 1, s_tok)
        lru_layer([free, x_tok[3]])
        s_tok = post(1)
        assert used[0] == len(chunks) == len(released)

        ov = out.rearrange("(t p) c -> p t c", t=2)
        for g in range(4):
            dma(sy, ov[:, :, 512 * g:512 * g + 512], X[:, :, 512 * g:512 * g + 512], s_out, 16 * g + 16, x_tok[g])
        arrange([(pe, 60.0), (dv, 60.0), (ac, 60.0), (sy, 2000.0), (po, 2500.0)])
        block = ctx.enter_context(nc.Block())

        @block.sync
        def _(e):
            sy.play(e)
            e.wait_ge(s_out, 64)

        @block.gpsimd
        def _(e):
            po.play(e)
            e.wait_ge(s_sp, n_sp[0])

        @block.tensor
        def _(e):
            pe.play(e)

        @block.vector
        def _(e):
            dv.play(e)

        @block.scalar
        def _(e):
            ac.play(e)


def kernel(**inputs):
    import concourse.bacc as bacc
    from concourse.bass_utils import run_bass_kernel_spmd as run

    arr = {n: np.asarray(v) for n, v in inputs.items()}
    flat = {"lru_w": np.concatenate([arr["lru_wa_2"].reshape(8, 512, 256), arr["lru_wx_2"].reshape(8, 512, 256)],
                                    axis=1).reshape(1, 8192, 256),
            "pool_w_2": arr["pool_w_2"].reshape(4, 1024, 1024)}
    ch = plan()
    total = sum(128 * nk * n for _, _, _, nk, _, n in ch)
    wall = np.empty(total, np.float32)
    off = 0
    for name, l, k0, nk, c0, n in ch:
        a = (flat[name] if name in flat else arr[name])[l][128 * k0:128 * (k0 + nk), c0:c0 + n]
        wall[off:off + 128 * nk * n] = a.reshape(nk, 128, n).transpose(1, 0, 2).ravel()
        off += 128 * nk * n
    const = const_columns()
    cols = []
    for name in table_order():
        if name in const:
            cols.append(const[name])
        elif name in CHAN:
            cols.append(arr[name].reshape(-1, 128).T)
        else:
            cols.append(np.broadcast_to(arr[name].reshape(1, -1), (128, arr[name].size)))
    tab = np.ascontiguousarray(np.concatenate(cols, axis=1))
    pT = np.ascontiguousarray(arr["p_2"][:, 0].reshape(2, 256, 2, 128).transpose(3, 0, 2, 1).reshape(128, 1024))
    arrays = {
        "wall": wall, "tab": tab, "pT": pT,
        "pos": np.ascontiguousarray(arr["positions"].reshape(2, 128).T),
        "x": np.ascontiguousarray(arr["x"].reshape(256, 2048)),
        "g_post": np.ascontiguousarray(arr["g_post_2"]), "g_ple_out": np.ascontiguousarray(arr["g_ple_out_2"]),
    }
    nc = bacc.Bacc("TRN2", target_bir_lowering=False, num_devices=1)
    d = {n: nc.dram_tensor("in_" + n, a.shape, mybir.dt.from_np(a.dtype), kind="ExternalInput").ap()
         for n, a in arrays.items()}
    out = nc.dram_tensor("out_0", (256, 2048), F32, kind="ExternalOutput").ap()
    xsave = nc.dram_tensor("xsave", (256, 2048), F32, kind="Internal").ap()
    program(nc, d["wall"], d["tab"], d["pos"], d["pT"], d["x"], d["g_post"], d["g_ple_out"], xsave, out)
    r = run(nc, [{"in_" + n: a for n, a in arrays.items()}], core_ids=[0])
    return r.results[0]["out_0"].reshape(1, 256, 2048)
```
